# Optimizing a Trainium2 kernel written in Bass

```python
import math
import jax, jax.numpy as jnp
from jax import lax
import numpy as np

D_MODEL = 1024
BATCH = 1
SEQ = 512
DEPTH = 1

SSM_WIDTH = 512
SSM_GROUP = 16
SSM_GROUPS = SSM_WIDTH // SSM_GROUP
SSM_STATE = 64
DT_MIN = 0.001
DT_MAX = 0.1
N_HEADS = 8
N_KV_HEADS = 2
HEAD_DIM = 64
Q_PER_KV = N_HEADS // N_KV_HEADS
ATTN_WIDTH = N_HEADS * HEAD_DIM
KV_WIDTH = N_KV_HEADS * HEAD_DIM
WINDOW = 128
BLOCK = 128
SPLITS = (SSM_WIDTH,
          SSM_WIDTH + ATTN_WIDTH,
          SSM_WIDTH + ATTN_WIDTH + KV_WIDTH,
          SSM_WIDTH + ATTN_WIDTH + 2 * KV_WIDTH,
          SSM_WIDTH + ATTN_WIDTH + 2 * KV_WIDTH + D_MODEL)
IN_COLS = SSM_WIDTH + ATTN_WIDTH + 2 * KV_WIDTH + 2 * D_MODEL
N_GROUPS = 4
EXPERTS_PER_GROUP = 4
N_EXPERTS = N_GROUPS * EXPERTS_PER_GROUP
TOP_K = 2
D_EXPERT = 256
EPS = 1e-6
NEG = -1e30

kernel_name = "hybrid_s5_swa_sink_hmoe"

def rmsnorm(x, g):
    xf = x.astype(jnp.float32)
    y = xf * lax.rsqrt(jnp.mean(xf * xf, axis=-1, keepdims=True) + EPS) * g.astype(jnp.float32)
    return y.astype(x.dtype)

def head_rmsnorm(t, g):
    tf = t.astype(jnp.float32)
    return tf * lax.rsqrt(jnp.mean(tf * tf, axis=-1, keepdims=True) + EPS) * g.astype(jnp.float32)

def alibi_slopes():
    return jnp.exp2(-8.0 * jnp.arange(1, N_HEADS + 1, dtype=jnp.float32) / N_HEADS)

def s5_mixer(u, lam_re, lam_im, log_dt, b_re, b_im, c_re, c_im, d_skip):
    f32 = jnp.float32
    bsz, L, _ = u.shape
    uf = u.astype(f32).reshape(bsz, L, SSM_GROUPS, SSM_GROUP)
    lam = lax.complex(lam_re.astype(f32), lam_im.astype(f32))
    dt = jnp.exp(log_dt.astype(f32))[:, None]
    lam_bar = jnp.exp(lam * dt)
    b = lax.complex(b_re.astype(f32), b_im.astype(f32))
    b_bar = ((lam_bar - 1.0) / lam)[..., None] * b
    bu = jnp.einsum('gph,blgh->blgp', b_bar, uf)
    a = jnp.broadcast_to(lam_bar, bu.shape)

    def combine(e1, e2):
        a1, s1 = e1
        a2, s2 = e2
        return a1 * a2, a2 * s1 + s2

    _, states = lax.associative_scan(combine, (a, bu), axis=1)
    c = lax.complex(c_re.astype(f32), c_im.astype(f32))
    y = jnp.einsum('ghp,blgp->blgh', c, states).real
    y = y + d_skip.astype(f32).reshape(SSM_GROUPS, SSM_GROUP) * uf
    return y.reshape(bsz, L, SSM_WIDTH).astype(u.dtype)

def with_prev_block(t):
    pad = ((0, 0), (1, 0)) + ((0, 0),) * (t.ndim - 2)
    prev = jnp.pad(t[:, :-1], pad)
    return jnp.concatenate([prev, t], axis=2)

def sliding_window_attention(q, k, v, q_gain, k_gain, sinks):
    f32 = jnp.float32
    bsz, L, _ = q.shape
    nb = L // BLOCK
    qh = head_rmsnorm(q.reshape(bsz, L, N_HEADS, HEAD_DIM), q_gain)
    kh = head_rmsnorm(k.reshape(bsz, L, N_KV_HEADS, HEAD_DIM), k_gain)
    vh = v.astype(f32).reshape(bsz, L, N_KV_HEADS, HEAD_DIM)
    qb = qh.reshape(bsz, nb, BLOCK, N_KV_HEADS, Q_PER_KV, HEAD_DIM)
    kw = with_prev_block(kh.reshape(bsz, nb, BLOCK, N_KV_HEADS, HEAD_DIM))
    vw = with_prev_block(vh.reshape(bsz, nb, BLOCK, N_KV_HEADS, HEAD_DIM))
    scores = jnp.einsum('bnqkgd,bnskd->bnkgqs', qb, kw) * (HEAD_DIM ** -0.5)
    qpos = jnp.arange(BLOCK)[:, None] + BLOCK
    kpos = jnp.arange(2 * BLOCK)[None, :]
    dist = qpos - kpos
    blk = jnp.arange(nb)[:, None, None]
    valid = (dist >= 0) & (dist < WINDOW)
    valid = valid[None] & ((blk > 0) | (kpos[None] >= BLOCK))
    slopes = alibi_slopes().reshape(N_KV_HEADS, Q_PER_KV)
    scores = scores - slopes[:, :, None, None] * dist.astype(f32)
    scores = jnp.where(valid[None, :, None, None], scores, NEG)
    sink = sinks.astype(f32).reshape(N_KV_HEADS, Q_PER_KV)[None, None, :, :, None, None]
    m = jnp.maximum(jnp.max(scores, axis=-1, keepdims=True), sink)
    p = jnp.exp(scores - m)
    denom = jnp.sum(p, axis=-1, keepdims=True) + jnp.exp(sink - m)
    out = jnp.einsum('bnkgqs,bnskd->bnqkgd', p / denom, vw)
    return out.reshape(bsz, L, ATTN_WIDTH).astype(q.dtype)

def hierarchical_moe(h, w_coarse, w_fine, w_up, w_down):
    f32 = jnp.float32
    bsz, L, D = h.shape
    t = h.reshape(-1, D)
    n_tok = t.shape[0]
    coarse = jax.nn.softmax((t @ w_coarse).astype(f32), axis=-1)
    g_prob, g_idx = lax.top_k(coarse, 1)
    g_idx = g_idx[:, 0]
    fine = (t @ w_fine).astype(f32).reshape(n_tok, N_GROUPS, EXPERTS_PER_GROUP)
    fine = fine[jnp.arange(n_tok), g_idx]
    top_vals, top_idx = lax.top_k(fine, TOP_K)
    top_w = jax.nn.softmax(top_vals, axis=-1) * g_prob
    expert_id = g_idx[:, None] * EXPERTS_PER_GROUP + top_idx
    gates = jnp.sum(jax.nn.one_hot(expert_id, N_EXPERTS, dtype=f32) * top_w[..., None], axis=1)
    gu = jnp.einsum('nd,edf->nef', t, w_up)
    g_part, u_part = jnp.split(gu, 2, axis=-1)
    act = jax.nn.silu(g_part) * u_part * gates[..., None].astype(t.dtype)
    out = jnp.einsum('nef,efd->nd', act, w_down)
    return out.reshape(bsz, L, D)

def setup_inputs(seed: int = 0) -> dict:
    key = jax.random.key(seed)
    ks = jax.random.split(key, 24)
    f32 = jnp.float32

    def normal(k, shape):
        return jax.random.normal(k, shape, f32)

    def dense(k, shape, fan_in):
        return normal(k, shape) * fan_in ** -0.5

    n_idx = jnp.arange(SSM_STATE, dtype=f32)
    gp = (DEPTH, SSM_GROUPS, SSM_STATE)
    return {
        "x": normal(ks[0], (BATCH, SEQ, D_MODEL)),
        "norm_mix": 1.0 + 0.02 * normal(ks[1], (DEPTH, D_MODEL)),
        "w_in": dense(ks[2], (DEPTH, D_MODEL, IN_COLS), D_MODEL),
        "ssm_lam_re": -0.5 + 0.01 * normal(ks[3], gp),
        "ssm_lam_im": math.pi * n_idx + 0.01 * normal(ks[4], gp),
        "ssm_log_dt": jax.random.uniform(ks[5], (DEPTH, SSM_GROUPS), f32, math.log(DT_MIN), math.log(DT_MAX)),
        "ssm_b_re": dense(ks[6], (DEPTH, SSM_GROUPS, SSM_STATE, SSM_GROUP), 2 * SSM_GROUP),
        "ssm_b_im": dense(ks[7], (DEPTH, SSM_GROUPS, SSM_STATE, SSM_GROUP), 2 * SSM_GROUP),
        "ssm_c_re": dense(ks[8], (DEPTH, SSM_GROUPS, SSM_GROUP, SSM_STATE), SSM_STATE),
        "ssm_c_im": dense(ks[9], (DEPTH, SSM_GROUPS, SSM_GROUP, SSM_STATE), SSM_STATE),
        "ssm_d": normal(ks[10], (DEPTH, SSM_WIDTH)),
        "w_ssm_glu_val": dense(ks[11], (DEPTH, SSM_WIDTH, D_MODEL), SSM_WIDTH),
        "w_ssm_glu_gate": dense(ks[12], (DEPTH, SSM_WIDTH, D_MODEL), SSM_WIDTH),
        "q_norm": 1.0 + 0.02 * normal(ks[13], (DEPTH, HEAD_DIM)),
        "k_norm": 1.0 + 0.02 * normal(ks[14], (DEPTH, HEAD_DIM)),
        "attn_sinks": normal(ks[15], (DEPTH, N_HEADS)),
        "w_attn_up": dense(ks[16], (DEPTH, ATTN_WIDTH, D_MODEL), ATTN_WIDTH),
        "w_out": dense(ks[17], (DEPTH, D_MODEL, D_MODEL), D_MODEL),
        "norm_ffn": 1.0 + 0.02 * normal(ks[18], (DEPTH, D_MODEL)),
        "w_coarse": dense(ks[19], (DEPTH, D_MODEL, N_GROUPS), D_MODEL),
        "w_fine": dense(ks[20], (DEPTH, D_MODEL, N_EXPERTS), D_MODEL),
        "w_expert_up": dense(ks[21], (DEPTH, N_EXPERTS, D_MODEL, 2 * D_EXPERT), D_MODEL),
        "w_expert_down": dense(ks[22], (DEPTH, N_EXPERTS, D_EXPERT, D_MODEL), D_EXPERT),
    }

def reference(x, norm_mix, w_in, ssm_lam_re, ssm_lam_im, ssm_log_dt, ssm_b_re, ssm_b_im,
              ssm_c_re, ssm_c_im, ssm_d, w_ssm_glu_val, w_ssm_glu_gate, q_norm, k_norm,
              attn_sinks, w_attn_up, w_out, norm_ffn, w_coarse, w_fine, w_expert_up,
              w_expert_down):
    for i in range(DEPTH):
        h = rmsnorm(x, norm_mix[i])
        proj = h @ w_in[i]
        u, q, k, v, gate_s, gate_a = jnp.split(proj, SPLITS, axis=-1)
        y_s = s5_mixer(u, ssm_lam_re[i], ssm_lam_im[i], ssm_log_dt[i], ssm_b_re[i], ssm_b_im[i],
                       ssm_c_re[i], ssm_c_im[i], ssm_d[i])
        z = jax.nn.gelu(y_s)
        branch_s = (z @ w_ssm_glu_val[i]) * jax.nn.sigmoid(z @ w_ssm_glu_gate[i])
        y_a = sliding_window_attention(q, k, v, q_norm[i], k_norm[i], attn_sinks[i])
        branch_a = y_a @ w_attn_up[i]
        merged = jax.nn.sigmoid(gate_s) * branch_s + jax.nn.sigmoid(gate_a) * branch_a
        x = x + merged @ w_out[i]
        h2 = rmsnorm(x, norm_ffn[i])
        x = x + hierarchical_moe(h2, w_coarse[i], w_fine[i], w_expert_up[i], w_expert_down[i])
    return x


_drawn_inputs = setup_inputs


def setup_inputs(seed=0):
    import zlib

    import numpy as np

    out = dict(_drawn_inputs(seed))
    spreads = {}
    factors = {'norm_mix': 3.914,
     'ssm_lam_re': 200.0,
     'ssm_b_re': 2.686,
     'ssm_c_im': 2.684,
     'q_norm': 5.909,
     'k_norm': 8.0,
     'attn_sinks': 26.748,
     'norm_ffn': 4.745}
    for name, (base, spread) in spreads.items():
        noise = np.random.default_rng([zlib.crc32(name.encode()), seed]).standard_normal(out[name].shape)
        drawn = base * np.exp(spread * noise) if base else spread * noise
        out[name] = __import__('jax').numpy.asarray(drawn.astype(out[name].dtype))
    for name, factor in factors.items():
        out[name] = (out[name] * factor).astype(out[name].dtype)
    return out
```

```python
import math
from contextlib import ExitStack

import concourse.bass as bass
from concourse import mybir

F32 = mybir.dt.float32
I32 = mybir.dt.int32
U32 = mybir.dt.uint32
ALU = mybir.AluOpType
ACT = mybir.ActivationFunctionType
AX_X = mybir.AxisListType.X

P = 128
EPS = 1e-6
MAGIC = 1.5 * 2.0 ** 23
TWO_PI_HIGH = 6.28125
TWO_PI_LOW = 2.0 * math.pi - TWO_PI_HIGH
HIDE = 1e30
GELU_IN = math.sqrt(2.0 / math.pi)
GELU_CUBE = 0.044715


def hybrid_layer(nc, x, norm_mix, w_in, lam_re, lam_im, log_dt, b_re, b_im, c_re, c_im, d_skip,
                 w_glu_val, w_glu_gate, q_norm, k_norm, sinks, w_attn_up, w_out, norm_ffn,
                 w_coarse, w_fine, w_up, w_down, out):
    SEQ, D = x.shape[1], x.shape[2]
    DC = D // P
    TT = SEQ // P
    SSM_W = d_skip.shape[1]
    CT_ = SSM_W // P
    GROUPS, STATE = lam_re.shape[1], lam_re.shape[2]
    GCH = b_re.shape[3]
    ST = GROUPS * STATE // P
    SPC = ST // CT_
    SUB = 4
    CH = SEQ // SUB
    TCH = 2 * GCH
    HEADS, HD = sinks.shape[1], q_norm.shape[1]
    KVH = 2
    QPK = HEADS // KVH
    AW = HEADS * HD
    KW = KVH * HD
    NG = w_coarse.shape[2]
    NE = w_fine.shape[2]
    EPG = NE // NG
    DE = w_down.shape[2]
    UP_N = 2 * DE
    CAP = P
    MORE = SEQ // CAP - 1
    EARLY = 2
    NQ = 2 * KVH * QPK // 2
    assert CH == P and TCH * SUB == P and SPC * TCH == P and HD * 2 == P and UP_N == 512

    h2_rows = nc.dram_tensor("h2_rows", [SEQ, D], F32, kind="Internal").ap()
    y_rows = nc.dram_tensor("y_rows", [NE * CAP, D], F32, kind="Internal").ap()
    y_all = nc.dram_tensor("y_all", [NE * SEQ, D], F32, kind="Internal").ap()

    with ExitStack() as ctx:
        def sb(name, shape, dt=F32):
            return ctx.enter_context(nc.sbuf_tensor(name, shape, dt))

        def sem(name):
            return ctx.enter_context(nc.semaphore(name))

        SLOT = DC * 512
        DOWN = 2 * D
        SSM_FLOATS = 2 * 512 + 2 * 512 + 2 * 2 * SPC * (SUB + 1) * TCH + 512 + 2 * 512 + 2 * 512 + 2 * 512 + 6 * 512
        sizes = dict(ring=3 * SLOT, uz=CT_ * 512, qy=4 * 512, ht=SLOT, gs=SLOT, ga=SLOT, u4=ST * CH,
                     qk=2 * 640 + 2 * 640 + 2 * 256 + TT * KW, kt=KVH * SEQ, att=3 * 1024,
                     ssm=max(SSM_FLOATS, 4 * DOWN))
        arena = sb("arena", [P, sum(sizes.values())])
        at, off = {}, 0
        for name, n in sizes.items():
            at[name] = off
            off += n

        def part(name, start, size, /, **dims):
            v = arena[:, at[name] + start:at[name] + start + size]
            if dims:
                v = v.rearrange("row (%s) -> row %s" % (" ".join(dims), " ".join(dims)),
                                **{k: d for k, d in list(dims.items())[1:]})
            return v

        ring = [part("ring", s * SLOT, SLOT) for s in range(3)] + [part("uz", 0, SLOT)]
        down = [part("ssm", s * DOWN, DOWN, k=2, n=D) for s in range(4)]
        x_in = part("gs", 0, SLOT, t=TT, d=D)
        xn = part("ga", 0, SLOT, t=TT, d=D)
        hT = part("ht", 0, SLOT, k=DC, t=SEQ)
        x2 = part("ht", 0, SLOT, t=TT, d=D)
        ts_gate = part("gs", 0, SLOT, m=DC, t=SEQ)
        ta_gate = part("ga", 0, SLOT, m=DC, t=SEQ)
        uT = part("uz", 0, CT_ * 512, c=CT_, j=SUB, n=CH)
        zT = part("uz", 0, CT_ * 512, c=CT_, t=SEQ)
        qT = part("qy", 0, 4 * 512, h=4, t=SEQ)
        u4 = part("u4", 0, ST * CH, s=ST, n=CH)
        qk_raw = [part("qk", 640 * i, 640, h=10, d=HD) for i in range(2)]
        qk_sq = [part("qk", 1280 + 640 * i, 640, h=10, d=HD) for i in range(2)]
        k_dup = [part("qk", 2560 + 256 * i, 256, g=KVH, r=2, d=HD) for i in range(2)]
        v_tok = part("qk", 3072, TT * KW, t=TT, n=KW)
        kT = part("kt", 0, KVH * SEQ, g=KVH, t=SEQ)
        probs = [part("att", 1024 * i, 1024, h=QPK, k=2 * P) for i in range(2)]
        pT = part("att", 2048, 1024, f=2, h=QPK, q=P)
        def R(i):
            place = part("ring", 2 * SLOT + SLOT // 2 + i * P, P) if i < 16 else part("kt", (i - 16) * P, P)
            return place[0:ST, :]

        o = 0
        ssm = {}
        for name, n in [("Bre", 512), ("Bim", 512), ("Cre", 512), ("Cim", 512), ("CL0", 2 * SPC * (SUB + 1) * TCH),
                        ("CL1", 2 * SPC * (SUB + 1) * TCH), ("toep", 512), ("Ec", 512), ("Es", 512),
                        ("w1T", 1024), ("w1", 1024)] + [(f"t{i}", 512) for i in range(4)] + [("Sre", 512), ("Sim", 512)]:
            ssm[name] = (o, n)
            o += n

        def spart(name, start=0, size=None, /, **dims):
            return part("ssm", ssm[name][0] + start, size or ssm[name][1], **dims)

        Bre, Bim = (spart(n, s=ST, c=TCH) for n in ("Bre", "Bim"))
        Cre, Cim = (spart(n, s=ST, c=TCH) for n in ("Cre", "Cim"))
        NCL = SPC * (SUB + 1) * TCH
        CLre = [spart(f"CL{i}", 0, NCL, s=SPC, j=SUB + 1, c=TCH) for i in range(2)]
        CLim = [spart(f"CL{i}", NCL, NCL, s=SPC, j=SUB + 1, c=TCH) for i in range(2)]
        toep = spart("toep", q=SPC, n=SUB * TCH)
        Ec, Es = spart("Ec", q=SPC, n=CH), spart("Es", q=SPC, n=CH)
        w1T = spart("w1T", f=2, q=SPC, n=P)
        w1 = spart("w1", f=2, q=SPC, i=SUB, c=TCH)
        tb = [spart(f"t{i}", q=SPC, n=CH) for i in range(4)]
        Sre, Sim = spart("Sre", q=SPC, n=CH), spart("Sim", q=SPC, n=CH)
        xg = [part("ga", D * i, D) for i in range(2)]
        xgT = [part("ga", 2 * D + D * i, D, k=DC, n=P) for i in range(2)]
        y_out = [part("gs", D * i, D) for i in range(2)]
        th_e = [part("gs", 2048 + 256 * i, 256) for i in range(2)]
        a1_e = [part("gs", 2560 + 256 * i, 256) for i in range(2)]
        act_e = [part("gs", 3072 + 256 * i, 256) for i in range(2)]
        actT = [part("gs", 3584 + 256 * i, 256, k=2, n=P) for i in range(2)]
        pick = [part("u4", 512 * i, 512, t=TT, n=CAP) for i in range(2)]
        gath = [part("ring", D * i, D) for i in range(2 * TT)]

        ident = sb("ident", [P, P])
        before = sb("before", [P, P])
        ones = sb("ones", [P, P])
        slot_no = sb("slot_no", [P, CAP])
        neg_dist = sb("neg_dist", [P, 2 * P])
        tok_id = sb("tok_id", [P, TT])
        e_no = sb("e_no", [P, NE])
        e_rev = sb("e_rev", [P, NE])
        par_i = sb("par_i", [P, 1], I32)
        par = sb("par", [P, 3])
        half_col = sb("half_col", [P, 16])
        halfpi = sb("halfpi", [P, 1])
        g_mix = sb("g_mix", [P, DC])
        g_ffn = sb("g_ffn", [P, DC])
        d_col = sb("d_col", [P, CT_])
        qg = sb("qg", [P, 3])
        sink = sb("sink", [P, HEADS])
        ssq = sb("ssq", [P, 2 * TT])
        rstd = sb("rstd", [P, 2 * TT])
        qss = sb("qss", [P, TT, 10])
        qrs = sb("qrs", [P, TT, 10])
        ldt = sb("ldt", [ST, 2, 2])
        prm = sb("prm", [P, 7, ST])
        b_raw = part("att", 0, 512, f=2, s=ST, h=GCH)
        c_raw = part("att", 512, 512, f=2, c=CT_, p=STATE)
        c_exp = part("att", 1024, 1024, f=2, c=CT_, g=2, p=STATE)
        pw = sb("pw", [P, 2, SUB + 1, ST])
        e1 = sb("e1", [P, 2, 3, ST])
        sc_t = sb("sc_t", [P, 6, ST])
        et = sb("et", [P, 4, SPC, CH // 2])
        small_t = sb("small_t", [P, 4, SPC, TCH])
        smx = sb("smx", [P, 2, 6, QPK])
        rw = sb("rw", [P, DC, NG + NE])
        rt = part("qk", 0, 12 * TT * NE, f=12, t=TT, e=NE)
        lg = part("qk", 768, TT * (NG + NE), t=TT, n=NG + NE)
        rs_ = sb("rs_", [P, 16, TT])
        tg = part("qk", 1024, NE * TT * 2, e=NE, t=TT, n=2)
        pos = sb("pos", [P, NE, TT])
        cnt = sb("cnt", [P, NE])
        flag_f = sb("flag_f", [P, 1])
        flag = sb("flag", [1, 1], I32)
        idx_all = sb("idx_all", [P, NE], U32)
        gate_all = sb("gate_all", [P, NE])
        idx = sb("idx", [P, 2], U32)
        gate = sb("gate", [P, 1])
        dest = sb("dest", [P, 2, TT], U32)

        def bank(name):
            return ctx.enter_context(nc.psum_tensor(name, [P, 512], F32))

        pj = [bank("pj0"), bank("pj1")]
        tp = [bank("tp0"), bank("tp1")]
        sc = [bank("sc0"), bank("sc1")]
        mb = [bank("m0"), bank("m1")]

        const_ready = sem("const_ready")
        small_loaded, rows_loaded, gain_loaded = sem("small_loaded"), sem("rows_loaded"), sem("gain_loaded")
        x_loaded = [sem(f"x_loaded{t}") for t in range(TT)]
        x_again = sem("x_again")
        ring_loaded = [sem(f"ring_loaded{s}") for s in range(4)]
        down_loaded = [sem(f"down_loaded{s}") for s in range(4)]
        sq_done = sem("sq_done")
        var_done = sem("var_done")
        rstd_done = sem("rstd_done")
        xn_done = sem("xn_done")
        hT_done = sem("hT_done")
        pj_full, tp_full = sem("pj_full"), sem("tp_full")
        pj_free = [sem("pj_free0"), sem("pj_free1")]
        tp_free = [sem("tp_free0"), sem("tp_free1")]
        uT_done, u4_loaded = sem("uT_done"), sem("u4_loaded")
        qk_evac, qk_var, qk_rstd, qk_norm = sem("qk_evac"), sem("qk_var"), sem("qk_rstd"), sem("qk_norm")
        v_done, qT_done, kT_done = sem("v_done"), sem("qT_done"), sem("kT_done")
        gates_done = sem("gates_done")
        sc_full, sc_read, m_ready, exp_done, p_done = (sem(n) for n in ("sc_full", "sc_read", "m_ready", "exp_done", "p_done"))
        pT_done, av_done = sem("pT_done"), sem("av_done")
        prm_act, prm_dve = sem("prm_act"), sem("prm_dve")
        rows_done, prm_done, cexp_done, ct_done, bbd_done = (sem(n) for n in ("rows_done", "prm_done", "cexp_done", "ct_done", "bbd_done"))
        rot_done, pow_ready = sem("rot_done"), sem("pow_ready")
        e_done = sem("e_done")
        w1_done, w1T_done, cl_done, toep_done = (sem(n) for n in ("w1_done", "w1T_done", "cl_done", "toep_done"))
        bu_full, bu_read, S_done = sem("bu_full"), sem("bu_read"), sem("S_done")
        y_full, y_evac, z_full, yv_done = (sem(n) for n in ("y_full", "y_evac", "z_full", "yv_done"))
        z_sq, z_arg, z_th, z_done = (sem(n) for n in ("z_sq", "z_arg", "z_th", "z_done"))
        mg_full, mg_act, mg_free, merged_done = (sem(n) for n in ("mg_full", "mg_act", "mg_free", "merged_done"))
        x2_done = sem("x2_done")
        n2_done, h2T_done, lg_full = (sem(n) for n in ("n2_done", "h2T_done", "lg_full"))
        h2_stored = [sem(f"h2_stored{t}") for t in range(TT)]
        r_dve, r_act, r_pe = sem("r_dve"), sem("r_act"), sem("r_pe")
        route_done, flag_done = sem("route_done"), sem("flag_done")
        dve_chain, act_chain, pool_chain = sem("dve_chain"), sem("act_chain"), sem("pool_chain")
        pick_done, idx_full, idx_done = (sem(n) for n in ("pick_done", "idx_full", "idx_done"))
        gathered = [sem("gathered0"), sem("gathered1")]
        y_stored = [sem("y_stored0"), sem("y_stored1")]
        xt_full, xt_done, up_full, th_done, act_done = (sem(n) for n in ("xt_full", "xt_done", "up_full", "th_done", "act_done"))
        at_full, at_done, dn_full, y_scaled = (sem(n) for n in ("at_full", "at_done", "dn_full", "y_scaled"))
        o_pick, o_idxf, o_idx, o_gath, o_xt, o_xtd, o_up = (sem(n) for n in ("o_pick", "o_idxf", "o_idx", "o_gath", "o_xt", "o_xtd", "o_up"))
        o_th, o_act, o_at, o_atd, o_dn, o_y, o_st, o_w, o_pos, o_copy = (sem(n) for n in ("o_th", "o_act", "o_at", "o_atd", "o_dn", "o_y", "o_st", "o_w", "o_pos", "o_copy"))
        rows_back = [sem(f"rows_back{t}") for t in range(TT)]
        idx_taken = sem("idx_taken")
        gather_turn = sem("gather_turn")
        sum_done, out_stored = sem("sum_done"), sem("out_stored")

        pj_order, tp_order = [], []
        for t in range(TT):
            tp_order += [("h", t, f) for f in range(2)]
        pj_order += [("u", c) for c in range(CT_)]
        tp_order += [("prm",)]
        for t in range(TT):
            pj_order += [("q", t), ("kv", t)]
            if t == 0:
                tp_order += [("ct", 0), ("ct", 1)]
            else:
                tp_order += [("qt", t - 1), ("kt", t - 1)]
        tp_order += [("qt", TT - 1), ("kt", TT - 1)]
        for i in range(2 * DC + 1):
            if i < 2 * DC:
                pj_order += [("gate", i)]
            if i % 4 == 0 and i < 2 * DC:
                tp_order += [("w", i // 4, 0), ("w", i // 4, 1), ("k", i // 4)]
            if i % 2 == 1:
                tp_order += [("pt", i // 2, f) for f in range(2 if i // 2 >= KVH else 1)]
            if i % 2 == 0 and i >= 2:
                pj_order += [("av", i // 2 - 1)]
        n_pj, n_tp = len(pj_order), len(tp_order)

        def uses(order, key):
            n = order.index(key)
            return n, n % 2, n // 2

        jobs = [("in", 0), ("in", 512), ("kv", 1024)] + [("in", SSM_W + AW + 2 * KW + 512 * i) for i in range(4)] + \
               [("glu", 0), ("au", 0), ("glu", 512), ("out", 0), ("out", 512)]
        NJ = len(jobs)
        J_U, J_Q, J_KV, J_G, J_GLU, J_AU, J_OUT = 0, 1, 2, 3, (7, 9), 8, 10
        HM = DC // 2

        def job_used(eng, n):
            if n in (J_U, J_Q, J_KV):
                eng.wait_ge(pj_full, pj_order.index([("u", CT_ - 1), ("q", TT - 1), ("kv", TT - 1)][n]) + 1)
            elif n < J_GLU[0]:
                eng.wait_ge(pj_full, pj_order.index(("gate", 4 * (n - J_G) + 3)) + 1)
            elif n < J_OUT:
                eng.wait_ge(mg_full, 3 * HM if n == J_GLU[0] else 3 * DC)
            else:
                eng.wait_ge(pj_full, n_pj + TT * (n - J_OUT + 1))

        def ring_w(job, k, n):
            return ring[job % 3][:, 0:k * n].rearrange("p (k n) -> p k n", k=k)

        def glu_w(n):
            return ring[n % 3].rearrange("p (f k n) -> p f k n", f=2, k=4)

        def loads_until(s, n):
            return sum(16 * (2 if jobs[j][0] == "glu" else 1) for j in range(s, n + 1, 3))

        def job_loaded(eng, job):
            eng.wait_ge(ring_loaded[job % 3], loads_until(job % 3, job))

        def merge_banks(m):
            return [pj[0], sc[0], mb[0]] if m % 2 == 0 else [pj[1], sc[1], mb[1]]

        def merge_tmp(m):
            return part("att", (m % 2) * 1536, 1536, f=3, t=SEQ)

        def bc(v, shape):
            return v.broadcast_to(shape)

        block = ctx.enter_context(nc.Block())

        ctx.enter_context(nc.allow_non_contiguous_dma(reason="small parameters"))

        @block.sync
        def _(sp):
            for t in range(TT):
                sp.dma_start(x_in[:, t, :], x[0, t * P:(t + 1) * P, :]).then_inc(x_loaded[t], 16)

            def load_job(n):
                kind, c0 = jobs[n]
                if n >= 3:
                    job_used(sp, n - 3)
                if kind == "in":
                    dst, src = ring_w(n, DC, 512), w_in[0, :, c0:c0 + 512]
                elif kind == "kv":
                    dst, src = ring_w(n, DC, 2 * KW), w_in[0, :, c0:c0 + 2 * KW]
                elif kind == "out":
                    dst, src = ring_w(n, DC, 512), w_out[0, :, c0:c0 + 512]
                elif kind == "glu":
                    for f, w in enumerate((w_glu_val, w_glu_gate)):
                        sp.dma_start(glu_w(n)[:, f], w[0, :, c0:c0 + 512].rearrange("(k p) n -> p k n", p=P)
                                     ).then_inc(ring_loaded[n % 3], 16)
                    return
                else:
                    dst, src = ring_w(n, 4, D), w_attn_up[0]
                sp.dma_start(dst, src.rearrange("(k p) n -> p k n", p=P)).then_inc(ring_loaded[n % 3], 16)

            load_job(J_U)
            for f, m in enumerate((b_re, b_im)):
                v = m[0].rearrange("(s g) p h -> g p s h", g=2)
                for gl in range(2):
                    sp.dma_start(b_raw[gl * STATE:(gl + 1) * STATE, f], v[gl]).then_inc(small_loaded, 16)
            for f, m in enumerate((c_re, c_im)):
                sp.dma_start(c_raw[:, f], m[0].rearrange("(c g) h p -> (g h) c p", c=CT_)).then_inc(small_loaded, 16)
            load_job(J_Q)
            sp.dma_start(g_ffn[:], norm_ffn[0].rearrange("(k p) -> p k", p=P)).then_inc(small_loaded, 16)
            sp.dma_start(d_col[:], d_skip[0].rearrange("(k p) -> p k", p=P)).then_inc(small_loaded, 16)
            for h in range(2):
                sp.dma_start(qg[h * HD:(h + 1) * HD, 0:1], q_norm[0].rearrange("(p o) -> p o", o=1)).then_inc(small_loaded, 16)
                sp.dma_start(qg[h * HD:(h + 1) * HD, 1:2], k_norm[0].rearrange("(p o) -> p o", o=1)).then_inc(small_loaded, 16)
            sp.dma_start(sink[:], sinks[0:1, :].broadcast_to([P, HEADS])).then_inc(small_loaded, 16)
            sp.dma_start(rw[:, :, 0:NG], w_coarse[0].rearrange("(k p) n -> p k n", p=P)).then_inc(small_loaded, 16)
            sp.dma_start(rw[:, :, NG:NG + NE], w_fine[0].rearrange("(k p) n -> p k n", p=P)).then_inc(small_loaded, 16)
            load_job(J_KV)
            sp.wait_ge(uT_done, CT_)
            for j in range(SUB):
                for q in range(SPC):
                    sp.dma_start(u4[j * TCH:(j + 1) * TCH, q::SPC, :],
                                 uT[q * TCH:(q + 1) * TCH, :, j, :]).then_inc(u4_loaded, 16)
            for n in range(3, NJ):
                if n == J_OUT:
                    sp.wait_ge(gates_done, 2 * DC)
                    sp.dma_start(x2[:, :, :], x[0].rearrange("(t p) d -> p t d", p=P)).then_inc(x_again, 16)
                load_job(n)
            for e in range(4):
                if e < 3:
                    job_used(sp, NJ - 3 + e)
                else:
                    sp.wait_ge(merged_done, DC)
                sp.dma_start(ring[e].rearrange("p (k n) -> p k n", k=DC),
                             w_up[0, e].rearrange("(k p) n -> p k n", p=P)).then_inc(ring_loaded[e], 16)
                if e == 0:
                    sp.wait_ge(z_done, CT_)
                sp.dma_start(down[e], w_down[0, e].rearrange("(k p) n -> p k n", p=P)).then_inc(down_loaded[e], 16)
            with sp.Fori(0, NE // 4 - 1) as i:
                for r in range(4):
                    sp.wait_ge(up_full, i * 4 + (r + 1))
                    sp.dma_start(ring[r].rearrange("p (k n) -> p k n", k=DC),
                                 w_up[0, bass.ds(i * 4 + (r + 4), 1)].rearrange("e (k p) n -> p (e k) n", p=P)
                                 ).then_inc(ring_loaded[r], 16)
                    sp.wait_ge(dn_full, i * 4 + (r + 1))
                    sp.dma_start(down[r], w_down[0, bass.ds(i * 4 + (r + 4), 1)].rearrange("e (k p) n -> p (e k) n", p=P)
                                 ).then_inc(down_loaded[r], 16)
            sp.wait_ge(flag_done, 1)
            over = sp.value_load(flag[0:1, 0:1], min_val=0, max_val=1)
            with sp.If(over > 0):
                with sp.Fori(0, MORE) as j:
                    with sp.Fori(0, NE) as e:
                        sp.wait_ge(o_dn, j * NE + e + 1)
                        sp.dma_start(ring[0].rearrange("p (k n) -> p k n", k=DC),
                                     w_up[0, bass.ds(e, 1)].rearrange("e (k p) n -> p (e k) n", p=P)).then_inc(o_w, 16)
                        sp.dma_start(down[0], w_down[0, bass.ds(e, 1)].rearrange("e (k p) n -> p (e k) n", p=P)).then_inc(o_w, 16)
            for t in range(TT):
                sp.wait_ge(sum_done, t + 1)
                sp.dma_start(out[0, t * P:(t + 1) * P, :], x2[:, t, :]).then_inc(out_stored, 16)
            sp.wait_ge(out_stored, 16 * TT)
            for b in range(2):
                sp.wait_ge(y_stored[b], 8 * NE)
            for t in range(TT):
                sp.wait_ge(h2_stored[t], 16)

        @block.gpsimd
        def _(g):
            n_pool = [0]

            def link(ins):
                n_pool[0] += 1
                ins.then_inc(pool_chain, 1)
                g.wait_ge(pool_chain, n_pool[0])

            g.memset(half_col[:], -0.5).then_inc(const_ready, 1)
            g.memset(halfpi[:], math.pi / 2).then_inc(const_ready, 1)
            link(g.memset(ident[:], 0.0))
            g.affine_select(out=ident[:], in_=ident[:], compare_op=ALU.not_equal, fill=1.0, base=0,
                            pattern=[[-1, P]], channel_multiplier=1).then_inc(const_ready, 1)
            g.iota(par_i[:], pattern=[[0, 1]], base=0, channel_multiplier=1).then_inc(const_ready, 1)

            g.wait_ge(const_ready, 1)

            def inverse_root(dst, src, width, ready, n, done):
                g.wait_ge(ready, n)
                g.tensor_tensor(dst, src, half_col[:, 0:width], ALU.pow).then_inc(done, 1)

            for t in range(TT):
                inverse_root(rstd[:, t:t + 1], ssq[:, t:t + 1], 1, var_done, t + 1, rstd_done)
            link(g.memset(ones[:], 1.0))
            g.affine_select(out=before[:], in_=ones[:], compare_op=ALU.is_gt, fill=0.0, base=0,
                            pattern=[[1, P]], channel_multiplier=-1).then_inc(const_ready, 1)
            g.iota(slot_no[:], pattern=[[1, CAP]], base=0, channel_multiplier=0,
                   allow_small_or_imprecise_dtypes=True).then_inc(const_ready, 1)
            g.iota(tok_id[:], pattern=[[P, TT]], base=0, channel_multiplier=1,
                   allow_small_or_imprecise_dtypes=True).then_inc(const_ready, 1)
            g.iota(e_no[:], pattern=[[1, NE]], base=0, channel_multiplier=0,
                   allow_small_or_imprecise_dtypes=True).then_inc(const_ready, 1)
            g.iota(e_rev[:], pattern=[[-1, NE]], base=NE, channel_multiplier=0,
                   allow_small_or_imprecise_dtypes=True).then_inc(const_ready, 1)
            link(g.iota(neg_dist[:], pattern=[[1, 2 * P]], base=-P, channel_multiplier=-1,
                        allow_small_or_imprecise_dtypes=True))
            link(g.affine_select(out=neg_dist[:], in_=neg_dist[:], compare_op=ALU.is_ge, fill=-HIDE, base=P,
                                 pattern=[[-1, 2 * P]], channel_multiplier=1))
            g.affine_select(out=neg_dist[:], in_=neg_dist[:], compare_op=ALU.is_ge, fill=-HIDE, base=-1,
                            pattern=[[1, 2 * P]], channel_multiplier=-1).then_inc(const_ready, 1)
            def rotations(c):
                s0 = slice(c * SPC, (c + 1) * SPC)
                if c:
                    g.wait_ge(S_done, c)
                g.memset(Ec[:, :, 0:1], 1.0)
                link(g.memset(Es[:, :, 0:1], 0.0))
                g.tensor_copy(Ec[:, :, 1:2], e1[:, 0, 2, s0].rearrange("p (s o) -> p s o", o=1))
                link(g.tensor_copy(Es[:, :, 1:2], e1[:, 1, 2, s0].rearrange("p (s o) -> p s o", o=1)))
                m = 1
                while m < CH // 2:
                    er, ei = Ec[:, :, m:m + 1], Es[:, :, m:m + 1]
                    tq = et[:, :, :, 0:1]
                    g.tensor_tensor(tq[:, 0], er, er, ALU.mult)
                    g.tensor_tensor(tq[:, 1], ei, ei, ALU.mult)
                    link(g.tensor_tensor(tq[:, 2], er, ei, ALU.mult))
                    g.tensor_tensor(Ec[:, :, 2 * m:2 * m + 1], tq[:, 0], tq[:, 1], ALU.subtract)
                    link(g.tensor_tensor(Es[:, :, 2 * m:2 * m + 1], tq[:, 2], tq[:, 2], ALU.add))
                    m *= 2
                    w = m - 1
                    er, ei = (bc(v[:, :, m:m + 1], [P, SPC, w]) for v in (Ec, Es))
                    ar, ai = Ec[:, :, 1:m], Es[:, :, 1:m]
                    tq = et[:, :, :, 0:w]
                    g.tensor_tensor(tq[:, 0], ar, er, ALU.mult)
                    g.tensor_tensor(tq[:, 1], ai, ei, ALU.mult)
                    g.tensor_tensor(tq[:, 2], ar, ei, ALU.mult)
                    link(g.tensor_tensor(tq[:, 3], ai, er, ALU.mult))
                    g.tensor_tensor(Ec[:, :, m + 1:2 * m], tq[:, 0], tq[:, 1], ALU.subtract)
                    link(g.tensor_tensor(Es[:, :, m + 1:2 * m], tq[:, 2], tq[:, 3], ALU.add))
                g.sem_inc(e_done, 1)

            g.wait_ge(rot_done, 1)
            rotations(0)
            for t in range(TT):
                inverse_root(qrs[:, t, :], qss[:, t, :], 10, qk_var, t + 1, qk_rstd)
            for c in range(1, CT_):
                rotations(c)

            for t in range(TT):
                inverse_root(rstd[:, TT + t:TT + t + 1], ssq[:, TT + t:TT + t + 1], 1, var_done, TT + t + 1, rstd_done)

            for t in range(TT):
                g.wait_ge(h2_stored[t], 16)

            def gather(e2, e, n_free):
                if n_free is not None:
                    g.wait_ge(xt_full, n_free)
                g.tensor_copy(idx[:, e2:e2 + 1], idx_all[:, bass.ds(e, 1)]).then_inc(idx_taken, 1)
                g.wait_ge(idx_taken, e + 1)
                g.sem_inc(gather_turn, 1)
                g.indirect_dma_start(xg[e2], None, h2_rows,
                                     bass.IndirectOffsetOnAxis(idx[:, e2:e2 + 1], 0)).then_inc(gathered[e2], 16)

            g.wait_ge(idx_done, 1)
            gather(0, 0, None)
            gather(1, 1, None)
            g.wait_ge(idx_done, 2)
            with g.Fori(0, NE // 2 - 1) as i:
                for r in range(2):
                    gather(r, i * 2 + (r + 2), i * 4 + 2 * (r + 1))
            def rows_of_tokens(rows):
                for t in range(TT):
                    for k in range(2):
                        g.indirect_dma_start(gath[2 * t + k], None, rows,
                                             bass.IndirectOffsetOnAxis(dest[:, k, t:t + 1], 0)).then_inc(rows_back[t], 16)

            g.wait_ge(flag_done, 1)
            over = g.value_load(flag[0:1, 0:1], min_val=0, max_val=1)
            with g.If(over > 0):
                with g.Fori(0, MORE * NE) as b:
                    g.wait_ge(o_idx, b + 1)
                    g.sem_inc(gather_turn, 1)
                    g.indirect_dma_start(xg[0], None, h2_rows,
                                         bass.IndirectOffsetOnAxis(idx[:, 0:1], 0)).then_inc(o_gath, 16)
                g.wait_ge(o_st, 16 * MORE * NE)
                for b in range(2):
                    g.wait_ge(y_stored[b], 8 * NE)
                g.dma_start(y_all[0:NE * CAP, :], y_rows).then_inc(o_copy, 16)
                g.wait_ge(o_copy, 16)
                rows_of_tokens(y_all)
            with g.If(over < 1):
                for b in range(2):
                    g.wait_ge(y_stored[b], 8 * NE)
                g.wait_ge(dn_full, NE)
                rows_of_tokens(y_rows)

        @block.scalar
        def _(act):
            act.dma_start(R(0), lam_re[0].rearrange("(s g) p -> s (g p)", g=2)).then_inc(rows_loaded, 16)
            act.dma_start(R(1), lam_im[0].rearrange("(s g) p -> s (g p)", g=2)).then_inc(rows_loaded, 16)
            act.dma_start(ldt[:, 0, :], log_dt[0].rearrange("(s g) -> s g", g=2)).then_inc(rows_loaded, 16)
            act.dma_start(g_mix[:], norm_mix[0].rearrange("(k p) -> p k", p=P)).then_inc(gain_loaded, 16)
            act.wait_ge(rows_loaded, 16 * 3)
            act.activation(ldt[:, 1, :], ldt[:, 0, :], ACT.Exp).then_inc(prm_act, 1)
            act.wait_ge(prm_dve, 1)
            act.activation(R(5), R(2), ACT.Exp).then_inc(prm_act, 1)
            act.activation(R(6), R(2), ACT.Exp, scale=float(SUB)).then_inc(prm_act, 1)
            for t in range(TT):
                act.wait_ge(x_loaded[t], 16)
                act.activation(xn[:, t, :], x_in[:, t, :], ACT.Square, accum_out=ssq[:, t:t + 1]).then_inc(sq_done, 1)
                if t == 0:
                    act.wait_ge(prm_dve, 2)
                    act.wait_ge(const_ready, 2)
                    act.activation(R(7), R(4), ACT.Sin).then_inc(prm_act, 1)
                    act.activation(R(8), R(9), ACT.Sin, scale=-1.0, bias=halfpi[0:ST, :]).then_inc(prm_act, 1)
            for c in range(CT_):
                n, b, _ = uses(pj_order, ("u", c))
                act.wait_ge(pj_full, n + 1)
                act.activation(uT[:, c].rearrange("p j n -> p n j"), pj[b][:].rearrange("p (n j) -> p n j", j=SUB),
                               ACT.Copy).then_inc(pj_free[b], 1)
                act.wait_ge(pj_free[b], uses(pj_order, ("u", c))[2] + 1)
                act.sem_inc(uT_done, 1)
            for t in range(TT):
                if t >= 2:
                    act.wait_ge(qT_done, t - 1)
                    act.wait_ge(kT_done, t - 1)
                n, b, _ = uses(pj_order, ("q", t))
                act.wait_ge(pj_full, n + 1)
                act.activation(qk_sq[t % 2][:, 0:8, :], pj[b][:], ACT.Square).then_inc(qk_evac, 1)
                act.activation(qk_raw[t % 2][:, 0:8, :], pj[b][:], ACT.Copy).then_inc(pj_free[b], 1)
                n, b, _ = uses(pj_order, ("kv", t))
                act.wait_ge(pj_full, n + 1)
                act.activation(v_tok[:, t, :], pj[b][:, KW:2 * KW], ACT.Copy).then_inc(v_done, 1)
                act.activation(qk_sq[t % 2][:, 8:10, :], pj[b][:, 0:KW], ACT.Square).then_inc(qk_evac, 1)
                act.activation(qk_raw[t % 2][:, 8:10, :], pj[b][:, 0:KW], ACT.Copy).then_inc(pj_free[b], 1)
            for i in range(2 * DC + 1):
                if i < 2 * DC:
                    n, b, used = uses(pj_order, ("gate", i))
                    act.wait_ge(pj_full, n + 1)
                    dst = ts_gate[:, i, :] if i < DC else ta_gate[:, i - DC, :]
                    act.activation(dst, pj[b][:], ACT.Tanh, scale=0.5).then_inc(pj_free[b], 1)
                    act.wait_ge(pj_free[b], used + 1)
                    act.sem_inc(gates_done, 1)
                if i % 4 == 0 and i < 2 * DC:
                    c = i // 4
                    if c:
                        act.wait_ge(bu_full, c)
                    for f in range(2):
                        n, b, _ = uses(tp_order, ("w", c, f))
                        act.wait_ge(tp_full, n + 1)
                        act.activation(w1T[:, f], tp[b][:], ACT.Copy).then_inc(tp_free[b], 1)
                        act.wait_ge(tp_free[b], uses(tp_order, ("w", c, f))[2] + 1)
                        act.sem_inc(w1T_done, 1)
                    n, b, _ = uses(tp_order, ("k", c))
                    act.wait_ge(tp_full, n + 1)
                    if c:
                        act.wait_ge(y_full, c)
                    act.wait_ge(bbd_done, 1)
                    kps = tp[b][0:TCH, :].rearrange("p (q n) -> p q n", q=SPC)
                    for j in range(SUB):
                        ins = act.activation(toep[j * TCH:(j + 1) * TCH, :, j * TCH:], kps[:, :, 0:(SUB - j) * TCH], ACT.Copy)
                        ins.then_inc(toep_done if j < SUB - 1 else tp_free[b], 1)
                    act.wait_ge(tp_free[b], uses(tp_order, ("k", c))[2] + 1)
                    act.sem_inc(toep_done, 1)
                if i % 2 == 0 and i >= 2:
                    a = i // 2 - 1
                    n, b, _ = uses(pj_order, ("av", a))
                    act.wait_ge(pj_full, n + 1)
                    blk, kv = a // KVH, a % KVH
                    act.activation(qT[:, 2 * kv:2 * kv + 2, blk * P:(blk + 1) * P],
                                   pj[b][:, 0:2 * P].rearrange("p (h q) -> p h q", h=2), ACT.Copy).then_inc(pj_free[b], 1)
                    act.wait_ge(pj_free[b], uses(pj_order, ("av", a))[2] + 1)
                    act.sem_inc(av_done, 1)
                if i % 2 == 0 and i < 2 * DC:
                    a = i // 2
                    W = 2 * P if a >= KVH else P
                    act.wait_ge(m_ready, 2 * (a + 1))
                    for h in range(QPK):
                        act.activation(probs[a % 2][:, h, 0:W], probs[a % 2][:, h, 0:W], ACT.Exp,
                                       bias=smx[:, a % 2, 1, h:h + 1],
                                       accum_out=smx[:, a % 2, 4, h:h + 1]).then_inc(exp_done, 1)
                    act.activation(smx[:, a % 2, 3, :], smx[:, a % 2, 2, :], ACT.Exp).then_inc(exp_done, 1)
                if i % 2 == 1:
                    a = i // 2
                    if a:
                        act.wait_ge(pj_full, uses(pj_order, ("av", a - 1))[0] + 1)
                    for f in range(2 if a >= KVH else 1):
                        n, b, _ = uses(tp_order, ("pt", a, f))
                        act.wait_ge(tp_full, n + 1)
                        act.activation(pT[:, f], tp[b][:], ACT.Copy).then_inc(tp_free[b], 1)
                        act.wait_ge(tp_free[b], uses(tp_order, ("pt", a, f))[2] + 1)
                        act.sem_inc(pT_done, 1)
                if i % 4 == 3:
                    c = i // 4
                    act.wait_ge(y_full, c + 1)
                    act.activation(tb[0], mb[0][:], ACT.Copy).then_inc(y_evac, 1)
                if i % 4 == 0 and i >= 4:
                    c = i // 4 - 1
                    act.wait_ge(yv_done, c + 1)
                    act.activation(tb[2], tb[1], ACT.Square).then_inc(z_sq, 1)
                    act.wait_ge(z_arg, c + 1)
                    act.activation(tb[2], tb[2], ACT.Tanh, scale=GELU_IN).then_inc(z_th, 1)
            for m in range(DC):
                if m >= 2:
                    act.wait_ge(merged_done, m - 1)
                act.wait_ge(mg_full, 3 * m + 1)
                act.activation(merge_tmp(m)[:, 0, :], merge_banks(m)[0][:], ACT.Tanh, scale=0.25).then_inc(mg_act, 1)
            for t in range(TT):
                act.wait_ge(x2_done, TT + t + 1)
                act.activation(part("att", t % 2 * D, D), x2[:, t, :], ACT.Square, accum_out=ssq[:, TT + t:TT + t + 1]).then_inc(sq_done, 1)
                if t:
                    act.wait_ge(n2_done, t)
                    act.dma_start(h2_rows[(t - 1) * P:t * P, :], xg[(t - 1) % 2]).then_inc(h2_stored[t - 1], 16)
            act.wait_ge(n2_done, TT)
            act.dma_start(h2_rows[(TT - 1) * P:, :], xg[(TT - 1) % 2]).then_inc(h2_stored[TT - 1], 16)
            act.wait_ge(r_dve, 1)
            act.activation(rt[:, 0, :, 0:NG], rt[:, 0, :, 0:NG], ACT.Exp).then_inc(r_act, 1)
            act.wait_ge(r_dve, 2)
            act.activation(rs_[:, 6, :], rs_[:, 6, :], ACT.Exp).then_inc(r_act, 1)

            def up_part(e4, n):
                act.wait_ge(up_full, n)
                b = e4 % 2
                act.activation(th_e[b], pj[b][:, 0:DE], ACT.Tanh, scale=0.5).then_inc(th_done, 1)

            def down_part(e4, e, n_at, n_dn, n_store):
                b = e4 % 2
                act.wait_ge(at_full, n_at)
                act.activation(actT[b], sc[1][:, 0:2 * P], ACT.Copy).then_inc(at_done, 1)
                if n_store is not None:
                    act.wait_ge(y_stored[b], n_store)
                act.wait_ge(dn_full, n_dn)
                for h in range(2):
                    act.activation(y_out[b][:, h * 512:(h + 1) * 512], mb[h][:], ACT.Copy,
                                   scale=gate_all[:, bass.ds(e, 1)]).then_inc(y_scaled, 1)
                act.wait_ge(y_scaled, n_dn * 2)
                act.dma_start(y_rows[bass.ds(e * CAP, CAP), :], y_out[b]).then_inc(y_stored[b], 16)

            up_part(0, 1)
            for e in range(1, 3):
                up_part(e, e + 1)
                down_part(e - 1, e - 1, e, e, None)
            up_part(3, 4)
            down_part(2, 2, 3, 3, 16)
            with act.Fori(0, NE // 4 - 1) as i:
                for r in range(4):
                    up_part(r, i * 4 + (r + 5))
                    down_part((r + 3) % 4, i * 4 + (r + 3), i * 4 + (r + 4), i * 4 + (r + 4), (i * 2 + (r + 3) // 2) * 16)
            down_part(3, NE - 1, NE, NE, 16 * ((NE - 1) // 2))
            act.wait_ge(flag_done, 1)
            over = act.value_load(flag[0:1, 0:1], min_val=0, max_val=1)
            with act.If(over > 0):
                for b in range(2):
                    act.wait_ge(y_stored[b], 8 * NE)
                with act.Fori(0, MORE) as j:
                    with act.Fori(0, NE) as e:
                        act.wait_ge(o_up, j * NE + e + 1)
                        act.activation(th_e[0], pj[0][:, 0:DE], ACT.Tanh, scale=0.5).then_inc(o_th, 1)
                        act.wait_ge(o_at, j * NE + e + 1)
                        act.activation(actT[0], sc[1][:, 0:2 * P], ACT.Copy).then_inc(o_atd, 1)
                        act.wait_ge(o_dn, j * NE + e + 2)
                        for h in range(2):
                            act.activation(y_out[0][:, h * 512:(h + 1) * 512], mb[h][:], ACT.Copy,
                                           scale=gate[:, 0:1]).then_inc(o_y, 1)
                        act.wait_ge(o_y, (j * NE + e + 1) * 2)
                        act.dma_start(y_all[bass.ds((j + 1) * (NE * CAP) + e * CAP, CAP), :], y_out[0]).then_inc(o_st, 16)
                        act.wait_ge(o_st, (j * NE + e + 1) * 16)

        @block.vector
        def _(v):
            n_dve = [0]

            def mark(ins):
                n_dve[0] += 1
                ins.then_inc(dve_chain, 1)

            def settle():
                v.wait_ge(dve_chain, n_dve[0])

            def link(ins):
                mark(ins)
                settle()

            tt, ts, stt = v.tensor_tensor, v.tensor_scalar, v.scalar_tensor_tensor

            def scale_tile(t):
                v.wait_ge(rstd_done, t + 1)
                ts(xn[:, t, :], x_in[:, t, :], rstd[:, t:t + 1], None, ALU.mult).then_inc(xn_done, 1)

            def norm2(t):
                v.wait_ge(sq_done, TT + t + 1)
                mean_var(ssq[:, TT + t:TT + t + 1], D)
                v.wait_ge(rstd_done, TT + t + 1)
                if t >= 2:
                    v.wait_ge(h2_stored[t - 2], 16)
                    v.wait_ge(tp_full, n_tp + 2 * (t - 1))
                ts(xg[t % 2], x2[:, t, :], rstd[:, TT + t:TT + t + 1], None, ALU.mult).then_inc(n2_done, 1)

            def norm2_turned(t):
                if t >= 2:
                    v.wait_ge(lg_full, t - 1)
                for f in range(2):
                    v.wait_ge(tp_full, n_tp + 2 * t + f + 1)
                    tt(xgT[t % 2][:, 4 * f:4 * f + 4, :], tp[f][:].rearrange("p (k n) -> p k n", k=4), gain[f],
                       ALU.mult).then_inc(h2T_done, 1)

            gain = [bc(g_ffn[:, 4 * f:4 * f + 4].rearrange("p (k o) -> p k o", o=1), [P, 4, P]) for f in range(2)]

            def mean_var(dst, n):
                ts(dst, dst, 1.0 / n, EPS, ALU.mult, ALU.add).then_inc(var_done, 1)

            v.wait_ge(rows_loaded, 16 * 3)
            v.wait_ge(prm_act, 1)
            dt_bc = bc(ldt[:, 1, :].rearrange("s (g o) -> s g o", o=1), [ST, 2, STATE])
            g2 = lambda i: R(i).rearrange("s (g p) -> s g p", g=2)
            tt(g2(2), g2(0), dt_bc, ALU.mult).then_inc(prm_dve, 1)
            link(tt(g2(3), g2(1), dt_bc, ALU.mult))
            link(ts(R(10), R(3), 1.0 / (2 * math.pi), MAGIC, ALU.mult, ALU.add))
            link(ts(R(10), R(10), MAGIC, None, ALU.subtract))
            link(stt(R(4), R(10), -TWO_PI_HIGH, R(3), ALU.mult, ALU.add))
            link(stt(R(4), R(10), -TWO_PI_LOW, R(4), ALU.mult, ALU.add))
            link(ts(R(4), R(4), 3.1415925, -3.1415925, ALU.min, ALU.max))
            link(ts(R(9), R(4), -1.0, None, ALU.mult))
            tt(R(9), R(9), R(4), ALU.max).then_inc(prm_dve, 1)
            for t in range(TT):
                v.wait_ge(sq_done, t + 1)
                mean_var(ssq[:, t:t + 1], D)
                if t == 0:
                    mark(tt(R(11), R(0), R(0), ALU.mult))
                    link(tt(R(12), R(1), R(1), ALU.mult))
                    link(tt(R(11), R(11), R(12), ALU.add))
                    link(v.reciprocal(R(12), R(11)))
                if t > 0:
                    scale_tile(t - 1)
            scale_tile(TT - 1)
            v.wait_ge(gain_loaded, 16)
            for t in range(TT):
                for f in range(2):
                    n, b, used = uses(tp_order, ("h", t, f))
                    v.wait_ge(tp_full, n + 1)
                    tt(hT[:, 4 * f:4 * f + 4, t * P:(t + 1) * P], tp[b][:].rearrange("p (k n) -> p k n", k=4),
                       bc(g_mix[:, 4 * f:4 * f + 4].rearrange("p (k o) -> p k o", o=1), [P, 4, P]),
                       ALU.mult).then_inc(tp_free[b], 1)
                v.wait_ge(tp_free[0], t + 1)
                v.wait_ge(tp_free[1], t + 1)
                v.sem_inc(hT_done, 1)
            v.wait_ge(prm_act, 5)
            mark(tt(R(13), R(5), R(8), ALU.mult))
            mark(tt(R(14), R(5), R(7), ALU.mult))
            settle()
            link(ts(R(17), R(13), 1.0, None, ALU.subtract))
            mark(tt(R(18), R(17), R(0), ALU.mult))
            mark(tt(R(19), R(14), R(1), ALU.mult))
            mark(tt(R(20), R(14), R(0), ALU.mult))
            mark(tt(R(21), R(17), R(1), ALU.mult))
            settle()
            mark(tt(R(18), R(18), R(19), ALU.add))
            mark(tt(R(20), R(20), R(21), ALU.subtract))
            settle()
            mark(tt(R(15), R(18), R(12), ALU.mult))
            link(tt(R(16), R(20), R(12), ALU.mult))
            v.sem_inc(rows_done, 1)
            v.wait_ge(const_ready, 4)
            v.wait_ge(small_loaded, 16 * 15)
            link(ts(par_i[:], par_i[:], GCH, None, ALU.bitwise_and))
            link(ts(par[:, 0:1], par_i[:], 0.0, None, ALU.is_gt))
            link(ts(par[:, 1:2], par[:, 0:1], -1.0, 1.0, ALU.mult, ALU.add))
            for f in range(2):
                for gl in range(2):
                    mark(ts(c_exp[:, f, :, gl, :], c_raw[:, f], par[:, 1 - gl:2 - gl], (1.0, -1.0)[f], ALU.mult, ALU.mult))
            settle()
            v.sem_inc(cexp_done, 1)
            n, b, used = uses(tp_order, ("prm",))
            v.wait_ge(tp_full, n + 1)
            v.tensor_copy(prm[:], tp[b][:, 0:7 * ST].rearrange("p (f s) -> p f s", f=7)).then_inc(tp_free[b], 1)
            v.wait_ge(tp_free[b], used + 1)
            pr, pi = (lambda j: pw[:, 0, j, :]), (lambda j: pw[:, 1, j, :])
            mark(v.memset(pr(0), 1.0))
            mark(v.memset(pi(0), 0.0))
            mark(v.tensor_copy(pw[:, :, 1, :], prm[:, 0:2, :]))
            mark(v.tensor_copy(e1[:, :, 0, :], prm[:, 5:7, :]))
            settle()

            def cmul(dst, a, b_, tmp):
                mark(tt(tmp(0), a[0], b_[0], ALU.mult))
                mark(tt(tmp(1), a[1], b_[1], ALU.mult))
                mark(tt(tmp(2), a[0], b_[1], ALU.mult))
                mark(tt(tmp(3), a[1], b_[0], ALU.mult))
                settle()
                mark(tt(dst[0], tmp(0), tmp(1), ALU.subtract))
                mark(tt(dst[1], tmp(2), tmp(3), ALU.add))
                settle()

            pwj = lambda j: (pr(j), pi(j))
            ej = lambda j: (e1[:, 0, j, :], e1[:, 1, j, :])
            stmp = lambda i: sc_t[:, i, :]
            cmul(ej(1), ej(0), ej(0), stmp)
            cmul(ej(2), ej(1), ej(1), stmp)
            v.sem_inc(rot_done, 1)
            cmul(pwj(2), pwj(1), pwj(1), stmp)
            cmul(pwj(3), pwj(2), pwj(1), stmp)
            cmul(pwj(4), pwj(2), pwj(2), stmp)
            mark(v.memset(Bre, 0.0))
            mark(v.memset(Bim, 0.0))
            mark(v.memset(toep, 0.0))
            mark(v.memset(Sre[:, :, 0:1], 0.0))
            mark(v.memset(Sim[:, :, 0:1], 0.0))
            coef = [bc(prm[:, 2 + i, :].rearrange("p (s o) -> p s o", o=1), [P, ST, GCH]) for i in range(2)]
            bt = [tb[i][:, :, :].rearrange("p q n -> p (q n)")[:, 0:ST * GCH].rearrange("p (s h) -> p s h", s=ST) for i in range(4)]
            mark(tt(bt[0], b_raw[:, 0], coef[0], ALU.mult))
            mark(tt(bt[1], b_raw[:, 1], coef[1], ALU.mult))
            mark(tt(bt[2], b_raw[:, 0], coef[1], ALU.mult))
            mark(tt(bt[3], b_raw[:, 1], coef[0], ALU.mult))
            settle()
            v.sem_inc(bbd_done, 1)
            for gl in range(2):
                ps = slice(gl * STATE, (gl + 1) * STATE)
                cs = slice(gl * GCH, (gl + 1) * GCH)
                mark(tt(Bre[ps, :, cs], bt[0][ps], bt[1][ps], ALU.subtract))
                mark(tt(Bim[ps, :, cs], bt[2][ps], bt[3][ps], ALU.add))
            settle()
            for f, dst in enumerate((Cre, Cim)):
                n, b, used = uses(tp_order, ("ct", f))
                v.wait_ge(tp_full, n + 1)
                v.tensor_copy(dst, tp[b][:].rearrange("p (s c) -> p s c", c=TCH)).then_inc(tp_free[b], 1)
                v.wait_ge(tp_free[b], used + 1)
            mark(ts(qg[:, 2:3], qg[:, 0:1], qg[:, 1:2], HD ** -0.5, ALU.mult, ALU.mult))
            settle()

            def qk_normalise(t):
                v.wait_ge(qk_evac, 2 * (t + 1))
                link(v.tensor_reduce(qss[:, t, :], qk_sq[t % 2], AX_X, ALU.add))
                ts(qss[:, t, :], qss[:, t, :], 1.0 / HD, EPS, ALU.mult, ALU.add).then_inc(qk_var, 1)
                v.wait_ge(qk_rstd, t + 1)
                v.wait_ge(pj_free[0], uses(pj_order, ("kv", t))[0] // 2 + 1)
                v.wait_ge(pj_free[1], uses(pj_order, ("kv", t))[0] // 2 + 1)
                rb = qrs[:, t, :].rearrange("p (h o) -> p h o", o=1)
                mark(tt(qk_raw[t % 2][:, 0:8, :], qk_raw[t % 2][:, 0:8, :], bc(rb[:, 0:8], [P, 8, HD]), ALU.mult))
                for r in range(2):
                    mark(tt(k_dup[t % 2][:, :, r, :], qk_raw[t % 2][:, 8:10, :], bc(rb[:, 8:10], [P, 2, HD]), ALU.mult))
                settle()
                v.sem_inc(qk_norm, 1)

            def qk_turned(t):
                n, b, used = uses(tp_order, ("qt", t))
                v.wait_ge(tp_full, n + 1)
                ts(qT[:, :, t * P:(t + 1) * P], tp[b][:].rearrange("p (h n) -> p h n", h=4), qg[:, 2:3], None,
                   ALU.mult).then_inc(tp_free[b], 1)
                v.wait_ge(tp_free[b], used + 1)
                v.sem_inc(qT_done, 1)
                n, b, used = uses(tp_order, ("kt", t))
                v.wait_ge(tp_full, n + 1)
                v.tensor_copy(kT[:, :, t * P:(t + 1) * P],
                              tp[b][:, 0:2 * P].rearrange("p (h n) -> p h n", h=2)).then_inc(tp_free[b], 1)
                v.wait_ge(tp_free[b], used + 1)
                v.sem_inc(kT_done, 1)

            def input_weights(c):
                s0 = slice(c * SPC, (c + 1) * SPC)
                if c:
                    v.wait_ge(tp_full, uses(tp_order, ("w", c - 1, 1))[0] + 1)
                br, bi = Bre[:, s0], Bim[:, s0]
                mark(v.tensor_copy(w1[:, 0, :, SUB - 1, :], br))
                mark(v.tensor_copy(w1[:, 1, :, SUB - 1, :], bi))
                for i in range(SUB - 1):
                    a, b_ = (bc(pw[:, f, SUB - 1 - i, s0].rearrange("p (s o) -> p s o", o=1), [P, SPC, TCH]) for f in range(2))
                    cmul((w1[:, 0, :, i, :], w1[:, 1, :, i, :]), (br, bi), (a, b_), lambda k: lt(k))
                settle()
                v.sem_inc(w1_done, 1)

            lt = lambda k: small_t[:, k]

            def output_weights(c):
                s0 = slice(c * SPC, (c + 1) * SPC)
                b = c % 2
                if c >= 2:
                    v.wait_ge(y_full, c - 1)
                cr, cn = Cre[:, s0], Cim[:, s0]
                mark(v.tensor_copy(CLre[b][:, :, 0, :], cr))
                mark(v.tensor_copy(CLim[b][:, :, 0, :], cn))
                for j in range(1, SUB + 1):
                    a, b_ = (bc(pw[:, f, j, s0].rearrange("p (s o) -> p s o", o=1), [P, SPC, TCH]) for f in range(2))
                    mark(tt(lt(0), cr, a, ALU.mult))
                    mark(tt(lt(1), cn, b_, ALU.mult))
                    mark(tt(lt(2), cn, a, ALU.mult))
                    mark(tt(lt(3), cr, b_, ALU.mult))
                    settle()
                    mark(tt(CLre[b][:, :, j, :], lt(0), lt(1), ALU.add))
                    mark(tt(CLim[b][:, :, j, :], lt(2), lt(3), ALU.subtract))
                    settle()
                v.sem_inc(cl_done, 1)

            def softmax(a):
                blk, kv = a // KVH, a % KVH
                W = 2 * P if blk else P
                p_ = probs[a % 2]
                k0 = 2 * P - W
                if a >= 2:
                    v.wait_ge(tp_full, uses(tp_order, ("pt", a - 2, 1 if (a - 2) >= KVH else 0))[0] + 1)
                v.wait_ge(const_ready, 10)
                v.wait_ge(sc_full, a + 1)
                for h in range(QPK):
                    slope = 2.0 ** (-8.0 * (kv * QPK + h + 1) / HEADS)
                    mark(stt(p_[:, h, 0:W], neg_dist[:, k0:], slope,
                             sc[h % 2][:, (h // 2) * 2 * P:(h // 2) * 2 * P + W], ALU.mult, ALU.add))
                settle()
                v.sem_inc(sc_read, 1)
                st = lambda i: smx[:, a % 2, i, :]
                link(v.tensor_reduce(st(0), p_[:, :, 0:W], AX_X, ALU.max))
                snk = sink[:, kv * QPK:(kv + 1) * QPK]
                link(tt(st(0), st(0), snk, ALU.max))
                ts(st(1), st(0), -1.0, None, ALU.mult).then_inc(m_ready, 1)
                tt(st(2), snk, st(0), ALU.subtract).then_inc(m_ready, 1)
                v.wait_ge(exp_done, (QPK + 1) * (a + 1))
                link(tt(st(4), st(4), st(3), ALU.add))
                link(v.reciprocal(st(5), st(4)))
                for h in range(QPK):
                    mark(ts(p_[:, h, 0:W], p_[:, h, 0:W], smx[:, a % 2, 5, h:h + 1], None, ALU.mult))
                settle()
                v.sem_inc(p_done, 1)

            def scan_tile(c):
                v.wait_ge(bu_full, c + 1)
                v.wait_ge(e_done, c + 1)
                if c:
                    v.wait_ge(z_done, c)
                X, Y = (mb[i][:].rearrange("p (q n) -> p q n", q=SPC) for i in range(2))
                mark(tt(tb[0], X, Ec, ALU.mult))
                mark(tt(tb[1], Y, Es, ALU.mult))
                mark(tt(tb[2], Y, Ec, ALU.mult))
                mark(tt(tb[3], X, Es, ALU.mult))
                settle()
                v.sem_inc(bu_read, 1)
                mark(tt(tb[0], tb[0], tb[1], ALU.add))
                mark(tt(tb[2], tb[2], tb[3], ALU.subtract))
                settle()
                for q in range(SPC):
                    dec = bc(prm[:, 4, c * SPC + q:c * SPC + q + 1], [P, CH])
                    mark(v.tensor_tensor_scan(tb[1][:, q, :], dec, tb[0][:, q, :], 0.0, ALU.mult, ALU.add))
                    mark(v.tensor_tensor_scan(tb[3][:, q, :], dec, tb[2][:, q, :], 0.0, ALU.mult, ALU.add))
                settle()
                L = slice(0, CH - 1)
                wr, wi = tb[1][:, :, L], tb[3][:, :, L]
                if c:
                    v.wait_ge(y_full, c)
                mark(tt(tb[0][:, :, L], wr, Ec[:, :, L], ALU.mult))
                mark(tt(tb[2][:, :, L], wi, Es[:, :, L], ALU.mult))
                settle()
                mark(tt(Sre[:, :, 1:CH], tb[0][:, :, L], tb[2][:, :, L], ALU.subtract))
                settle()
                mark(tt(tb[0][:, :, L], wr, Es[:, :, L], ALU.mult))
                mark(tt(tb[2][:, :, L], wi, Ec[:, :, L], ALU.mult))
                settle()
                mark(tt(Sim[:, :, 1:CH], tb[0][:, :, L], tb[2][:, :, L], ALU.add))
                settle()
                v.sem_inc(S_done, 1)

            def gelu(c):
                v.wait_ge(z_full, c + 1)
                uc = uT[:, c].rearrange("p j n -> p (j n)")
                f1, f2 = (tb[i].rearrange("p q n -> p (q n)") for i in (1, 2))
                stt(f1, uc, d_col[:, c:c + 1], mb[1][:], ALU.mult, ALU.add).then_inc(yv_done, 1)
                v.wait_ge(z_sq, c + 1)
                link(ts(f2, f2, GELU_CUBE, 1.0, ALU.mult, ALU.add))
                v.wait_ge(yv_done, c + 1)
                tt(f2, f2, f1, ALU.mult).then_inc(z_arg, 1)
                v.wait_ge(z_th, c + 1)
                v.wait_ge(u4_loaded, 16 * SUB * SPC)
                stt(zT[:, c, :].rearrange("p (n j) -> p j n", j=SUB), f2.rearrange("p (j n) -> p j n", j=SUB), 1.0,
                    f1.rearrange("p (j n) -> p j n", j=SUB), ALU.add, ALU.mult).then_inc(z_done, 1)

            for t in range(TT):
                qk_normalise(t)
                if t == 0:
                    input_weights(0)
                if t == 1:
                    output_weights(0)
                if t > 0:
                    qk_turned(t - 1)
            qk_turned(TT - 1)
            for i in range(2 * DC + 1):
                if i % 2 == 0 and i < 2 * DC:
                    softmax(i // 2)
                if i % 4 == 0 and i >= 4:
                    gelu(i // 4 - 1)
                if i % 4 == 1:
                    scan_tile(i // 4)
                if i % 4 == 2 and i // 4 + 1 < CT_:
                    input_weights(i // 4 + 1)
                    output_weights(i // 4 + 1)
            v.wait_ge(gates_done, 2 * DC)
            for m in range(DC):
                G, V, A = merge_banks(m)
                t3 = merge_tmp(m)
                v.wait_ge(mg_act, m + 1)
                v.wait_ge(mg_full, 3 * (m + 1))
                mark(stt(t3[:, 1, :], t3[:, 0, :], 1.0, V[:], ALU.add, ALU.mult))
                mark(stt(t3[:, 2, :], ta_gate[:, m, :], 1.0, A[:], ALU.add, ALU.mult))
                settle()
                v.sem_inc(mg_free, 1)
                link(stt(t3[:, 1, :], ts_gate[:, m, :], 1.0, t3[:, 1, :], ALU.add, ALU.mult))
                stt(ts_gate[:, m, :], t3[:, 1, :], 0.25, t3[:, 2, :], ALU.mult, ALU.add).then_inc(merged_done, 1)
            v.wait_ge(x_again, 16)
            for h in range(2):
                for t in range(TT):
                    n = TT * h + t
                    v.wait_ge(pj_full, n_pj + n + 1)
                    xs = x2[:, t, h * 512:(h + 1) * 512]
                    stt(xs, pj[n % 2][:], 0.5, xs, ALU.mult, ALU.add).then_inc(x2_done, 1)
                    if h and t >= 1:
                        norm2(t - 1)
                    if h and t >= 2:
                        norm2_turned(t - 2)
            norm2(TT - 1)
            for t in range(TT - 2, TT):
                norm2_turned(t)
            v.wait_ge(lg_full, TT)
            link(v.tensor_copy(lg[:], sc[0][:, 0:TT * (NG + NE)].rearrange("p (t n) -> p t n", t=TT)))
            r = lambda i, n=NE: rt[:, i, :, 0:n]
            s_ = lambda i: rs_[:, i, :]
            col = lambda i: s_(i).rearrange("p (t o) -> p t o", o=1)
            rev = lambda n: bc(e_rev[:, NE - n:NE].rearrange("p (o n) -> p o n", o=1), [P, TT, n])

            def first_max(dst, src, top, n):
                link(tt(r(11, n), src, bc(col(top), [P, TT, n]), ALU.is_equal))
                link(tt(r(11, n), r(11, n), rev(n), ALU.mult))
                link(v.tensor_reduce(s_(15), r(11, n), AX_X, ALU.max))
                link(tt(dst, r(11, n), bc(col(15), [P, TT, n]), ALU.is_equal))

            coarse, fine = lg[:, :, 0:NG], lg[:, :, NG:NG + NE]
            link(v.tensor_reduce(s_(0), coarse, AX_X, ALU.max))
            tt(r(0, NG), coarse, bc(col(0), [P, TT, NG]), ALU.subtract).then_inc(r_dve, 1)
            v.wait_ge(const_ready, 10)
            first_max(r(1, NG), coarse, 0, NG)
            link(ts(r(1, NG), r(1, NG), HIDE, -HIDE, ALU.mult, ALU.add))
            link(tt(r(2).rearrange("p t (g e) -> p t g e", g=NG), fine.rearrange("p t (g e) -> p t g e", g=NG),
                    bc(r(1, NG).rearrange("p t (g o) -> p t g o", o=1), [P, TT, NG, EPG]), ALU.add))
            link(v.tensor_reduce(s_(1), r(2), AX_X, ALU.max))
            first_max(r(3), r(2), 1, NE)
            link(stt(r(4), r(3), -3 * HIDE, r(2), ALU.mult, ALU.add))
            link(v.tensor_reduce(s_(2), r(4), AX_X, ALU.max))
            first_max(r(5), r(4), 2, NE)
            link(tt(r(6), r(3), r(5), ALU.add))
            link(v.memset(r(7)[:, 0:1], 0.0))
            for t in range(1, TT):
                link(tt(rt[:, 7, t, :], rt[:, 7, t - 1, :], rt[:, 6, t - 1, :], ALU.add))
            link(tt(cnt[:], rt[:, 7, TT - 1, :], rt[:, 6, TT - 1, :], ALU.add))
            v.sem_inc(r_pe, 1)
            tt(s_(6), s_(2), s_(1), ALU.subtract).then_inc(r_dve, 1)
            v.wait_ge(r_act, 1)
            link(v.tensor_reduce(s_(3), r(0, NG), AX_X, ALU.add))
            link(v.reciprocal(s_(4), s_(3)))
            v.wait_ge(r_act, 2)
            link(ts(s_(7), s_(6), 1.0, None, ALU.add))
            link(v.reciprocal(s_(8), s_(7)))
            link(tt(s_(9), s_(8), s_(4), ALU.mult))
            link(tt(s_(10), s_(9), s_(6), ALU.mult))
            link(tt(r(8), r(3), bc(col(9), [P, TT, NE]), ALU.mult))
            link(tt(r(9), r(5), bc(col(10), [P, TT, NE]), ALU.mult))
            ev = lambda w: w.rearrange("p t e -> p e t")
            mark(tt(tg[:, :, :, 1], ev(r(8)), ev(r(9)), ALU.add))
            mark(v.tensor_copy(tg[:, :, :, 0], bc(tok_id[:, :].rearrange("p (o t) -> p o t", o=1), [P, NE, TT])))
            settle()
            v.wait_ge(lg_full, TT + 1)
            link(v.tensor_copy(r(10), sc[0][:, 0:TT * NE].rearrange("p (t e) -> p t e", t=TT)))
            link(ts(r(7), r(6), -float(4 * SEQ), float(4 * SEQ), ALU.mult, ALU.add))
            tt(pos[:].rearrange("p e t -> p t e"), r(10), r(7), ALU.add).then_inc(route_done, 1)

            v.wait_ge(route_done, 1)
            for e in range(NE):
                if e >= 2:
                    v.wait_ge(idx_full, e - 1)
                tt(pick[e % 2], bc(slot_no[:].rearrange("p (o n) -> p o n", o=1), [P, TT, CAP]),
                   bc(pos[:, e, :].rearrange("p (t o) -> p t o", o=1), [P, TT, CAP]), ALU.is_equal).then_inc(pick_done, 1)
                if e in (EARLY + 1, NE - 1):
                    k = 0 if e < NE - 1 else 1
                    lo, hi = (0, EARLY) if k == 0 else (EARLY, NE)
                    v.wait_ge(idx_full, hi)
                    got = sc[k][:, 128:128 + 2 * (hi - lo)].rearrange("p (e n) -> p n e", n=2)
                    v.tensor_copy(idx_all[:, lo:hi], got[:, 0, :])
                    v.tensor_copy(gate_all[:, lo:hi], got[:, 1, :]).then_inc(idx_done, 1)
            for k, oh in enumerate((3, 5)):
                link(tt(r(8), r(oh), bc(e_no[:].rearrange("p (o n) -> p o n", o=1), [P, TT, NE]), ALU.mult))
                link(v.tensor_reduce(s_(11), r(8), AX_X, ALU.add))
                link(tt(r(9), r(oh), r(10), ALU.mult))
                link(v.tensor_reduce(s_(12), r(9), AX_X, ALU.add))
                link(stt(s_(11), s_(11), float(CAP), s_(12), ALU.mult, ALU.add))
                for j in range(1, MORE + 1):
                    link(ts(s_(13), s_(12), float(j * CAP), float((NE - 1) * CAP), ALU.is_ge, ALU.mult))
                    link(tt(s_(11), s_(11), s_(13), ALU.add))
                link(v.tensor_copy(dest[:, k, :], s_(11)))
            v.wait_ge(lg_full, TT + 2)
            link(v.tensor_reduce(flag_f[:], mb[0][:, 0:NE], AX_X, ALU.max))
            v.tensor_scalar(flag[0:1, 0:1], flag_f[0:1, 0:1], float(CAP), None, ALU.is_gt).then_inc(flag_done, 1)

            def rows_turned(e4, n):
                for f in range(2):
                    v.wait_ge(xt_full, n * 2 + (f - 1))
                    tt(xgT[e4 % 2][:, 4 * f:4 * f + 4, :], tp[f][:].rearrange("p (k n) -> p k n", k=4), gain[f],
                       ALU.mult).then_inc(xt_done, 1)

            def swiglu(e4, n):
                b = e4 % 2
                v.wait_ge(th_done, n)
                stt(a1_e[b], th_e[b], 1.0, pj[b][:, 0:DE], ALU.add, ALU.mult).then_inc(act_done, 1)
                v.wait_ge(act_done, n * 2 - 1)
                stt(act_e[b], a1_e[b], 0.5, pj[b][:, DE:UP_N], ALU.mult, ALU.mult).then_inc(act_done, 1)

            rows_turned(0, 1)
            with v.Fori(0, NE // 2 - 1) as i:
                for r_ in range(2):
                    swiglu(r_, i * 2 + (r_ + 1))
                    rows_turned(1 - r_, i * 2 + (r_ + 2))
            swiglu(0, NE - 1)
            rows_turned(1, NE)
            swiglu(1, NE)
            over = v.value_load(flag[0:1, 0:1], min_val=0, max_val=1)
            with v.If(over > 0):
                for b in range(2):
                    v.wait_ge(y_stored[b], 8 * NE)
                with v.Fori(0, MORE) as j:
                    ts(pos[:], pos[:], float(-CAP), None, ALU.add).then_inc(o_pos, 1)
                    v.wait_ge(o_pos, j + 1)
                    v.sem_inc(gather_turn, 1)
                    with v.Fori(0, NE) as e:
                        tt(pick[0], bc(slot_no[:].rearrange("p (o n) -> p o n", o=1), [P, TT, CAP]),
                           bc(pos[:, bass.ds(e, 1), :].rearrange("p e (t o) -> p (e t) o", o=1), [P, TT, CAP]),
                           ALU.is_equal).then_inc(o_pick, 1)
                        v.wait_ge(o_idxf, j * NE + e + 1)
                        v.tensor_copy(idx[:, 0:1], sc[0][:, 128:129])
                        v.tensor_copy(gate[:, 0:1], sc[0][:, 129:130]).then_inc(o_idx, 1)
                        v.wait_ge(o_xt, j * NE + e + 1)
                        for f in range(2):
                            tt(xgT[0][:, 4 * f:4 * f + 4, :], tp[f][:].rearrange("p (k n) -> p k n", k=4), gain[f],
                               ALU.mult).then_inc(o_xtd, 1)
                        v.wait_ge(o_th, j * NE + e + 1)
                        stt(a1_e[0], th_e[0], 1.0, pj[0][:, 0:DE], ALU.add, ALU.mult).then_inc(o_act, 1)
                        v.wait_ge(o_act, (j * NE + e) * 2 + 1)
                        stt(act_e[0], a1_e[0], 0.5, pj[0][:, DE:UP_N], ALU.mult, ALU.mult).then_inc(o_act, 1)
                        v.wait_ge(o_st, (j * NE + e + 1) * 16)
            for t in range(TT):
                v.wait_ge(rows_back[t], 32)
                for k in range(2):
                    ins = tt(x2[:, t, :], x2[:, t, :], gath[2 * t + k], ALU.add)
                    if k:
                        ins.then_inc(sum_done, 1)
                    else:
                        link(ins)

        @block.tensor
        def _(pe):
            def fill(order, frees, key):
                n, b, used = uses(order, key)
                if used:
                    pe.wait_ge(frees[b], used)
                return b

            pe.wait_ge(const_ready, 3)
            for t in range(TT):
                pe.wait_ge(xn_done, t + 1)
                for f in range(2):
                    b = fill(tp_order, tp_free, ("h", t, f))
                    for k in range(4):
                        ins = pe.transpose(tp[b][:, k * P:(k + 1) * P], xn[:, t, (4 * f + k) * P:(4 * f + k + 1) * P], ident[:])
                    ins.then_inc(tp_full, 1)
            job_loaded(pe, J_U)
            pe.wait_ge(hT_done, TT)
            w = ring_w(J_U, DC, 512)
            for c in range(CT_):
                b = fill(pj_order, pj_free, ("u", c))
                for k in range(DC):
                    ins = pe.matmul(pj[b][:], w[:, k, c * P:(c + 1) * P], hT[:, k, :], start=k == 0, stop=k == DC - 1)
                ins.then_inc(pj_full, 1)
            b = fill(tp_order, tp_free, ("prm",))
            pe.wait_ge(rows_done, 1)
            for i, src in enumerate((13, 14, 15, 16, 6, 8, 7)):
                ins = pe.transpose(tp[b][:, i * ST:(i + 1) * ST], R(src), ident[0:ST, 0:ST])
            ins.then_inc(tp_full, 1)

            def turn_qk(t):
                pe.wait_ge(qk_norm, t + 1)
                b = fill(tp_order, tp_free, ("qt", t))
                q2 = qk_raw[t % 2].rearrange("p (a b) d -> p a (b d)", b=2)
                for k in range(4):
                    ins = pe.transpose(tp[b][:, k * P:(k + 1) * P], q2[:, k, :], ident[:])
                ins.then_inc(tp_full, 1)
                b = fill(tp_order, tp_free, ("kt", t))
                for g_ in range(KVH):
                    ins = pe.transpose(tp[b][:, g_ * P:(g_ + 1) * P],
                                       k_dup[t % 2][:, g_].rearrange("p r d -> p (r d)"), ident[:])
                ins.then_inc(tp_full, 1)

            for t in range(TT):
                for kind, job, width in (("q", J_Q, AW), ("kv", J_KV, 2 * KW)):
                    if t == 0:
                        job_loaded(pe, job)
                    w = ring_w(job, DC, width)
                    b = fill(pj_order, pj_free, (kind, t))
                    for k in range(DC):
                        ins = pe.matmul(pj[b][:, 0:width], hT[:, k, t * P:(t + 1) * P], w[:, k, :], start=k == 0, stop=k == DC - 1)
                    ins.then_inc(pj_full, 1)
                if t == 0:
                    pe.wait_ge(cexp_done, 1)
                    for f in range(2):
                        b = fill(tp_order, tp_free, ("ct", f))
                        for c in range(CT_):
                            ins = pe.transpose(tp[b][:, c * P:(c + 1) * P], c_exp[:, f, c].rearrange("p g s -> p (g s)"), ident[:])
                        ins.then_inc(tp_full, 1)
                else:
                    turn_qk(t - 1)
            turn_qk(TT - 1)

            def scores(a):
                blk, kv = a // KVH, a % KVH
                W = 2 * P if blk else P
                t0 = blk * P
                pe.wait_ge(kT_done, TT)
                if a:
                    pe.wait_ge(sc_read, a)
                for h in range(QPK):
                    hh = kv * QPK + h
                    ps = slice((hh % 2) * HD, (hh % 2) * HD + HD)
                    ins = pe.matmul(sc[h % 2][:, (h // 2) * 2 * P:(h // 2) * 2 * P + W], qT[ps, hh // 2, t0:t0 + P],
                                    kT[ps, kv, t0 + P - W:t0 + P], start=True, stop=True)
                ins.then_inc(sc_full, 1)

            def turn_probs(a):
                blk = a // KVH
                pe.wait_ge(p_done, a + 1)
                for f in range(2 if blk else 1):
                    b = fill(tp_order, tp_free, ("pt", a, f))
                    for h in range(QPK):
                        ins = pe.transpose(tp[b][:, h * P:(h + 1) * P], probs[a % 2][:, h, f * P:(f + 1) * P], ident[:])
                    ins.then_inc(tp_full, 1)

            n_pt = [0]

            def values(a):
                blk, kv = a // KVH, a % KVH
                nf = 2 if blk else 1
                n_pt[0] += nf
                pe.wait_ge(pT_done, n_pt[0])
                pe.wait_ge(v_done, TT)
                b = fill(pj_order, pj_free, ("av", a))
                ph = pT.rearrange("p f (a b) q -> p f b a q", b=2)
                for odd in range(2):
                    for f in range(nf):
                        ins = pe.matmul(pj[b][odd * HD:(odd + 1) * HD, 0:2 * P].rearrange("p (a q) -> p a q", a=2),
                                        v_tok[:, blk - nf + 1 + f, kv * HD:(kv + 1) * HD], ph[:, f, odd],
                                        start=f == 0, stop=f == nf - 1)
                ins.then_inc(pj_full, 1)

            def turn_input_weights(c):
                pe.wait_ge(w1_done, c + 1)
                for f in range(2):
                    b = fill(tp_order, tp_free, ("w", c, f))
                    for q in range(SPC):
                        ins = pe.transpose(tp[b][:, q * P:(q + 1) * P], w1[:, f, q].rearrange("p i c -> p (i c)"), ident[:])
                    ins.then_inc(tp_full, 1)
                pe.wait_ge(cl_done, c + 1)
                b = fill(tp_order, tp_free, ("k", c))
                for q in range(SPC):
                    s = c * SPC + q
                    dst = tp[b][0:TCH, q * P:(q + 1) * P]
                    pe.matmul(dst, Bre[:, s, :], CLre[c % 2][:, q, 0:SUB, :], start=True, stop=False)
                    ins = pe.matmul(dst, Bim[:, s, :], CLim[c % 2][:, q, 0:SUB, :], start=False, stop=True)
                ins.then_inc(tp_full, 1)

            def chunk_inputs(c):
                pe.wait_ge(w1T_done, 2 * (c + 1))
                pe.wait_ge(u4_loaded, 16 * SUB * SPC)
                if c:
                    pe.wait_ge(yv_done, c)
                    pe.wait_ge(y_evac, c)
                for q in range(SPC):
                    for f in range(2):
                        ins = pe.matmul(mb[f][:, q * P:(q + 1) * P], w1T[:, f, q, :], u4[:, c * SPC + q, :], start=True, stop=True)
                ins.then_inc(bu_full, 1)

            def chunk_outputs(c):
                pe.wait_ge(S_done, c + 1)
                pe.wait_ge(toep_done, SUB * (c + 1))
                yb = mb[0][:].rearrange("p (j c) -> p j c", j=SUB)
                for q in range(SPC):
                    dst = yb[:, :, q * TCH:(q + 1) * TCH]
                    pe.matmul(dst, u4[:, c * SPC + q, :], toep[:, q, :], start=q == 0, stop=False, skip_group_check=True)
                for q in range(SPC):
                    dst = yb[:, :, q * TCH:(q + 1) * TCH]
                    pe.matmul(dst, Sre[:, q, :], CLre[c % 2][:, q, 1:, :], start=False, stop=False, skip_group_check=True)
                    ins = pe.matmul(dst, Sim[:, q, :], CLim[c % 2][:, q, 1:, :], start=False, stop=q == SPC - 1, skip_group_check=True)
                ins.then_inc(y_full, 1)

            def turn_outputs(c):
                pe.wait_ge(y_evac, c + 1)
                yt = tb[0].rearrange("p q n -> p (q n)")
                for j in range(SUB):
                    ins = pe.transpose(mb[1][:, j * P:(j + 1) * P], yt[:, j * P:(j + 1) * P], ident[:])
                ins.then_inc(z_full, 1)

            for i in range(2 * DC + 1):
                if i < 2 * DC:
                    job = J_G + i // 4
                    if i % 4 == 0:
                        job_loaded(pe, job)
                    w = ring_w(job, DC, 512)
                    b = fill(pj_order, pj_free, ("gate", i))
                    for k in range(DC):
                        ins = pe.matmul(pj[b][:], w[:, k, (i % 4) * P:(i % 4 + 1) * P], hT[:, k, :], start=k == 0, stop=k == DC - 1)
                    ins.then_inc(pj_full, 1)
                if i % 4 == 0 and i >= 4:
                    turn_outputs(i // 4 - 1)
                if i % 4 == 0 and i < 2 * DC:
                    turn_input_weights(i // 4)
                if i % 4 == 1:
                    chunk_inputs(i // 4)
                if i % 2 == 0 and i < 2 * DC:
                    scores(i // 2)
                if i % 2 == 1:
                    if i % 4 == 3:
                        chunk_outputs(i // 4)
                    turn_probs(i // 2)
                if i % 2 == 0 and i >= 2:
                    values(i // 2 - 1)
            job_loaded(pe, J_AU)
            pe.wait_ge(gates_done, 2 * DC)
            pe.wait_ge(z_done, CT_)
            pe.wait_ge(av_done, NQ)
            pe.wait_ge(sc_read, NQ)
            for m in range(DC):
                if m >= 2:
                    pe.wait_ge(mg_free, m - 1)
                if m % HM == 0:
                    job_loaded(pe, J_GLU[m // HM])
                glu = glu_w(J_GLU[m // HM])
                for dst, w, c0, src in zip(merge_banks(m), (glu[:, 1], glu[:, 0], ring_w(J_AU, 4, D)),
                                           (m % HM * P, m % HM * P, m * P), (zT, zT, qT)):
                    for k in range(4):
                        ins = pe.matmul(dst[:], w[:, k, c0:c0 + P], src[:, k, :], start=k == 0, stop=k == 3)
                    ins.then_inc(mg_full, 1)
            pe.wait_ge(merged_done, DC)

            def turn_norm2(t):
                pe.wait_ge(n2_done, t + 1)
                if t:
                    pe.wait_ge(h2T_done, 2 * t)
                else:
                    for b in range(2):
                        pe.wait_ge(tp_free[b], (n_tp + 1 - b) // 2)
                for f in range(2):
                    for k in range(4):
                        ins = pe.transpose(tp[f][:, k * P:(k + 1) * P], xg[t % 2][:, (4 * f + k) * P:(4 * f + k + 1) * P], ident[:])
                    ins.then_inc(tp_full, 1)

            def router(t):
                pe.wait_ge(h2T_done, 2 * (t + 1))
                for k in range(DC):
                    ins = pe.matmul(sc[0][:, t * (NG + NE):(t + 1) * (NG + NE)], xgT[t % 2][:, k, :], rw[:, k, :],
                                    start=k == 0, stop=k == DC - 1)
                ins.then_inc(lg_full, 1)

            for h in range(2):
                job_loaded(pe, J_OUT + h)
                w = ring_w(J_OUT + h, DC, 512)
                for t in range(TT):
                    n = TT * h + t
                    if n >= 2:
                        pe.wait_ge(x2_done, n - 1)
                    for k in range(DC):
                        ins = pe.matmul(pj[n % 2][:], ts_gate[:, k, t * P:(t + 1) * P], w[:, k, :], start=k == 0, stop=k == DC - 1)
                    ins.then_inc(pj_full, 1)
                    if h and t >= 2:
                        turn_norm2(t - 2)
                        router(t - 2)
            for t in range(TT - 2, TT):
                turn_norm2(t)
                router(t)
            pe.wait_ge(r_pe, 1)
            pe.wait_ge(const_ready, 10)
            flat = lambda i: rt[:, i].rearrange("p t e -> p (t e)")
            pe.matmul(sc[0][:, 0:TT * NE], before[:], flat(6), start=True, stop=False)
            pe.matmul(sc[0][:, 0:TT * NE], ones[:], flat(7), start=False, stop=True).then_inc(lg_full, 1)
            pe.matmul(mb[0][:, 0:NE], ones[:], cnt[:], start=True, stop=True).then_inc(lg_full, 1)

            pe.wait_ge(route_done, 1)
            for e in range(NE):
                k = 0 if e < EARLY else 1
                c0 = 128 + 2 * (e - EARLY * k)
                pe.wait_ge(pick_done, e + 1)
                for t in range(TT):
                    ins = pe.matmul(sc[k][:, c0:c0 + 2], pick[e % 2][:, t, :], tg[:, e, t, :], start=t == 0, stop=t == TT - 1)
                ins.then_inc(idx_full, 1)

            def turn_rows(e4, e, n_rows):
                pe.wait_ge(gathered[e4 % 2], n_rows)
                for f in range(2):
                    if not (isinstance(e, int) and e == 0):
                        pe.wait_ge(xt_done, e * 2 + (f - 1))
                    for k in range(4):
                        ins = pe.transpose(tp[f][:, k * P:(k + 1) * P], xg[e4 % 2][:, (4 * f + k) * P:(4 * f + k + 1) * P], ident[:])
                    ins.then_inc(xt_full, 1)

            def up(e4, e, n_loaded):
                pe.wait_ge(ring_loaded[e4], n_loaded)
                pe.wait_ge(xt_done, (e + 1) * 2)
                if not (isinstance(e, int) and e < 2):
                    pe.wait_ge(act_done, e * 2 - 2)
                w = ring[e4].rearrange("p (k n) -> p k n", k=DC)
                for k in range(DC):
                    ins = pe.matmul(pj[e4 % 2][:], xgT[e4 % 2][:, k, :], w[:, k, :], start=k == 0, stop=k == DC - 1)
                ins.then_inc(up_full, 1)

            def turn_act(n4, e):
                e4 = (n4 + 3) % 4
                pe.wait_ge(act_done, (e + 1) * 2)
                if not (isinstance(e, int) and e == 0):
                    pe.wait_ge(at_done, e)
                for k in range(2):
                    ins = pe.transpose(sc[1][:, k * P:(k + 1) * P], act_e[e4 % 2][:, k * P:(k + 1) * P], ident[:])
                ins.then_inc(at_full, 1)

            def down_(e4, e, n_loaded):
                pe.wait_ge(at_done, e + 1)
                pe.wait_ge(down_loaded[e4], n_loaded)
                if not (isinstance(e, int) and e == 0):
                    pe.wait_ge(y_scaled, e * 2)
                for h in range(2):
                    for k in range(2):
                        ins = pe.matmul(mb[h][:], actT[e4 % 2][:, k, :], down[e4][:, k, h * 512:(h + 1) * 512], start=k == 0, stop=k == 1)
                ins.then_inc(dn_full, 1)

            front = [loads_until(s, NJ - 1) for s in range(3)] + [0]

            def step(e4, e, rnd, first=False, last=False):
                up(e4, e, rnd * 16 + (front[e4] + 16))
                if not first:
                    turn_act(e4, e - 1)
                if not last:
                    n4 = (e4 + 1) % 4
                    turn_rows(n4, e + 1, (rnd if e4 < 3 else rnd + 1) * 32 + (16 * (n4 // 2) + 16))
                if not first:
                    p4 = (e4 + 3) % 4
                    down_(p4, e - 1, (rnd if e4 else rnd - 1) * 16 + 16)

            pe.wait_ge(idx_done, 2)
            turn_rows(0, 0, 16)
            for e in range(4):
                step(e, e, 0, first=e == 0)
            with pe.Fori(0, NE // 4 - 2) as i:
                for r in range(4):
                    step(r, i * 4 + (r + 4), i + 1)
            for e in range(NE - 4, NE):
                step(e % 4, e, e // 4, last=e == NE - 1)
            turn_act(0, NE - 1)
            down_(3, NE - 1, 16 * (NE // 4))
            pe.wait_ge(dn_full, NE)
            pe.sem_inc(o_dn, 1)
            pe.wait_ge(flag_done, 1)
            over = pe.value_load(flag[0:1, 0:1], min_val=0, max_val=1)
            with pe.If(over > 0):
                w = ring[0].rearrange("p (k n) -> p k n", k=DC)
                with pe.Fori(0, MORE) as j:
                    with pe.Fori(0, NE) as e:
                        b = j * NE + e
                        pe.wait_ge(o_pick, b + 1)
                        for t in range(TT):
                            ins = pe.matmul(sc[0][:, 128:130], pick[0][:, t, :],
                                            tg[:, bass.ds(e, 1), t, :].rearrange("p e n -> p (e n)"), start=t == 0, stop=t == TT - 1)
                        ins.then_inc(o_idxf, 1)
                        pe.wait_ge(o_gath, (b + 1) * 16)
                        for k in range(DC):
                            ins = pe.transpose(tp[k // 4][:, (k % 4) * P:(k % 4 + 1) * P], xg[0][:, k * P:(k + 1) * P], ident[:])
                        ins.then_inc(o_xt, 1)
                        pe.wait_ge(o_xtd, (b + 1) * 2)
                        pe.wait_ge(o_w, (b + 1) * 32)
                        for k in range(DC):
                            ins = pe.matmul(pj[0][:], xgT[0][:, k, :], w[:, k, :], start=k == 0, stop=k == DC - 1)
                        ins.then_inc(o_up, 1)
                        pe.wait_ge(o_act, (b + 1) * 2)
                        for k in range(2):
                            ins = pe.transpose(sc[1][:, k * P:(k + 1) * P], act_e[0][:, k * P:(k + 1) * P], ident[:])
                        ins.then_inc(o_at, 1)
                        pe.wait_ge(o_atd, b + 1)
                        for h in range(2):
                            for k in range(2):
                                ins = pe.matmul(mb[h][:], actT[0][:, k, :], down[0][:, k, h * 512:(h + 1) * 512], start=k == 0, stop=k == 1)
                        ins.then_inc(o_dn, 1)


_INS = ['x', 'norm_mix', 'w_in', 'ssm_lam_re', 'ssm_lam_im', 'ssm_log_dt', 'ssm_b_re', 'ssm_b_im', 'ssm_c_re',
        'ssm_c_im', 'ssm_d', 'w_ssm_glu_val', 'w_ssm_glu_gate', 'q_norm', 'k_norm', 'attn_sinks', 'w_attn_up',
        'w_out', 'norm_ffn', 'w_coarse', 'w_fine', 'w_expert_up', 'w_expert_down']
_OUTS = [((1, 512, 1024), 'float32')]


def kernel(**inputs):
    import numpy as _np
    import concourse.bacc as _bacc
    from concourse import mybir as _mybir
    from concourse.bass_utils import run_bass_kernel_spmd as _run

    nc = _bacc.Bacc("TRN2", target_bir_lowering=False, num_devices=1)
    arrays, args = {}, []
    for name in _INS:
        a = _np.ascontiguousarray(inputs[name])
        arrays[f"in_{name}_dram"] = a
        args.append(nc.dram_tensor(f"in_{name}_dram", a.shape, _mybir.dt.from_np(a.dtype), kind="ExternalInput").ap())
    for i, (shape, dtype) in enumerate(_OUTS):
        dt = _mybir.dt.from_np(_np.dtype(dtype))
        args.append(nc.dram_tensor(f"out_{i}_dram", shape, dt, kind="ExternalOutput").ap())
    hybrid_layer(nc, *args)
    r = _run(nc, [arrays], core_ids=[0])
    got = tuple(r.results[0][f"out_{i}_dram"] for i in range(len(_OUTS)))
    return got[0]
```

```python
import math
from contextlib import ExitStack

import concourse.bass as bass
from concourse import mybir

F32 = mybir.dt.float32
F32R = mybir.dt.float32r
I32 = mybir.dt.int32
U32 = mybir.dt.uint32
ALU = mybir.AluOpType
ACT = mybir.ActivationFunctionType
AX_X = mybir.AxisListType.X

P = 128
EPS = 1e-6
MAGIC = 1.5 * 2.0 ** 23
TWO_PI_HIGH = 6.28125
TWO_PI_LOW = 2.0 * math.pi - TWO_PI_HIGH
HIDE = 1e30
GELU_IN = math.sqrt(2.0 / math.pi)
GELU_CUBE = 0.044715


def hybrid_layer(nc, x, norm_mix, w_in, lam_re, lam_im, log_dt, b_re, b_im, c_re, c_im, d_skip,
                 w_glu_val, w_glu_gate, q_norm, k_norm, sinks, w_attn_up, w_out, norm_ffn,
                 w_coarse, w_fine, w_up, w_down, out):
    SEQ, D = x.shape[1], x.shape[2]
    DC = D // P
    TT = SEQ // P
    SSM_W = d_skip.shape[1]
    CT_ = SSM_W // P
    GROUPS, STATE = lam_re.shape[1], lam_re.shape[2]
    GCH = b_re.shape[3]
    ST = GROUPS * STATE // P
    SPC = ST // CT_
    SUB = 4
    CH = SEQ // SUB
    TCH = 2 * GCH
    HEADS, HD = sinks.shape[1], q_norm.shape[1]
    KVH = 2
    QPK = HEADS // KVH
    AW = HEADS * HD
    KW = KVH * HD
    NG = w_coarse.shape[2]
    NE = w_fine.shape[2]
    EPG = NE // NG
    DE = w_down.shape[2]
    UP_N = 2 * DE
    CAP = P
    MORE = SEQ // CAP - 1
    EARLY = 2
    NQ = 2 * KVH * QPK // 2
    assert CH == P and TCH * SUB == P and SPC * TCH == P and HD * 2 == P and UP_N == 512

    h2_rows = nc.dram_tensor("h2_rows", [SEQ, D], F32, kind="Internal").ap()
    y_rows = nc.dram_tensor("y_rows", [NE * CAP, D], F32, kind="Internal").ap()
    y_all = nc.dram_tensor("y_all", [NE * SEQ, D], F32, kind="Internal").ap()

    with ExitStack() as ctx:
        def sb(name, shape, dt=F32):
            return ctx.enter_context(nc.sbuf_tensor(name, shape, dt))

        def sem(name):
            return ctx.enter_context(nc.semaphore(name))

        SLOT = DC * 512
        DOWN = 2 * D
        SSM_FLOATS = 2 * 512 + 2 * 512 + 2 * SPC * (SUB + 1) * TCH + 512 + 2 * 512 + 2 * 512 + 2 * 512 + 6 * 512
        PIECE = DC * 256
        sizes = dict(raw=2 * PIECE, pair=4 * PIECE, ht=2 * SLOT, uz=CT_ * 512, qy=4 * 512, gs=SLOT, ga=SLOT, u4=ST * CH,
                     att=3 * 1024, v=TT * KW, kt=KVH * SEQ, ssm=max(SSM_FLOATS, 4 * DOWN))
        arena_at = (nc.sbuf_base + 31) // 32 * 32
        front = ("raw", "pair", "ht")
        n_front = sum(sizes[name] for name in front)
        arenas = [sb("arena_front", [P, n_front]), sb("arena_back", [P, sum(sizes.values()) - n_front])]
        at, off = {}, 0
        for name, n in sizes.items():
            at[name] = off
            off += n

        def part(name, start, size, /, **dims):
            o = at[name] + start
            v = arenas[0][:, o:o + size] if name in front else arenas[1][:, o - n_front:o - n_front + size]
            if dims:
                v = v.rearrange("row (%s) -> row %s" % (" ".join(dims), " ".join(dims)),
                                **{k: d for k, d in list(dims.items())[1:]})
            return v

        def rounded(name, where, start, shape):
            return nc.alloc_sbuf_tensor_at(name, shape, F32R, offset=arena_at + 4 * (at[where] + start))

        raw = [part("raw", s * PIECE, PIECE) for s in range(2)]
        places = [("pair", 0), ("pair", 2 * PIECE), ("ht", 0), ("ht", 2 * PIECE)]
        w_high = [rounded(f"w_high{s}", name, o, [P, PIECE]) for s, (name, o) in enumerate(places)]
        w_low = [rounded(f"w_low{s}", name, o + PIECE, [P, PIECE]) for s, (name, o) in enumerate(places)]
        h_high = rounded("h_high", "ht", 0, [P, DC, SEQ])
        h_low = rounded("h_low", "ht", SLOT, [P, DC, SEQ])
        m_high = rounded("m_high", "gs", 0, [P, DC, SEQ])
        m_low = rounded("m_low", "ga", 0, [P, DC, SEQ])
        down = [part("ssm", s * DOWN, DOWN, k=2, n=D) for s in range(4)]
        x_in = part("gs", 0, SLOT, t=TT, d=D)
        xn = part("ga", 0, SLOT, t=TT, d=D)
        mix_gain = part("qy", 0, D)
        ffn_gain = part("kt", 0, D)
        x2 = part("uz", 0, SLOT, t=TT, d=D)
        ts_gate = part("gs", 0, SLOT, m=DC, t=SEQ)
        ta_gate = part("ga", 0, SLOT, m=DC, t=SEQ)
        uT = part("uz", 0, CT_ * 512, c=CT_, j=SUB, n=CH)
        zT = part("uz", 0, CT_ * 512, c=CT_, t=SEQ)
        qT = part("qy", 0, 4 * 512, h=4, t=SEQ)
        u4 = part("u4", 0, ST * CH, s=ST, n=CH)
        qk_raw = [part("att", 256 * i, 256, h=4, d=HD) for i in range(2)]
        qk_sq = [part("att", 512 + 256 * i, 256, h=4, d=HD) for i in range(2)]
        qk_nrm = [part("att", 1024 + 256 * i, 256, h=4, d=HD) for i in range(4)]
        v_tok = part("v", 0, TT * KW, t=TT, n=KW)
        kT = part("kt", 0, KVH * SEQ, g=KVH, t=SEQ)
        probs = [part("att", 1024 * i, 1024, h=QPK, k=2 * P) for i in range(2)]
        pT = part("att", 2048, 1024, f=2, h=QPK, q=P)
        def R(i):
            return part("att", i * P, P)[0:ST, :]

        o = 0
        ssm = {}
        for name, n in [("Bre", 512), ("Bim", 512), ("Cre", 512), ("Cim", 512), ("CL", 2 * SPC * (SUB + 1) * TCH), ("toep", 512), ("Ec", 512), ("Es", 512),
                        ("w1T", 1024), ("w1", 1024)] + [(f"t{i}", 512) for i in range(4)] + [("Sre", 512), ("Sim", 512)]:
            ssm[name] = (o, n)
            o += n

        def spart(name, start=0, size=None, /, **dims):
            return part("ssm", ssm[name][0] + start, size or ssm[name][1], **dims)

        Bre, Bim = (spart(n, s=ST, c=TCH) for n in ("Bre", "Bim"))
        Cre, Cim = (spart(n, s=ST, c=TCH) for n in ("Cre", "Cim"))
        NCL = SPC * (SUB + 1) * TCH
        CLre, CLim = (spart("CL", f * NCL, NCL, s=SPC, j=SUB + 1, c=TCH) for f in range(2))
        toep = spart("toep", q=SPC, n=SUB * TCH)
        Ec, Es = spart("Ec", q=SPC, n=CH), spart("Es", q=SPC, n=CH)
        w1T = spart("w1T", f=2, q=SPC, n=P)
        w1 = spart("w1", f=2, q=SPC, i=SUB, c=TCH)
        tb = [spart(f"t{i}", q=SPC, n=CH) for i in range(4)]
        Sre, Sim = spart("Sre", q=SPC, n=CH), spart("Sim", q=SPC, n=CH)
        xg = [part("raw", D * i, D) for i in range(2)]
        xgT = [part("raw", 2 * D + D * i, D, k=DC, n=P) for i in range(2)]
        y_out = [part("gs", D * i, D) for i in range(2)]
        th_e = [part("gs", 2048 + 256 * i, 256) for i in range(2)]
        a1_e = [part("gs", 2560 + 256 * i, 256) for i in range(2)]
        act_e = [part("gs", 3072 + 256 * i, 256) for i in range(2)]
        actT = [part("gs", 3584 + 256 * i, 256, k=2, n=P) for i in range(2)]
        pick = [rounded(f"pick{i}", "u4", 512 * i, [P, TT, CAP])[:] for i in range(2)]
        gath = [part("pair", D * i, D) for i in range(2 * TT)]

        ident = sb("ident", [P, P])
        before = sb("before", [P, P])
        ones = sb("ones", [P, P])
        slot_no = sb("slot_no", [P, CAP])
        neg_dist = sb("neg_dist", [P, 2 * P])
        tok_id = sb("tok_id", [P, TT])
        e_no = sb("e_no", [P, NE])
        e_rev = sb("e_rev", [P, NE])
        par_i = sb("par_i", [P, 1], I32)
        par = sb("par", [P, 3])
        half_col = sb("half_col", [P, 16])
        halfpi = sb("halfpi", [P, 1])
        d_col = sb("d_col", [P, CT_])
        qg = sb("qg", [P, 3])
        sink = sb("sink", [P, HEADS])
        ssq = sb("ssq", [P, 2 * TT])
        rstd = sb("rstd", [P, 2 * TT])
        qss = sb("qss", [P, 3 * TT, 4])
        qrs = sb("qrs", [P, 3 * TT, 4])
        ldt = sb("ldt", [ST, 2, 2])
        prm = sb("prm", [P, 7, ST])
        b_raw = spart("Sre", 0, 512, f=2, s=ST, h=GCH)
        c_raw = spart("Sim", 0, 512, f=2, c=CT_, p=STATE)
        c_exp = part("ga", 0, 1024, f=2, c=CT_, g=2, p=STATE)
        pw = sb("pw", [P, 2, SUB + 1, ST])
        e1 = sb("e1", [P, 2, 3, ST])
        sc_t = sb("sc_t", [P, 6, ST])
        et = sb("et", [P, 4, SPC, CH // 2])
        small_t = sb("small_t", [P, 4, SPC, TCH])
        smx = sb("smx", [P, 2, 6, QPK])
        rw = sb("rw", [P, DC, NG + NE])
        rt = part("att", 0, 12 * TT * NE, f=12, t=TT, e=NE)
        lg = part("att", 768, TT * (NG + NE), t=TT, n=NG + NE)
        rs_ = sb("rs_", [P, 16, TT])
        tg = rounded("tg", "att", 1024, [P, NE, TT, 4])
        pos = sb("pos", [P, NE, TT])
        cnt = sb("cnt", [P, NE])
        flag_f = sb("flag_f", [P, 1])
        flag = sb("flag", [1, 1], I32)
        idx_all = sb("idx_all", [P, NE], U32)
        gate_all = sb("gate_all", [P, NE])
        idx = sb("idx", [P, 2], U32)
        gate = sb("gate", [P, 1])
        dest = sb("dest", [P, 2, TT], U32)

        def bank(name):
            return ctx.enter_context(nc.psum_tensor(name, [P, 512], F32))

        pj = [bank("pj0"), bank("pj1")]
        tp = [bank("tp0"), bank("tp1")]
        sc = [bank("sc0"), bank("sc1")]
        mb = [bank("m0"), bank("m1")]

        const_ready = sem("const_ready")
        small_loaded, rows_loaded = sem("small_loaded"), sem("rows_loaded")
        mix_gain_loaded, ffn_gain_loaded = sem("mix_gain_loaded"), sem("ffn_gain_loaded")
        x_loaded = [sem(f"x_loaded{t}") for t in range(TT)]
        x_again = sem("x_again")
        ring_loaded = [sem(f"ring_loaded{s}") for s in range(4)]
        raw_loaded = [sem("raw_loaded0"), sem("raw_loaded1")]
        high_done, low_done_v, low_done_p = sem("high_done"), sem("low_done_v"), sem("low_done_p")
        h_high_done = sem("h_high_done")
        zy_high, zy_low = sem("zy_high"), sem("zy_low")
        m_high_done, m_low_done = sem("m_high_done"), sem("m_low_done")
        down_loaded = [sem(f"down_loaded{s}") for s in range(4)]
        sq_done = sem("sq_done")
        var_done = sem("var_done")
        rstd_done = sem("rstd_done")
        xn_done = sem("xn_done")
        hT_done = sem("hT_done")
        pj_full, tp_full = sem("pj_full"), sem("tp_full")
        pj_free = [sem("pj_free0"), sem("pj_free1")]
        tp_free = [sem("tp_free0"), sem("tp_free1")]
        uT_done, u4_loaded = sem("uT_done"), sem("u4_loaded")
        qk_evac, qk_var, qk_rstd, qk_norm = sem("qk_evac"), sem("qk_var"), sem("qk_rstd"), sem("qk_norm")
        v_done, qT_done, kT_done = sem("v_done"), sem("qT_done"), sem("kT_done")
        gates_done = sem("gates_done")
        sc_full, sc_read, m_ready, exp_done, p_done = (sem(n) for n in ("sc_full", "sc_read", "m_ready", "exp_done", "p_done"))
        pT_done, av_done = sem("pT_done"), sem("av_done")
        prm_act, prm_dve = sem("prm_act"), sem("prm_dve")
        rows_done, prm_done, cexp_done, ct_done, bbd_done = (sem(n) for n in ("rows_done", "prm_done", "cexp_done", "ct_done", "bbd_done"))
        rot_done, pow_ready = sem("rot_done"), sem("pow_ready")
        e_done = sem("e_done")
        w1_done, w1T_done, cl_done, toep_done = (sem(n) for n in ("w1_done", "w1T_done", "cl_done", "toep_done"))
        bu_full, bu_read, S_done = sem("bu_full"), sem("bu_read"), sem("S_done")
        y_full, y_evac, z_full, yv_done = (sem(n) for n in ("y_full", "y_evac", "z_full", "yv_done"))
        z_sq, z_arg, z_th, z_done = (sem(n) for n in ("z_sq", "z_arg", "z_th", "z_done"))
        mg_full, mg_act, mg_free, merged_done = (sem(n) for n in ("mg_full", "mg_act", "mg_free", "merged_done"))
        x2_done = sem("x2_done")
        n2_done, h2T_done, lg_full = (sem(n) for n in ("n2_done", "h2T_done", "lg_full"))
        h2_stored = [sem(f"h2_stored{t}") for t in range(TT)]
        r_dve, r_act, r_pe = sem("r_dve"), sem("r_act"), sem("r_pe")
        route_done, flag_done = sem("route_done"), sem("flag_done")
        dve_chain, act_chain, pool_chain = sem("dve_chain"), sem("act_chain"), sem("pool_chain")
        pick_done, idx_full, idx_done = (sem(n) for n in ("pick_done", "idx_full", "idx_done"))
        gathered = [sem("gathered0"), sem("gathered1")]
        y_stored = [sem("y_stored0"), sem("y_stored1")]
        xt_full, xt_done, up_full, th_done, act_done = (sem(n) for n in ("xt_full", "xt_done", "up_full", "th_done", "act_done"))
        at_full, at_done, dn_full, y_scaled = (sem(n) for n in ("at_full", "at_done", "dn_full", "y_scaled"))
        o_pick, o_idxf, o_idx, o_gath, o_xt, o_xtd, o_up = (sem(n) for n in ("o_pick", "o_idxf", "o_idx", "o_gath", "o_xt", "o_xtd", "o_up"))
        o_th, o_act, o_at, o_atd, o_dn, o_y, o_st, o_w, o_pos, o_copy = (sem(n) for n in ("o_th", "o_act", "o_at", "o_atd", "o_dn", "o_y", "o_st", "o_w", "o_pos", "o_copy"))
        rows_back = [sem(f"rows_back{t}") for t in range(TT)]
        idx_taken = sem("idx_taken")
        gather_turn = sem("gather_turn")
        sum_done, out_stored = sem("sum_done"), sem("out_stored")

        pj_order, tp_order = [], []
        for t in range(TT):
            tp_order += [("h", t, f) for f in range(2)]
        pj_order += [("u", c) for c in range(CT_)]
        tp_order += [("prm",), ("ct", 0), ("ct", 1)]
        for j in range(3 * TT):
            pj_order += [("qkv", j)]
            if j >= 2:
                tp_order += [("qkt", j - 2)]
        tp_order += [("qkt", j) for j in range(3 * TT - 2, 3 * TT)]
        for i in range(2 * DC + 1):
            if i < 2 * DC:
                pj_order += [("gate", i)]
            if i % 4 == 0 and i < 2 * DC:
                tp_order += [("w", i // 4, 0), ("w", i // 4, 1)]
            if i % 4 == 1:
                tp_order += [("k", i // 4)]
            if i % 2 == 1:
                tp_order += [("pt", i // 2, f) for f in range(2 if i // 2 >= KVH else 1)]
            if i % 2 == 0 and i >= 2:
                pj_order += [("av", i // 2 - 1)]
        n_pj, n_tp = len(pj_order), len(tp_order)

        def uses(order, key):
            n = order.index(key)
            return n, n % 2, n // 2

        KV0 = SSM_W + AW
        G0 = KV0 + 2 * KW
        pieces = [("in", 0), ("in", 256), ("in", KV0), ("in", SSM_W), ("in", SSM_W + 256)] + \
                 [("in", G0 + 256 * i) for i in range(DC)] + [("merge", P * m) for m in range(DC)] + \
                 [("out", 256 * i) for i in range(D // 256)]
        NP = len(pieces)
        P_U, P_QKV, P_G, P_M, P_OUT = 0, 2, 5, 5 + DC, 5 + 2 * DC
        NOUT = NP - P_OUT
        on_pool = [n for n in range(NP) if n == 0 or P_G <= n < P_M]
        on_dve = [n for n in range(NP) if n not in on_pool]

        def split_place(n):
            return n % 2 if n < P_OUT + 2 else 2 + n % 2

        ring = [part(name, o, SLOT) for name, o in (places[split_place(P_OUT + e)] for e in range(4))]

        def piece_size(n):
            return 3 * 512 if pieces[n][0] == "merge" else PIECE

        def piece_used(eng, n):
            if n < P_QKV:
                eng.wait_ge(pj_full, pj_order.index(("u", 2 * n + 1)) + 1)
            elif n < P_G:
                eng.wait_ge(pj_full, pj_order.index(("qkv", TT * (n - P_QKV + 1) - 1)) + 1)
            elif n < P_M:
                eng.wait_ge(pj_full, pj_order.index(("gate", 2 * (n - P_G) + 1)) + 1)
            elif n < P_OUT:
                eng.wait_ge(mg_full, 3 * (n - P_M + 1))
            else:
                eng.wait_ge(pj_full, n_pj + NOUT * (TT - 1) + n - P_OUT + 1)

        def low_ready(eng, n):
            if n in on_pool:
                eng.wait_ge(low_done_p, on_pool.index(n) + 1)
            else:
                eng.wait_ge(low_done_v, on_dve.index(n) + 1)

        def piece_loads(n):
            return sum(16 * (3 if pieces[j][0] == "merge" else 1) for j in range(n % 2, n + 1, 2))

        def split_high(n):
            nc.scalar.wait_ge(raw_loaded[n % 2], piece_loads(n))
            if n >= P_OUT + 2:
                piece_used(nc.scalar, P_OUT - 1)
            elif n >= 2:
                piece_used(nc.scalar, n - 2)
            z = piece_size(n)
            nc.scalar.activation(w_high[split_place(n)][:, 0:z], raw[n % 2][:, 0:z], ACT.Copy).then_inc(high_done, 1)

        def split_low(eng, n):
            eng.wait_ge(high_done, n + 1)
            z = piece_size(n)
            s = split_place(n)
            eng.tensor_tensor(w_low[s][:, 0:z], raw[n % 2][:, 0:z], w_high[s][:, 0:z].bitcast(F32), ALU.subtract
                              ).then_inc(low_done_p if n in on_pool else low_done_v, 1)

        def piece_w(n, /, **dims):
            z = piece_size(n)
            pat = "p (%s) -> p %s" % (" ".join(dims), " ".join(dims))
            return [w[split_place(n)][:, 0:z].rearrange(pat, **dims) for w in (w_high, w_low)]

        def merge_banks(m):
            return [pj[0], sc[0], mb[0]] if m % 2 == 0 else [pj[1], sc[1], mb[1]]

        def merge_tmp(m):
            return part("att", (m % 2) * 1536, 1536, f=3, t=SEQ)

        def bc(v, shape):
            return v.broadcast_to(shape)

        block = ctx.enter_context(nc.Block())

        ctx.enter_context(nc.allow_non_contiguous_dma(reason="small parameters"))

        @block.sync
        def _(sp):
            for t in range(TT):
                sp.dma_start(x_in[:, t, :], x[0, t * P:(t + 1) * P, :]).then_inc(x_loaded[t], 16)

            def load_piece(n):
                kind, c0 = pieces[n]
                if n >= 2:
                    low_ready(sp, n - 2)
                done = raw_loaded[n % 2]
                if kind == "merge":
                    v = raw[n % 2][:, 0:1536].rearrange("p (f k n) -> p f k n", f=3, k=4)
                    for f, w in enumerate((w_glu_gate, w_glu_val, w_attn_up)):
                        sp.dma_start(v[:, f], w[0, :, c0:c0 + P].rearrange("(k p) n -> p k n", p=P)).then_inc(done, 16)
                else:
                    w = w_in if kind == "in" else w_out
                    sp.dma_start(raw[n % 2].rearrange("p (k n) -> p k n", k=DC),
                                 w[0, :, c0:c0 + 256].rearrange("(k p) n -> p k n", p=P)).then_inc(done, 16)

            load_piece(0)
            load_piece(1)
            for f, m in enumerate((b_re, b_im)):
                v = m[0].rearrange("(s g) p h -> g p s h", g=2)
                for gl in range(2):
                    sp.dma_start(b_raw[gl * STATE:(gl + 1) * STATE, f], v[gl]).then_inc(small_loaded, 16)
            for f, m in enumerate((c_re, c_im)):
                sp.dma_start(c_raw[:, f], m[0].rearrange("(c g) h p -> (g h) c p", c=CT_)).then_inc(small_loaded, 16)
            sp.dma_start(d_col[:], d_skip[0].rearrange("(k p) -> p k", p=P)).then_inc(small_loaded, 16)
            for h in range(2):
                sp.dma_start(qg[h * HD:(h + 1) * HD, 0:1], q_norm[0].rearrange("(p o) -> p o", o=1)).then_inc(small_loaded, 16)
                sp.dma_start(qg[h * HD:(h + 1) * HD, 1:2], k_norm[0].rearrange("(p o) -> p o", o=1)).then_inc(small_loaded, 16)
            sp.dma_start(sink[:], sinks[0:1, :].broadcast_to([P, HEADS])).then_inc(small_loaded, 16)
            sp.dma_start(rw[:, :, 0:NG], w_coarse[0].rearrange("(k p) n -> p k n", p=P)).then_inc(small_loaded, 16)
            sp.dma_start(rw[:, :, NG:NG + NE], w_fine[0].rearrange("(k p) n -> p k n", p=P)).then_inc(small_loaded, 16)
            load_piece(2)
            load_piece(3)
            sp.wait_ge(uT_done, CT_)
            for j in range(SUB):
                for q in range(SPC):
                    sp.dma_start(u4[j * TCH:(j + 1) * TCH, q::SPC, :],
                                 uT[q * TCH:(q + 1) * TCH, :, j, :]).then_inc(u4_loaded, 16)
            for n in range(4, NP):
                if n == P_OUT:
                    sp.wait_ge(zy_low, 2)
                    sp.dma_start(ffn_gain, norm_ffn[0:1, :].broadcast_to([P, D])).then_inc(ffn_gain_loaded, 16)
                    sp.dma_start(x2[:, :, :], x[0].rearrange("(t p) d -> p t d", p=P)).then_inc(x_again, 16)
                load_piece(n)
            for e in range(4):
                sp.dma_start(down[e], w_down[0, e].rearrange("(k p) n -> p k n", p=P)).then_inc(down_loaded[e], 16)
            for e in range(4):
                piece_used(sp, P_OUT + e)
                sp.dma_start(ring[e].rearrange("p (k n) -> p k n", k=DC),
                             w_up[0, e].rearrange("(k p) n -> p k n", p=P)).then_inc(ring_loaded[e], 16)
            with sp.Fori(0, NE // 4 - 1) as i:
                for r in range(4):
                    sp.wait_ge(up_full, i * 4 + (r + 1))
                    sp.dma_start(ring[r].rearrange("p (k n) -> p k n", k=DC),
                                 w_up[0, bass.ds(i * 4 + (r + 4), 1)].rearrange("e (k p) n -> p (e k) n", p=P)
                                 ).then_inc(ring_loaded[r], 16)
                    sp.wait_ge(dn_full, i * 4 + (r + 1))
                    sp.dma_start(down[r], w_down[0, bass.ds(i * 4 + (r + 4), 1)].rearrange("e (k p) n -> p (e k) n", p=P)
                                 ).then_inc(down_loaded[r], 16)
            sp.wait_ge(flag_done, 1)
            over = sp.value_load(flag[0:1, 0:1], min_val=0, max_val=1)
            with sp.If(over > 0):
                with sp.Fori(0, MORE) as j:
                    with sp.Fori(0, NE) as e:
                        sp.wait_ge(o_dn, j * NE + e + 1)
                        sp.dma_start(ring[0].rearrange("p (k n) -> p k n", k=DC),
                                     w_up[0, bass.ds(e, 1)].rearrange("e (k p) n -> p (e k) n", p=P)).then_inc(o_w, 16)
                        sp.dma_start(down[0], w_down[0, bass.ds(e, 1)].rearrange("e (k p) n -> p (e k) n", p=P)).then_inc(o_w, 16)
            for t in range(TT):
                sp.wait_ge(sum_done, t + 1)
                sp.dma_start(out[0, t * P:(t + 1) * P, :], x2[:, t, :]).then_inc(out_stored, 16)
            sp.wait_ge(out_stored, 16 * TT)
            for b in range(2):
                sp.wait_ge(y_stored[b], 8 * NE)
            for t in range(TT):
                sp.wait_ge(h2_stored[t], 16)

        @block.gpsimd
        def _(g):
            n_pool = [0]

            def link(ins):
                n_pool[0] += 1
                ins.then_inc(pool_chain, 1)
                g.wait_ge(pool_chain, n_pool[0])

            g.memset(half_col[:], -0.5).then_inc(const_ready, 1)
            g.memset(halfpi[:], math.pi / 2).then_inc(const_ready, 1)
            link(g.memset(ident[:], 0.0))
            g.affine_select(out=ident[:], in_=ident[:], compare_op=ALU.not_equal, fill=1.0, base=0,
                            pattern=[[-1, P]], channel_multiplier=1).then_inc(const_ready, 1)
            g.iota(par_i[:], pattern=[[0, 1]], base=0, channel_multiplier=1).then_inc(const_ready, 1)

            g.wait_ge(const_ready, 1)

            def inverse_root(dst, src, width, ready, n, done):
                g.wait_ge(ready, n)
                g.tensor_tensor(dst, src, half_col[:, 0:width], ALU.pow).then_inc(done, 1)

            for t in range(TT):
                inverse_root(rstd[:, t:t + 1], ssq[:, t:t + 1], 1, var_done, t + 1, rstd_done)
            split_low(g, 0)
            link(g.memset(ones[:], 1.0))
            g.affine_select(out=before[:], in_=ones[:], compare_op=ALU.is_gt, fill=0.0, base=0,
                            pattern=[[1, P]], channel_multiplier=-1).then_inc(const_ready, 1)
            g.iota(slot_no[:], pattern=[[1, CAP]], base=0, channel_multiplier=0,
                   allow_small_or_imprecise_dtypes=True).then_inc(const_ready, 1)
            g.iota(tok_id[:], pattern=[[P, TT]], base=0, channel_multiplier=1,
                   allow_small_or_imprecise_dtypes=True).then_inc(const_ready, 1)
            g.iota(e_no[:], pattern=[[1, NE]], base=0, channel_multiplier=0,
                   allow_small_or_imprecise_dtypes=True).then_inc(const_ready, 1)
            g.iota(e_rev[:], pattern=[[-1, NE]], base=NE, channel_multiplier=0,
                   allow_small_or_imprecise_dtypes=True).then_inc(const_ready, 1)
            link(g.iota(neg_dist[:], pattern=[[1, 2 * P]], base=-P, channel_multiplier=-1,
                        allow_small_or_imprecise_dtypes=True))
            link(g.affine_select(out=neg_dist[:], in_=neg_dist[:], compare_op=ALU.is_ge, fill=-HIDE, base=P,
                                 pattern=[[-1, 2 * P]], channel_multiplier=1))
            g.affine_select(out=neg_dist[:], in_=neg_dist[:], compare_op=ALU.is_ge, fill=-HIDE, base=-1,
                            pattern=[[1, 2 * P]], channel_multiplier=-1).then_inc(const_ready, 1)
            def rotations(c):
                s0 = slice(c * SPC, (c + 1) * SPC)
                if c:
                    g.wait_ge(S_done, c)
                g.memset(Ec[:, :, 0:1], 1.0)
                link(g.memset(Es[:, :, 0:1], 0.0))
                g.tensor_copy(Ec[:, :, 1:2], e1[:, 0, 2, s0].rearrange("p (s o) -> p s o", o=1))
                link(g.tensor_copy(Es[:, :, 1:2], e1[:, 1, 2, s0].rearrange("p (s o) -> p s o", o=1)))
                m = 1
                while m < CH // 2:
                    er, ei = Ec[:, :, m:m + 1], Es[:, :, m:m + 1]
                    tq = et[:, :, :, 0:1]
                    g.tensor_tensor(tq[:, 0], er, er, ALU.mult)
                    g.tensor_tensor(tq[:, 1], ei, ei, ALU.mult)
                    link(g.tensor_tensor(tq[:, 2], er, ei, ALU.mult))
                    g.tensor_tensor(Ec[:, :, 2 * m:2 * m + 1], tq[:, 0], tq[:, 1], ALU.subtract)
                    link(g.tensor_tensor(Es[:, :, 2 * m:2 * m + 1], tq[:, 2], tq[:, 2], ALU.add))
                    m *= 2
                    w = m - 1
                    er, ei = (bc(v[:, :, m:m + 1], [P, SPC, w]) for v in (Ec, Es))
                    ar, ai = Ec[:, :, 1:m], Es[:, :, 1:m]
                    tq = et[:, :, :, 0:w]
                    g.tensor_tensor(tq[:, 0], ar, er, ALU.mult)
                    g.tensor_tensor(tq[:, 1], ai, ei, ALU.mult)
                    g.tensor_tensor(tq[:, 2], ar, ei, ALU.mult)
                    link(g.tensor_tensor(tq[:, 3], ai, er, ALU.mult))
                    g.tensor_tensor(Ec[:, :, m + 1:2 * m], tq[:, 0], tq[:, 1], ALU.subtract)
                    link(g.tensor_tensor(Es[:, :, m + 1:2 * m], tq[:, 2], tq[:, 3], ALU.add))
                g.sem_inc(e_done, 1)

            g.wait_ge(rot_done, 1)
            rotations(0)
            for j in range(3 * TT):
                inverse_root(qrs[:, j, :], qss[:, j, :], 4, qk_var, j + 1, qk_rstd)
            split_low(g, P_G)
            split_low(g, P_G + 1)
            for c in range(1, CT_):
                split_low(g, P_G + 2 * c)
                rotations(c)
                split_low(g, P_G + 2 * c + 1)

            for t in range(TT):
                inverse_root(rstd[:, TT + t:TT + t + 1], ssq[:, TT + t:TT + t + 1], 1, var_done, TT + t + 1, rstd_done)

            for t in range(TT):
                g.wait_ge(h2_stored[t], 16)

            def gather(e2, e, n_free):
                if n_free is not None:
                    g.wait_ge(xt_full, n_free)
                g.tensor_copy(idx[:, e2:e2 + 1], idx_all[:, bass.ds(e, 1)]).then_inc(idx_taken, 1)
                g.wait_ge(idx_taken, e + 1)
                g.sem_inc(gather_turn, 1)
                g.indirect_dma_start(xg[e2], None, h2_rows,
                                     bass.IndirectOffsetOnAxis(idx[:, e2:e2 + 1], 0)).then_inc(gathered[e2], 16)

            g.wait_ge(idx_done, 1)
            gather(0, 0, None)
            gather(1, 1, None)
            g.wait_ge(idx_done, 2)
            with g.Fori(0, NE // 2 - 1) as i:
                for r in range(2):
                    gather(r, i * 2 + (r + 2), i * 4 + 2 * (r + 1))
            def rows_of_tokens(rows):
                for t in range(TT):
                    for k in range(2):
                        g.indirect_dma_start(gath[2 * t + k], None, rows,
                                             bass.IndirectOffsetOnAxis(dest[:, k, t:t + 1], 0)).then_inc(rows_back[t], 16)

            g.wait_ge(flag_done, 1)
            over = g.value_load(flag[0:1, 0:1], min_val=0, max_val=1)
            with g.If(over > 0):
                with g.Fori(0, MORE * NE) as b:
                    g.wait_ge(o_idx, b + 1)
                    g.sem_inc(gather_turn, 1)
                    g.indirect_dma_start(xg[0], None, h2_rows,
                                         bass.IndirectOffsetOnAxis(idx[:, 0:1], 0)).then_inc(o_gath, 16)
                g.wait_ge(o_st, 16 * MORE * NE)
                for b in range(2):
                    g.wait_ge(y_stored[b], 8 * NE)
                g.dma_start(y_all[0:NE * CAP, :], y_rows).then_inc(o_copy, 16)
                g.wait_ge(o_copy, 16)
                rows_of_tokens(y_all)
            with g.If(over < 1):
                for b in range(2):
                    g.wait_ge(y_stored[b], 8 * NE)
                g.wait_ge(dn_full, NE)
                rows_of_tokens(y_rows)

        @block.scalar
        def _(act):
            act.dma_start(R(0), lam_re[0].rearrange("(s g) p -> s (g p)", g=2)).then_inc(rows_loaded, 16)
            act.dma_start(R(1), lam_im[0].rearrange("(s g) p -> s (g p)", g=2)).then_inc(rows_loaded, 16)
            act.dma_start(ldt[:, 0, :], log_dt[0].rearrange("(s g) -> s g", g=2)).then_inc(rows_loaded, 16)
            act.dma_start(mix_gain, norm_mix[0:1, :].broadcast_to([P, D])).then_inc(mix_gain_loaded, 16)
            act.wait_ge(rows_loaded, 16 * 3)
            act.activation(ldt[:, 1, :], ldt[:, 0, :], ACT.Exp).then_inc(prm_act, 1)
            act.wait_ge(prm_dve, 1)
            act.activation(R(5), R(2), ACT.Exp).then_inc(prm_act, 1)
            act.activation(R(6), R(2), ACT.Exp, scale=float(SUB)).then_inc(prm_act, 1)
            for t in range(TT):
                act.wait_ge(x_loaded[t], 16)
                act.activation(xn[:, t, :], x_in[:, t, :], ACT.Square, accum_out=ssq[:, t:t + 1]).then_inc(sq_done, 1)
            act.wait_ge(prm_dve, 2)
            act.wait_ge(const_ready, 2)
            act.activation(R(7), R(4), ACT.Sin).then_inc(prm_act, 1)
            act.activation(R(8), R(9), ACT.Sin, scale=-1.0, bias=halfpi[0:ST, :]).then_inc(prm_act, 1)
            for n in range(2 * TT):
                t, f = n // 2, n % 2
                m, b, _ = uses(tp_order, ("h", t, f))
                act.wait_ge(tp_full, m + 1)
                act.activation(h_high[:, 4 * f:4 * f + 4, t * P:(t + 1) * P], tp[b][:].rearrange("p (k n) -> p k n", k=4),
                               ACT.Copy).then_inc(h_high_done, 1)
                if n in (TT - 1, 2 * TT - 1):
                    split_high(n // TT)
            for c in range(CT_):
                n, b, _ = uses(pj_order, ("u", c))
                act.wait_ge(pj_full, n + 1)
                act.activation(uT[:, c].rearrange("p j n -> p n j"), pj[b][:].rearrange("p (n j) -> p n j", j=SUB),
                               ACT.Copy).then_inc(pj_free[b], 1)
                act.wait_ge(pj_free[b], uses(pj_order, ("u", c))[2] + 1)
                act.sem_inc(uT_done, 1)
                if c == 2:
                    split_high(2)
            for j in range(3 * TT):
                n, b, _ = uses(pj_order, ("qkv", j))
                W = KW if j < TT else 2 * KW
                act.wait_ge(pj_full, n + 1)
                if j >= 2:
                    act.wait_ge(qk_norm, j - 1)
                act.activation(qk_sq[j % 2][:, 0:W // HD, :], pj[b][:, 0:W], ACT.Square).then_inc(qk_evac, 1)
                if j < TT:
                    act.activation(v_tok[:, j, :], pj[b][:, KW:2 * KW], ACT.Copy).then_inc(v_done, 1)
                act.activation(qk_raw[j % 2][:, 0:W // HD, :], pj[b][:, 0:W], ACT.Copy).then_inc(pj_free[b], 1)
                if j % TT == 0:
                    split_high(P_QKV + 1 + j // TT)
            for i in range(2 * DC + 1):
                if i < 2 * DC:
                    n, b, used = uses(pj_order, ("gate", i))
                    act.wait_ge(pj_full, n + 1)
                    dst = ts_gate[:, i, :] if i < DC else ta_gate[:, i - DC, :]
                    act.activation(dst, pj[b][:], ACT.Tanh, scale=0.5).then_inc(pj_free[b], 1)
                    if i % 2 == 0:
                        split_high(P_G + 1 + i // 2)
                    act.wait_ge(pj_free[b], used + 1)
                    act.sem_inc(gates_done, 1)
                if i % 4 == 0 and i < 2 * DC:
                    c = i // 4
                    if c:
                        act.wait_ge(bu_full, c)
                    for f in range(2):
                        n, b, _ = uses(tp_order, ("w", c, f))
                        act.wait_ge(tp_full, n + 1)
                        act.activation(w1T[:, f], tp[b][:], ACT.Copy).then_inc(tp_free[b], 1)
                        act.wait_ge(tp_free[b], uses(tp_order, ("w", c, f))[2] + 1)
                        act.sem_inc(w1T_done, 1)
                if i % 4 == 1:
                    c = i // 4
                    n, b, _ = uses(tp_order, ("k", c))
                    act.wait_ge(tp_full, n + 1)
                    if c:
                        act.wait_ge(y_full, c)
                    act.wait_ge(bbd_done, 1)
                    kps = tp[b][0:TCH, :].rearrange("p (q n) -> p q n", q=SPC)
                    for j in range(SUB):
                        ins = act.activation(toep[j * TCH:(j + 1) * TCH, :, j * TCH:], kps[:, :, 0:(SUB - j) * TCH], ACT.Copy)
                        ins.then_inc(toep_done if j < SUB - 1 else tp_free[b], 1)
                    act.wait_ge(tp_free[b], uses(tp_order, ("k", c))[2] + 1)
                    act.sem_inc(toep_done, 1)
                if i % 2 == 0 and i >= 2:
                    a = i // 2 - 1
                    n, b, _ = uses(pj_order, ("av", a))
                    act.wait_ge(pj_full, n + 1)
                    blk, kv = a // KVH, a % KVH
                    act.activation(qT[:, 2 * kv:2 * kv + 2, blk * P:(blk + 1) * P],
                                   pj[b][:, 0:2 * P].rearrange("p (h q) -> p h q", h=2), ACT.Copy).then_inc(pj_free[b], 1)
                    act.wait_ge(pj_free[b], uses(pj_order, ("av", a))[2] + 1)
                    act.sem_inc(av_done, 1)
                if i % 2 == 0 and i < 2 * DC:
                    a = i // 2
                    W = 2 * P if a >= KVH else P
                    act.wait_ge(m_ready, 2 * (a + 1))
                    for h in range(QPK):
                        act.activation(probs[a % 2][:, h, 0:W], probs[a % 2][:, h, 0:W], ACT.Exp,
                                       bias=smx[:, a % 2, 1, h:h + 1],
                                       accum_out=smx[:, a % 2, 4, h:h + 1]).then_inc(exp_done, 1)
                    act.activation(smx[:, a % 2, 3, :], smx[:, a % 2, 2, :], ACT.Exp).then_inc(exp_done, 1)
                if i % 2 == 1:
                    a = i // 2
                    if a:
                        act.wait_ge(pj_full, uses(pj_order, ("av", a - 1))[0] + 1)
                    for f in range(2 if a >= KVH else 1):
                        n, b, _ = uses(tp_order, ("pt", a, f))
                        act.wait_ge(tp_full, n + 1)
                        act.activation(pT[:, f], tp[b][:], ACT.Copy).then_inc(tp_free[b], 1)
                        act.wait_ge(tp_free[b], uses(tp_order, ("pt", a, f))[2] + 1)
                        act.sem_inc(pT_done, 1)
                if i % 4 == 3:
                    c = i // 4
                    act.wait_ge(y_full, c + 1)
                    act.activation(tb[0], mb[0][:], ACT.Copy).then_inc(y_evac, 1)
                if i % 4 == 0 and i >= 4:
                    c = i // 4 - 1
                    act.wait_ge(yv_done, c + 1)
                    act.activation(tb[2], tb[1], ACT.Square).then_inc(z_sq, 1)
                    act.wait_ge(z_arg, c + 1)
                    act.activation(tb[2], tb[2], ACT.Tanh, scale=GELU_IN).then_inc(z_th, 1)
            act.wait_ge(av_done, NQ)
            piece_used(act, P_M - 1)
            act.activation(h_high[:, 4:8, :], qT, ACT.Copy).then_inc(zy_high, 1)
            act.wait_ge(z_done, CT_)
            act.activation(h_high[:, 0:4, :], zT, ACT.Copy).then_inc(zy_high, 1)

            def merged_high(m):
                act.wait_ge(merged_done, m + 1)
                act.activation(m_high[:, m, :], merge_tmp(m)[:, 1, :], ACT.Copy).then_inc(m_high_done, 1)

            for m in range(DC):
                split_high(P_M + m + 1)
                act.wait_ge(mg_full, 3 * m + 1)
                if m >= 2:
                    act.wait_ge(mg_free, m - 1)
                act.activation(merge_tmp(m)[:, 0, :], merge_banks(m)[0][:], ACT.Tanh, scale=0.25).then_inc(mg_act, 1)
                if m:
                    merged_high(m - 1)
            merged_high(DC - 1)
            for n in range(P_OUT + 1, NP):
                split_high(n)
            for t in range(TT):
                act.wait_ge(x2_done, NOUT * (t + 1))
                act.activation(part("att", t % 2 * D, D), x2[:, t, :], ACT.Square, accum_out=ssq[:, TT + t:TT + t + 1]).then_inc(sq_done, 1)
                if t:
                    act.wait_ge(n2_done, t)
                    act.dma_start(h2_rows[(t - 1) * P:t * P, :], xg[(t - 1) % 2]).then_inc(h2_stored[t - 1], 16)
            act.wait_ge(n2_done, TT)
            act.dma_start(h2_rows[(TT - 1) * P:, :], xg[(TT - 1) % 2]).then_inc(h2_stored[TT - 1], 16)
            act.wait_ge(r_dve, 1)
            act.activation(rt[:, 0, :, 0:NG], rt[:, 0, :, 0:NG], ACT.Exp).then_inc(r_act, 1)
            act.wait_ge(r_dve, 2)
            act.activation(rs_[:, 6, :], rs_[:, 6, :], ACT.Exp).then_inc(r_act, 1)

            def up_part(e4, n):
                act.wait_ge(up_full, n)
                b = e4 % 2
                act.activation(th_e[b], pj[b][:, 0:DE], ACT.Tanh, scale=0.5).then_inc(th_done, 1)

            def down_part(e4, e, n_at, n_dn, n_store):
                b = e4 % 2
                act.wait_ge(at_full, n_at)
                act.activation(actT[b], sc[1][:, 0:2 * P], ACT.Copy).then_inc(at_done, 1)
                if n_store is not None:
                    act.wait_ge(y_stored[b], n_store)
                act.wait_ge(dn_full, n_dn)
                for h in range(2):
                    act.activation(y_out[b][:, h * 512:(h + 1) * 512], mb[h][:], ACT.Copy,
                                   scale=gate_all[:, bass.ds(e, 1)]).then_inc(y_scaled, 1)
                act.wait_ge(y_scaled, n_dn * 2)
                act.dma_start(y_rows[bass.ds(e * CAP, CAP), :], y_out[b]).then_inc(y_stored[b], 16)

            up_part(0, 1)
            for e in range(1, 3):
                up_part(e, e + 1)
                down_part(e - 1, e - 1, e, e, None)
            up_part(3, 4)
            down_part(2, 2, 3, 3, 16)
            with act.Fori(0, NE // 4 - 1) as i:
                for r in range(4):
                    up_part(r, i * 4 + (r + 5))
                    down_part((r + 3) % 4, i * 4 + (r + 3), i * 4 + (r + 4), i * 4 + (r + 4), (i * 2 + (r + 3) // 2) * 16)
            down_part(3, NE - 1, NE, NE, 16 * ((NE - 1) // 2))
            act.wait_ge(flag_done, 1)
            over = act.value_load(flag[0:1, 0:1], min_val=0, max_val=1)
            with act.If(over > 0):
                for b in range(2):
                    act.wait_ge(y_stored[b], 8 * NE)
                with act.Fori(0, MORE) as j:
                    with act.Fori(0, NE) as e:
                        act.wait_ge(o_up, j * NE + e + 1)
                        act.activation(th_e[0], pj[0][:, 0:DE], ACT.Tanh, scale=0.5).then_inc(o_th, 1)
                        act.wait_ge(o_at, j * NE + e + 1)
                        act.activation(actT[0], sc[1][:, 0:2 * P], ACT.Copy).then_inc(o_atd, 1)
                        act.wait_ge(o_dn, j * NE + e + 2)
                        for h in range(2):
                            act.activation(y_out[0][:, h * 512:(h + 1) * 512], mb[h][:], ACT.Copy,
                                           scale=gate[:, 0:1]).then_inc(o_y, 1)
                        act.wait_ge(o_y, (j * NE + e + 1) * 2)
                        act.dma_start(y_all[bass.ds((j + 1) * (NE * CAP) + e * CAP, CAP), :], y_out[0]).then_inc(o_st, 16)
                        act.wait_ge(o_st, (j * NE + e + 1) * 16)

        @block.vector
        def _(v):
            n_dve = [0]

            def mark(ins):
                n_dve[0] += 1
                ins.then_inc(dve_chain, 1)

            def settle():
                v.wait_ge(dve_chain, n_dve[0])

            def link(ins):
                mark(ins)
                settle()

            tt, ts, stt = v.tensor_tensor, v.tensor_scalar, v.scalar_tensor_tensor

            def scale_tile(t):
                v.wait_ge(rstd_done, t + 1)
                stt(xn[:, t, :], x_in[:, t, :], rstd[:, t:t + 1], mix_gain, ALU.mult, ALU.mult).then_inc(xn_done, 1)

            def norm2(t):
                v.wait_ge(sq_done, TT + t + 1)
                mean_var(ssq[:, TT + t:TT + t + 1], D)
                v.wait_ge(rstd_done, TT + t + 1)
                if t == 0:
                    v.wait_ge(ffn_gain_loaded, 16)
                    for n in range(NP - 2, NP):
                        low_ready(v, n)
                if t >= 2:
                    v.wait_ge(h2_stored[t - 2], 16)
                    v.wait_ge(tp_full, n_tp + 2 * (t - 1))
                stt(xg[t % 2], x2[:, t, :], rstd[:, TT + t:TT + t + 1], ffn_gain, ALU.mult, ALU.mult).then_inc(n2_done, 1)

            def norm2_turned(t):
                if t >= 2:
                    v.wait_ge(lg_full, t - 1)
                for f in range(2):
                    v.wait_ge(tp_full, n_tp + 2 * t + f + 1)
                    v.tensor_copy(xgT[t % 2][:, 4 * f:4 * f + 4, :], tp[f][:].rearrange("p (k n) -> p k n", k=4)
                                  ).then_inc(h2T_done, 1)

            def mean_var(dst, n):
                ts(dst, dst, 1.0 / n, EPS, ALU.mult, ALU.add).then_inc(var_done, 1)

            v.wait_ge(rows_loaded, 16 * 3)
            v.wait_ge(prm_act, 1)
            dt_bc = bc(ldt[:, 1, :].rearrange("s (g o) -> s g o", o=1), [ST, 2, STATE])
            g2 = lambda i: R(i).rearrange("s (g p) -> s g p", g=2)
            tt(g2(2), g2(0), dt_bc, ALU.mult).then_inc(prm_dve, 1)
            link(tt(g2(3), g2(1), dt_bc, ALU.mult))
            link(ts(R(10), R(3), 1.0 / (2 * math.pi), MAGIC, ALU.mult, ALU.add))
            link(ts(R(10), R(10), MAGIC, None, ALU.subtract))
            link(stt(R(4), R(10), -TWO_PI_HIGH, R(3), ALU.mult, ALU.add))
            link(stt(R(4), R(10), -TWO_PI_LOW, R(4), ALU.mult, ALU.add))
            link(ts(R(4), R(4), 3.1415925, -3.1415925, ALU.min, ALU.max))
            link(ts(R(9), R(4), -1.0, None, ALU.mult))
            tt(R(9), R(9), R(4), ALU.max).then_inc(prm_dve, 1)
            def turned_low(n):
                t, f = n // 2, n % 2
                _, b, _ = uses(tp_order, ("h", t, f))
                v.wait_ge(h_high_done, n + 1)
                hs = (slice(None), slice(4 * f, 4 * f + 4), slice(t * P, (t + 1) * P))
                tt(h_low[hs], tp[b][:].rearrange("p (k n) -> p k n", k=4), h_high[hs].bitcast(F32), ALU.subtract
                   ).then_inc(tp_free[b], 1)

            v.wait_ge(mix_gain_loaded, 16)
            for t in range(TT + 2):
                if t < TT:
                    v.wait_ge(sq_done, t + 1)
                    mean_var(ssq[:, t:t + 1], D)
                if t >= 2:
                    turned_low(2 * t - 4)
                    turned_low(2 * t - 3)
                if 1 <= t <= TT:
                    scale_tile(t - 1)
            mark(tt(R(11), R(0), R(0), ALU.mult))
            link(tt(R(12), R(1), R(1), ALU.mult))
            link(tt(R(11), R(11), R(12), ALU.add))
            link(v.reciprocal(R(12), R(11)))
            v.wait_ge(prm_act, 5)
            mark(tt(R(13), R(5), R(8), ALU.mult))
            mark(tt(R(14), R(5), R(7), ALU.mult))
            settle()
            link(ts(R(17), R(13), 1.0, None, ALU.subtract))
            mark(tt(R(18), R(17), R(0), ALU.mult))
            mark(tt(R(19), R(14), R(1), ALU.mult))
            mark(tt(R(20), R(14), R(0), ALU.mult))
            mark(tt(R(21), R(17), R(1), ALU.mult))
            settle()
            mark(tt(R(18), R(18), R(19), ALU.add))
            mark(tt(R(20), R(20), R(21), ALU.subtract))
            settle()
            mark(tt(R(15), R(18), R(12), ALU.mult))
            link(tt(R(16), R(20), R(12), ALU.mult))
            v.sem_inc(rows_done, 1)
            split_low(v, 1)
            v.wait_ge(const_ready, 4)
            v.wait_ge(small_loaded, 16 * 14)
            link(ts(par_i[:], par_i[:], GCH, None, ALU.bitwise_and))
            link(ts(par[:, 0:1], par_i[:], 0.0, None, ALU.is_gt))
            link(ts(par[:, 1:2], par[:, 0:1], -1.0, 1.0, ALU.mult, ALU.add))
            for f in range(2):
                for gl in range(2):
                    mark(ts(c_exp[:, f, :, gl, :], c_raw[:, f], par[:, 1 - gl:2 - gl], (1.0, -1.0)[f], ALU.mult, ALU.mult))
            settle()
            v.sem_inc(cexp_done, 1)
            n, b, used = uses(tp_order, ("prm",))
            v.wait_ge(tp_full, n + 1)
            v.tensor_copy(prm[:], tp[b][:, 0:7 * ST].rearrange("p (f s) -> p f s", f=7)).then_inc(tp_free[b], 1)
            v.wait_ge(tp_free[b], used + 1)
            pr, pi = (lambda j: pw[:, 0, j, :]), (lambda j: pw[:, 1, j, :])
            mark(v.memset(pr(0), 1.0))
            mark(v.memset(pi(0), 0.0))
            mark(v.tensor_copy(pw[:, :, 1, :], prm[:, 0:2, :]))
            mark(v.tensor_copy(e1[:, :, 0, :], prm[:, 5:7, :]))
            settle()

            def cmul(dst, a, b_, tmp):
                mark(tt(tmp(0), a[0], b_[0], ALU.mult))
                mark(tt(tmp(1), a[1], b_[1], ALU.mult))
                mark(tt(tmp(2), a[0], b_[1], ALU.mult))
                mark(tt(tmp(3), a[1], b_[0], ALU.mult))
                settle()
                mark(tt(dst[0], tmp(0), tmp(1), ALU.subtract))
                mark(tt(dst[1], tmp(2), tmp(3), ALU.add))
                settle()

            pwj = lambda j: (pr(j), pi(j))
            ej = lambda j: (e1[:, 0, j, :], e1[:, 1, j, :])
            stmp = lambda i: sc_t[:, i, :]
            cmul(ej(1), ej(0), ej(0), stmp)
            cmul(ej(2), ej(1), ej(1), stmp)
            v.sem_inc(rot_done, 1)
            cmul(pwj(2), pwj(1), pwj(1), stmp)
            cmul(pwj(3), pwj(2), pwj(1), stmp)
            cmul(pwj(4), pwj(2), pwj(2), stmp)
            mark(v.memset(Bre, 0.0))
            mark(v.memset(Bim, 0.0))
            mark(v.memset(toep, 0.0))
            coef = [bc(prm[:, 2 + i, :].rearrange("p (s o) -> p s o", o=1), [P, ST, GCH]) for i in range(2)]
            bt = [tb[i][:, :, :].rearrange("p q n -> p (q n)")[:, 0:ST * GCH].rearrange("p (s h) -> p s h", s=ST) for i in range(4)]
            mark(tt(bt[0], b_raw[:, 0], coef[0], ALU.mult))
            mark(tt(bt[1], b_raw[:, 1], coef[1], ALU.mult))
            mark(tt(bt[2], b_raw[:, 0], coef[1], ALU.mult))
            mark(tt(bt[3], b_raw[:, 1], coef[0], ALU.mult))
            settle()
            mark(v.memset(Sre[:, :, 0:1], 0.0))
            mark(v.memset(Sim[:, :, 0:1], 0.0))
            v.sem_inc(bbd_done, 1)
            for gl in range(2):
                ps = slice(gl * STATE, (gl + 1) * STATE)
                cs = slice(gl * GCH, (gl + 1) * GCH)
                mark(tt(Bre[ps, :, cs], bt[0][ps], bt[1][ps], ALU.subtract))
                mark(tt(Bim[ps, :, cs], bt[2][ps], bt[3][ps], ALU.add))
            settle()
            split_low(v, 2)
            for f, dst in enumerate((Cre, Cim)):
                n, b, used = uses(tp_order, ("ct", f))
                v.wait_ge(tp_full, n + 1)
                v.tensor_copy(dst, tp[b][:].rearrange("p (s c) -> p s c", c=TCH)).then_inc(tp_free[b], 1)
                v.wait_ge(tp_free[b], used + 1)
            mark(ts(qg[:, 2:3], qg[:, 0:1], qg[:, 1:2], HD ** -0.5, ALU.mult, ALU.mult))
            settle()

            def qk_variance(j):
                H = 2 if j < TT else 4
                v.wait_ge(qk_evac, j + 1)
                link(v.tensor_reduce(qss[:, j, 0:H], qk_sq[j % 2][:, 0:H, :], AX_X, ALU.add))
                if j < TT:
                    link(v.memset(qss[:, j, H:4], 1.0))
                ts(qss[:, j, :], qss[:, j, :], 1.0 / HD, EPS, ALU.mult, ALU.add).then_inc(qk_var, 1)

            def qk_normalise(j):
                _, b, used = uses(pj_order, ("qkv", j))
                v.wait_ge(pj_free[b], used + 1)
                v.wait_ge(qk_rstd, j + 1)
                rb = qrs[:, j, :].rearrange("p (h o) -> p h o", o=1)
                if j < TT:
                    k2 = qk_nrm[j % 4].rearrange("p (g r) d -> p g r d", r=2)
                    for r in range(2):
                        mark(tt(k2[:, :, r, :], qk_raw[j % 2][:, 0:2, :], bc(rb[:, 0:2], [P, 2, HD]), ALU.mult))
                else:
                    mark(tt(qk_nrm[j % 4], qk_raw[j % 2], bc(rb, [P, 4, HD]), ALU.mult))
                settle()
                v.sem_inc(qk_norm, 1)

            def qk_turned(j):
                n, b, used = uses(tp_order, ("qkt", j))
                v.wait_ge(tp_full, n + 1)
                t = j % TT
                src = tp[b][:, 0:2 * P].rearrange("p (h n) -> p h n", h=2)
                if j < TT:
                    v.tensor_copy(kT[:, :, t * P:(t + 1) * P], src).then_inc(tp_free[b], 1)
                else:
                    h0 = 2 * (j // TT - 1)
                    ts(qT[:, h0:h0 + 2, t * P:(t + 1) * P], src, qg[:, 2:3], None, ALU.mult).then_inc(tp_free[b], 1)
                v.wait_ge(tp_free[b], used + 1)
                v.sem_inc(qT_done, 1)

            def input_weights(c):
                s0 = slice(c * SPC, (c + 1) * SPC)
                if c:
                    v.wait_ge(tp_full, uses(tp_order, ("w", c - 1, 1))[0] + 1)
                br, bi = Bre[:, s0], Bim[:, s0]
                mark(v.tensor_copy(w1[:, 0, :, SUB - 1, :], br))
                mark(v.tensor_copy(w1[:, 1, :, SUB - 1, :], bi))
                for i in range(SUB - 1):
                    a, b_ = (bc(pw[:, f, SUB - 1 - i, s0].rearrange("p (s o) -> p s o", o=1), [P, SPC, TCH]) for f in range(2))
                    cmul((w1[:, 0, :, i, :], w1[:, 1, :, i, :]), (br, bi), (a, b_), lambda k: lt(k))
                settle()
                v.sem_inc(w1_done, 1)

            lt = lambda k: small_t[:, k]

            def output_weights(c):
                s0 = slice(c * SPC, (c + 1) * SPC)
                if c:
                    v.wait_ge(y_full, c)
                cr, cn = Cre[:, s0], Cim[:, s0]
                mark(v.tensor_copy(CLre[:, :, 0, :], cr))
                mark(v.tensor_copy(CLim[:, :, 0, :], cn))
                for j in range(1, SUB + 1):
                    a, b_ = (bc(pw[:, f, j, s0].rearrange("p (s o) -> p s o", o=1), [P, SPC, TCH]) for f in range(2))
                    mark(tt(lt(0), cr, a, ALU.mult))
                    mark(tt(lt(1), cn, b_, ALU.mult))
                    mark(tt(lt(2), cn, a, ALU.mult))
                    mark(tt(lt(3), cr, b_, ALU.mult))
                    settle()
                    mark(tt(CLre[:, :, j, :], lt(0), lt(1), ALU.add))
                    mark(tt(CLim[:, :, j, :], lt(2), lt(3), ALU.subtract))
                    settle()
                v.sem_inc(cl_done, 1)

            def softmax(a):
                blk, kv = a // KVH, a % KVH
                W = 2 * P if blk else P
                p_ = probs[a % 2]
                k0 = 2 * P - W
                if a >= 2:
                    v.wait_ge(tp_full, uses(tp_order, ("pt", a - 2, 1 if (a - 2) >= KVH else 0))[0] + 1)
                v.wait_ge(const_ready, 10)
                v.wait_ge(sc_full, a + 1)
                for h in range(QPK):
                    slope = 2.0 ** (-8.0 * (kv * QPK + h + 1) / HEADS)
                    mark(stt(p_[:, h, 0:W], neg_dist[:, k0:], slope,
                             sc[h % 2][:, (h // 2) * 2 * P:(h // 2) * 2 * P + W], ALU.mult, ALU.add))
                settle()
                v.sem_inc(sc_read, 1)
                st = lambda i: smx[:, a % 2, i, :]
                link(v.tensor_reduce(st(0), p_[:, :, 0:W], AX_X, ALU.max))
                snk = sink[:, kv * QPK:(kv + 1) * QPK]
                link(tt(st(0), st(0), snk, ALU.max))
                ts(st(1), st(0), -1.0, None, ALU.mult).then_inc(m_ready, 1)
                tt(st(2), snk, st(0), ALU.subtract).then_inc(m_ready, 1)
                v.wait_ge(exp_done, (QPK + 1) * (a + 1))
                link(tt(st(4), st(4), st(3), ALU.add))
                link(v.reciprocal(st(5), st(4)))
                for h in range(QPK):
                    mark(ts(p_[:, h, 0:W], p_[:, h, 0:W], smx[:, a % 2, 5, h:h + 1], None, ALU.mult))
                settle()
                v.sem_inc(p_done, 1)

            def scan_tile(c):
                v.wait_ge(bu_full, c + 1)
                v.wait_ge(e_done, c + 1)
                if c:
                    v.wait_ge(z_done, c)
                X, Y = (mb[i][:].rearrange("p (q n) -> p q n", q=SPC) for i in range(2))
                mark(tt(tb[0], X, Ec, ALU.mult))
                mark(tt(tb[1], Y, Es, ALU.mult))
                mark(tt(tb[2], Y, Ec, ALU.mult))
                mark(tt(tb[3], X, Es, ALU.mult))
                settle()
                v.sem_inc(bu_read, 1)
                mark(tt(tb[0], tb[0], tb[1], ALU.add))
                mark(tt(tb[2], tb[2], tb[3], ALU.subtract))
                settle()
                for q in range(SPC):
                    dec = bc(prm[:, 4, c * SPC + q:c * SPC + q + 1], [P, CH])
                    mark(v.tensor_tensor_scan(tb[1][:, q, :], dec, tb[0][:, q, :], 0.0, ALU.mult, ALU.add))
                    mark(v.tensor_tensor_scan(tb[3][:, q, :], dec, tb[2][:, q, :], 0.0, ALU.mult, ALU.add))
                settle()
                L = slice(0, CH - 1)
                wr, wi = tb[1][:, :, L], tb[3][:, :, L]
                if c:
                    v.wait_ge(y_full, c)
                mark(tt(tb[0][:, :, L], wr, Ec[:, :, L], ALU.mult))
                mark(tt(tb[2][:, :, L], wi, Es[:, :, L], ALU.mult))
                settle()
                mark(tt(Sre[:, :, 1:CH], tb[0][:, :, L], tb[2][:, :, L], ALU.subtract))
                settle()
                mark(tt(tb[0][:, :, L], wr, Es[:, :, L], ALU.mult))
                mark(tt(tb[2][:, :, L], wi, Ec[:, :, L], ALU.mult))
                settle()
                mark(tt(Sim[:, :, 1:CH], tb[0][:, :, L], tb[2][:, :, L], ALU.add))
                settle()
                v.sem_inc(S_done, 1)

            def gelu(c):
                v.wait_ge(z_full, c + 1)
                uc = uT[:, c].rearrange("p j n -> p (j n)")
                f1, f2 = (tb[i].rearrange("p q n -> p (q n)") for i in (1, 2))
                stt(f1, uc, d_col[:, c:c + 1], mb[1][:], ALU.mult, ALU.add).then_inc(yv_done, 1)
                v.wait_ge(z_sq, c + 1)
                link(ts(f2, f2, GELU_CUBE, 1.0, ALU.mult, ALU.add))
                v.wait_ge(yv_done, c + 1)
                tt(f2, f2, f1, ALU.mult).then_inc(z_arg, 1)
                v.wait_ge(z_th, c + 1)
                v.wait_ge(u4_loaded, 16 * SUB * SPC)
                stt(zT[:, c, :].rearrange("p (n j) -> p j n", j=SUB), f2.rearrange("p (j n) -> p j n", j=SUB), 1.0,
                    f1.rearrange("p (j n) -> p j n", j=SUB), ALU.add, ALU.mult).then_inc(z_done, 1)

            for j in range(3 * TT):
                qk_variance(j)
                if j >= 1:
                    qk_normalise(j - 1)
                if j >= 3:
                    qk_turned(j - 3)
                if j % TT == 0 and j // TT < 2:
                    split_low(v, P_QKV + 1 + j // TT)
                if j == 2:
                    input_weights(0)
                if j == TT + 2:
                    output_weights(0)
            qk_turned(3 * TT - 3)
            qk_normalise(3 * TT - 1)
            for j in range(3 * TT - 2, 3 * TT):
                qk_turned(j)
            for i in range(2 * DC + 1):
                if i % 2 == 0 and i < 2 * DC:
                    softmax(i // 2)
                if i % 4 == 0 and i >= 4:
                    gelu(i // 4 - 1)
                if i % 4 == 1:
                    scan_tile(i // 4)
                if i % 4 == 2 and i // 4 + 1 < CT_:
                    input_weights(i // 4 + 1)
                if i % 4 == 3 and i // 4 + 1 < CT_:
                    output_weights(i // 4 + 1)
            v.wait_ge(av_done, NQ)
            v.wait_ge(zy_high, 1)
            tt(h_low[:, 4:8, :], qT, h_high[:, 4:8, :].bitcast(F32), ALU.subtract).then_inc(zy_low, 1)
            v.wait_ge(zy_high, 2)
            v.wait_ge(z_done, CT_)
            tt(h_low[:, 0:4, :], zT, h_high[:, 0:4, :].bitcast(F32), ALU.subtract).then_inc(zy_low, 1)
            split_low(v, P_M)

            def merged_low(m):
                v.wait_ge(m_high_done, m + 1)
                mark(tt(m_low[:, m, :], merge_tmp(m)[:, 1, :], m_high[:, m, :].bitcast(F32), ALU.subtract))
                settle()
                v.sem_inc(m_low_done, 1)

            v.wait_ge(gates_done, 2 * DC)
            for m in range(DC):
                G, V, A = merge_banks(m)
                t3 = merge_tmp(m)
                split_low(v, P_M + m + 1)
                v.wait_ge(mg_act, m + 1)
                v.wait_ge(mg_full, 3 * (m + 1))
                mark(stt(t3[:, 1, :], t3[:, 0, :], 1.0, V[:], ALU.add, ALU.mult))
                mark(stt(t3[:, 2, :], ta_gate[:, m, :], 1.0, A[:], ALU.add, ALU.mult))
                settle()
                v.sem_inc(mg_free, 1)
                link(stt(t3[:, 1, :], ts_gate[:, m, :], 1.0, t3[:, 1, :], ALU.add, ALU.mult))
                stt(t3[:, 1, :], t3[:, 1, :], 0.25, t3[:, 2, :], ALU.mult, ALU.add).then_inc(merged_done, 1)
                if m:
                    merged_low(m - 1)
            merged_low(DC - 1)
            v.wait_ge(x_again, 16)
            for t in range(TT):
                for p_ in range(NOUT):
                    n = NOUT * t + p_
                    v.wait_ge(pj_full, n_pj + n + 1)
                    xs = x2[:, t, p_ * 256:(p_ + 1) * 256]
                    stt(xs, pj[n % 2][:, 0:256], 0.5, xs, ALU.mult, ALU.add).then_inc(x2_done, 1)
                    if t == 0 and p_ + 1 < NOUT:
                        split_low(v, P_OUT + p_ + 1)
                    if t and p_ == 0:
                        norm2(t - 1)
                    if t and p_ == NOUT // 2:
                        norm2_turned(t - 1)
            norm2(TT - 1)
            norm2_turned(TT - 1)
            v.wait_ge(lg_full, TT)
            link(v.tensor_copy(lg[:], sc[0][:, 0:TT * (NG + NE)].rearrange("p (t n) -> p t n", t=TT)))
            r = lambda i, n=NE: rt[:, i, :, 0:n]
            s_ = lambda i: rs_[:, i, :]
            col = lambda i: s_(i).rearrange("p (t o) -> p t o", o=1)
            rev = lambda n: bc(e_rev[:, NE - n:NE].rearrange("p (o n) -> p o n", o=1), [P, TT, n])

            def first_max(dst, src, top, n):
                link(tt(r(11, n), src, bc(col(top), [P, TT, n]), ALU.is_equal))
                link(tt(r(11, n), r(11, n), rev(n), ALU.mult))
                link(v.tensor_reduce(s_(15), r(11, n), AX_X, ALU.max))
                link(tt(dst, r(11, n), bc(col(15), [P, TT, n]), ALU.is_equal))

            coarse, fine = lg[:, :, 0:NG], lg[:, :, NG:NG + NE]
            link(v.tensor_reduce(s_(0), coarse, AX_X, ALU.max))
            tt(r(0, NG), coarse, bc(col(0), [P, TT, NG]), ALU.subtract).then_inc(r_dve, 1)
            v.wait_ge(const_ready, 10)
            first_max(r(1, NG), coarse, 0, NG)
            link(ts(r(1, NG), r(1, NG), HIDE, -HIDE, ALU.mult, ALU.add))
            link(tt(r(2).rearrange("p t (g e) -> p t g e", g=NG), fine.rearrange("p t (g e) -> p t g e", g=NG),
                    bc(r(1, NG).rearrange("p t (g o) -> p t g o", o=1), [P, TT, NG, EPG]), ALU.add))
            link(v.tensor_reduce(s_(1), r(2), AX_X, ALU.max))
            first_max(r(3), r(2), 1, NE)
            link(stt(r(4), r(3), -3 * HIDE, r(2), ALU.mult, ALU.add))
            link(v.tensor_reduce(s_(2), r(4), AX_X, ALU.max))
            first_max(r(5), r(4), 2, NE)
            link(tt(r(6), r(3), r(5), ALU.add))
            link(v.memset(r(7)[:, 0:1], 0.0))
            for t in range(1, TT):
                link(tt(rt[:, 7, t, :], rt[:, 7, t - 1, :], rt[:, 6, t - 1, :], ALU.add))
            link(tt(cnt[:], rt[:, 7, TT - 1, :], rt[:, 6, TT - 1, :], ALU.add))
            v.sem_inc(r_pe, 1)
            tt(s_(6), s_(2), s_(1), ALU.subtract).then_inc(r_dve, 1)
            v.wait_ge(r_act, 1)
            link(v.tensor_reduce(s_(3), r(0, NG), AX_X, ALU.add))
            link(v.reciprocal(s_(4), s_(3)))
            v.wait_ge(r_act, 2)
            link(ts(s_(7), s_(6), 1.0, None, ALU.add))
            link(v.reciprocal(s_(8), s_(7)))
            link(tt(s_(9), s_(8), s_(4), ALU.mult))
            link(tt(s_(10), s_(9), s_(6), ALU.mult))
            link(tt(r(8), r(3), bc(col(9), [P, TT, NE]), ALU.mult))
            link(tt(r(9), r(5), bc(col(10), [P, TT, NE]), ALU.mult))
            ev = lambda w: w.rearrange("p t e -> p e t")
            link(tt(r(8), r(8), r(9), ALU.add))
            for n in (0, 3):
                mark(v.tensor_copy(tg[:, :, :, n], bc(tok_id[:, :].rearrange("p (o t) -> p o t", o=1), [P, NE, TT])))
            link(v.tensor_copy(tg[:, :, :, 1], ev(r(8))))
            mark(tt(tg[:, :, :, 2], ev(r(8)), tg[:, :, :, 1].bitcast(F32), ALU.subtract))
            settle()
            v.wait_ge(lg_full, TT + 1)
            link(v.tensor_copy(r(10), sc[0][:, 0:TT * NE].rearrange("p (t e) -> p t e", t=TT)))
            link(ts(r(7), r(6), -float(4 * SEQ), float(4 * SEQ), ALU.mult, ALU.add))
            tt(pos[:].rearrange("p e t -> p t e"), r(10), r(7), ALU.add).then_inc(route_done, 1)

            v.wait_ge(route_done, 1)
            for e in range(NE):
                if e >= 2:
                    v.wait_ge(idx_full, e - 1)
                tt(pick[e % 2], bc(slot_no[:].rearrange("p (o n) -> p o n", o=1), [P, TT, CAP]),
                   bc(pos[:, e, :].rearrange("p (t o) -> p t o", o=1), [P, TT, CAP]), ALU.is_equal).then_inc(pick_done, 1)
                if e in (EARLY + 1, NE - 1):
                    k = 0 if e < NE - 1 else 1
                    lo, hi = (0, EARLY) if k == 0 else (EARLY, NE)
                    v.wait_ge(idx_full, hi)
                    got = sc[k][:, 128:128 + 4 * (hi - lo)].rearrange("p (e n) -> p e n", n=4)
                    v.tensor_copy(idx_all[:, lo:hi], got[:, :, 0])
                    v.tensor_reduce(gate_all[:, lo:hi], got[:, :, 1:3], AX_X, ALU.add).then_inc(idx_done, 1)
            def rows_turned(e4, n):
                for f in range(2):
                    v.wait_ge(xt_full, n * 2 + (f - 1))
                    v.tensor_copy(xgT[e4 % 2][:, 4 * f:4 * f + 4, :], tp[f][:].rearrange("p (k n) -> p k n", k=4)
                                  ).then_inc(xt_done, 1)

            def swiglu(e4, n):
                b = e4 % 2
                v.wait_ge(th_done, n)
                stt(a1_e[b], th_e[b], 1.0, pj[b][:, 0:DE], ALU.add, ALU.mult).then_inc(act_done, 1)
                v.wait_ge(act_done, n * 2 - 1)
                stt(act_e[b], a1_e[b], 0.5, pj[b][:, DE:UP_N], ALU.mult, ALU.mult).then_inc(act_done, 1)

            rows_turned(0, 1)
            for k, oh in enumerate((3, 5)):
                link(tt(r(8), r(oh), bc(e_no[:].rearrange("p (o n) -> p o n", o=1), [P, TT, NE]), ALU.mult))
                link(v.tensor_reduce(s_(11), r(8), AX_X, ALU.add))
                link(tt(r(9), r(oh), r(10), ALU.mult))
                link(v.tensor_reduce(s_(12), r(9), AX_X, ALU.add))
                link(stt(s_(11), s_(11), float(CAP), s_(12), ALU.mult, ALU.add))
                for j in range(1, MORE + 1):
                    link(ts(s_(13), s_(12), float(j * CAP), float((NE - 1) * CAP), ALU.is_ge, ALU.mult))
                    link(tt(s_(11), s_(11), s_(13), ALU.add))
                link(v.tensor_copy(dest[:, k, :], s_(11)))
            v.wait_ge(lg_full, TT + 2)
            link(v.tensor_reduce(flag_f[:], mb[0][:, 0:NE], AX_X, ALU.max))
            v.tensor_scalar(flag[0:1, 0:1], flag_f[0:1, 0:1], float(CAP), None, ALU.is_gt).then_inc(flag_done, 1)
            with v.Fori(0, NE // 2 - 1) as i:
                for r_ in range(2):
                    swiglu(r_, i * 2 + (r_ + 1))
                    rows_turned(1 - r_, i * 2 + (r_ + 2))
            swiglu(0, NE - 1)
            rows_turned(1, NE)
            swiglu(1, NE)
            over = v.value_load(flag[0:1, 0:1], min_val=0, max_val=1)
            with v.If(over > 0):
                for b in range(2):
                    v.wait_ge(y_stored[b], 8 * NE)
                with v.Fori(0, MORE) as j:
                    ts(pos[:], pos[:], float(-CAP), None, ALU.add).then_inc(o_pos, 1)
                    v.wait_ge(o_pos, j + 1)
                    v.sem_inc(gather_turn, 1)
                    with v.Fori(0, NE) as e:
                        tt(pick[0], bc(slot_no[:].rearrange("p (o n) -> p o n", o=1), [P, TT, CAP]),
                           bc(pos[:, bass.ds(e, 1), :].rearrange("p e (t o) -> p (e t) o", o=1), [P, TT, CAP]),
                           ALU.is_equal).then_inc(o_pick, 1)
                        v.wait_ge(o_idxf, j * NE + e + 1)
                        v.tensor_copy(idx[:, 0:1], sc[0][:, 128:129])
                        v.tensor_reduce(gate[:, 0:1], sc[0][:, 129:131], AX_X, ALU.add).then_inc(o_idx, 1)
                        v.wait_ge(o_xt, j * NE + e + 1)
                        for f in range(2):
                            v.tensor_copy(xgT[0][:, 4 * f:4 * f + 4, :], tp[f][:].rearrange("p (k n) -> p k n", k=4)
                                          ).then_inc(o_xtd, 1)
                        v.wait_ge(o_th, j * NE + e + 1)
                        stt(a1_e[0], th_e[0], 1.0, pj[0][:, 0:DE], ALU.add, ALU.mult).then_inc(o_act, 1)
                        v.wait_ge(o_act, (j * NE + e) * 2 + 1)
                        stt(act_e[0], a1_e[0], 0.5, pj[0][:, DE:UP_N], ALU.mult, ALU.mult).then_inc(o_act, 1)
                        v.wait_ge(o_st, (j * NE + e + 1) * 16)
            for t in range(TT):
                v.wait_ge(rows_back[t], 32)
                for k in range(2):
                    ins = tt(x2[:, t, :], x2[:, t, :], gath[2 * t + k], ALU.add)
                    if k:
                        ins.then_inc(sum_done, 1)
                    else:
                        link(ins)

        @block.tensor
        def _(pe):
            def fill(order, frees, key):
                n, b, used = uses(order, key)
                if used:
                    pe.wait_ge(frees[b], used)
                return b

            pe.wait_ge(const_ready, 3)
            for t in range(TT):
                pe.wait_ge(xn_done, t + 1)
                for f in range(2):
                    b = fill(tp_order, tp_free, ("h", t, f))
                    for k in range(4):
                        ins = pe.transpose(tp[b][:, k * P:(k + 1) * P], xn[:, t, (4 * f + k) * P:(4 * f + k + 1) * P], ident[:])
                    ins.then_inc(tp_full, 1)
            def product(dst, terms):
                for i, ((sh, sl), (mh, ml)) in enumerate(terms):
                    pe.matmul(dst, sh, mh, start=i == 0, stop=False)
                    pe.matmul(dst, sh, ml, start=False, stop=False)
                    ins = pe.matmul(dst, sl, mh, start=False, stop=i == len(terms) - 1)
                return ins

            def piece_ready(n):
                pe.wait_ge(high_done, n + 1)
                low_ready(pe, n)

            both = lambda hl, *ix: tuple(x[(slice(None),) + ix] for x in hl)
            h_hl = (h_high, h_low)
            for b in range(2):
                pe.wait_ge(tp_free[b], TT)
            for c in range(CT_):
                if c % 2 == 0:
                    piece_ready(P_U + c // 2)
                w = piece_w(P_U + c // 2, k=DC, n=256)
                b = fill(pj_order, pj_free, ("u", c))
                c0 = c % 2 * P
                product(pj[b][:], [(both(w, k, slice(c0, c0 + P)), both(h_hl, k, slice(None))) for k in range(DC)]
                        ).then_inc(pj_full, 1)
                if c == 0:
                    b = fill(tp_order, tp_free, ("prm",))
                    pe.wait_ge(rows_done, 1)
                    for i, src in enumerate((13, 14, 15, 16, 6, 8, 7)):
                        ins = pe.transpose(tp[b][:, i * ST:(i + 1) * ST], R(src), ident[0:ST, 0:ST])
                    ins.then_inc(tp_full, 1)
                if c == 2:
                    pe.wait_ge(cexp_done, 1)
                    for f in range(2):
                        b = fill(tp_order, tp_free, ("ct", f))
                        for g in range(CT_):
                            ins = pe.transpose(tp[b][:, g * P:(g + 1) * P], c_exp[:, f, g].rearrange("p g s -> p (g s)"), ident[:])
                        ins.then_inc(tp_full, 1)

            def turn_qk(j):
                pe.wait_ge(qk_norm, j + 1)
                b = fill(tp_order, tp_free, ("qkt", j))
                for k in range(2):
                    ins = pe.transpose(tp[b][:, k * P:(k + 1) * P],
                                       qk_nrm[j % 4][:, 2 * k:2 * k + 2, :].rearrange("p h d -> p (h d)"), ident[:])
                ins.then_inc(tp_full, 1)

            for j in range(3 * TT):
                if j % TT == 0:
                    piece_ready(P_QKV + j // TT)
                w = piece_w(P_QKV + j // TT, k=DC, n=256)
                b = fill(pj_order, pj_free, ("qkv", j))
                tok = slice(j % TT * P, (j % TT + 1) * P)
                product(pj[b][:, 0:256], [(both(h_hl, k, tok), both(w, k, slice(None))) for k in range(DC)]).then_inc(pj_full, 1)
                if j >= 2:
                    turn_qk(j - 2)
            for j in range(3 * TT - 2, 3 * TT):
                turn_qk(j)

            def scores(a):
                blk, kv = a // KVH, a % KVH
                W = 2 * P if blk else P
                t0 = blk * P
                pe.wait_ge(qT_done, 3 * TT)
                if a:
                    pe.wait_ge(sc_read, a)
                for h in range(QPK):
                    hh = kv * QPK + h
                    ps = slice((hh % 2) * HD, (hh % 2) * HD + HD)
                    ins = pe.matmul(sc[h % 2][:, (h // 2) * 2 * P:(h // 2) * 2 * P + W], qT[ps, hh // 2, t0:t0 + P],
                                    kT[ps, kv, t0 + P - W:t0 + P], start=True, stop=True)
                ins.then_inc(sc_full, 1)

            def turn_probs(a):
                blk = a // KVH
                pe.wait_ge(p_done, a + 1)
                for f in range(2 if blk else 1):
                    b = fill(tp_order, tp_free, ("pt", a, f))
                    for h in range(QPK):
                        ins = pe.transpose(tp[b][:, h * P:(h + 1) * P], probs[a % 2][:, h, f * P:(f + 1) * P], ident[:])
                    ins.then_inc(tp_full, 1)

            n_pt = [0]

            def values(a):
                blk, kv = a // KVH, a % KVH
                nf = 2 if blk else 1
                n_pt[0] += nf
                pe.wait_ge(pT_done, n_pt[0])
                pe.wait_ge(v_done, TT)
                b = fill(pj_order, pj_free, ("av", a))
                ph = pT.rearrange("p f (a b) q -> p f b a q", b=2)
                for odd in range(2):
                    for f in range(nf):
                        ins = pe.matmul(pj[b][odd * HD:(odd + 1) * HD, 0:2 * P].rearrange("p (a q) -> p a q", a=2),
                                        v_tok[:, blk - nf + 1 + f, kv * HD:(kv + 1) * HD], ph[:, f, odd],
                                        start=f == 0, stop=f == nf - 1)
                ins.then_inc(pj_full, 1)

            def turn_input_weights(c):
                pe.wait_ge(w1_done, c + 1)
                for f in range(2):
                    b = fill(tp_order, tp_free, ("w", c, f))
                    for q in range(SPC):
                        ins = pe.transpose(tp[b][:, q * P:(q + 1) * P], w1[:, f, q].rearrange("p i c -> p (i c)"), ident[:])
                    ins.then_inc(tp_full, 1)

            def own_inputs(c):
                pe.wait_ge(cl_done, c + 1)
                b = fill(tp_order, tp_free, ("k", c))
                for q in range(SPC):
                    s = c * SPC + q
                    dst = tp[b][0:TCH, q * P:(q + 1) * P]
                    pe.matmul(dst, Bre[:, s, :], CLre[:, q, 0:SUB, :], start=True, stop=False)
                    ins = pe.matmul(dst, Bim[:, s, :], CLim[:, q, 0:SUB, :], start=False, stop=True)
                ins.then_inc(tp_full, 1)

            def chunk_inputs(c):
                pe.wait_ge(w1T_done, 2 * (c + 1))
                pe.wait_ge(u4_loaded, 16 * SUB * SPC)
                if c:
                    pe.wait_ge(yv_done, c)
                    pe.wait_ge(y_evac, c)
                for q in range(SPC):
                    for f in range(2):
                        ins = pe.matmul(mb[f][:, q * P:(q + 1) * P], w1T[:, f, q, :], u4[:, c * SPC + q, :], start=True, stop=True)
                ins.then_inc(bu_full, 1)

            def chunk_outputs(c):
                pe.wait_ge(S_done, c + 1)
                pe.wait_ge(toep_done, SUB * (c + 1))
                yb = mb[0][:].rearrange("p (j c) -> p j c", j=SUB)
                for q in range(SPC):
                    dst = yb[:, :, q * TCH:(q + 1) * TCH]
                    pe.matmul(dst, u4[:, c * SPC + q, :], toep[:, q, :], start=q == 0, stop=False, skip_group_check=True)
                for q in range(SPC):
                    dst = yb[:, :, q * TCH:(q + 1) * TCH]
                    pe.matmul(dst, Sre[:, q, :], CLre[:, q, 1:, :], start=False, stop=False, skip_group_check=True)
                    ins = pe.matmul(dst, Sim[:, q, :], CLim[:, q, 1:, :], start=False, stop=q == SPC - 1, skip_group_check=True)
                ins.then_inc(y_full, 1)

            def turn_outputs(c):
                pe.wait_ge(y_evac, c + 1)
                yt = tb[0].rearrange("p q n -> p (q n)")
                for j in range(SUB):
                    ins = pe.transpose(mb[1][:, j * P:(j + 1) * P], yt[:, j * P:(j + 1) * P], ident[:])
                ins.then_inc(z_full, 1)

            for i in range(2 * DC + 1):
                if i < 2 * DC:
                    if i % 2 == 0:
                        piece_ready(P_G + i // 2)
                    w = piece_w(P_G + i // 2, k=DC, n=256)
                    b = fill(pj_order, pj_free, ("gate", i))
                    c0 = i % 2 * P
                    product(pj[b][:], [(both(w, k, slice(c0, c0 + P)), both(h_hl, k, slice(None))) for k in range(DC)]
                            ).then_inc(pj_full, 1)
                if i % 4 == 0 and i >= 4:
                    turn_outputs(i // 4 - 1)
                if i % 4 == 0 and i < 2 * DC:
                    turn_input_weights(i // 4)
                if i % 4 == 1:
                    chunk_inputs(i // 4)
                    own_inputs(i // 4)
                if i % 2 == 0 and i < 2 * DC:
                    scores(i // 2)
                if i % 2 == 1:
                    if i % 4 == 3:
                        chunk_outputs(i // 4)
                    turn_probs(i // 2)
                if i % 2 == 0 and i >= 2:
                    values(i // 2 - 1)
            pe.wait_ge(gates_done, 2 * DC)
            pe.wait_ge(z_done, CT_)
            pe.wait_ge(av_done, NQ)
            pe.wait_ge(sc_read, NQ)
            pe.wait_ge(zy_low, 2)
            for m in range(DC):
                if m >= 2:
                    pe.wait_ge(mg_free, m - 1)
                piece_ready(P_M + m)
                w = piece_w(P_M + m, f=3, k=4, n=P)
                for f, (dst, k0) in enumerate(zip(merge_banks(m), (0, 0, 4))):
                    product(dst[:], [(both(w, f, k, slice(None)), both(h_hl, k0 + k, slice(None))) for k in range(4)]
                            ).then_inc(mg_full, 1)
            pe.wait_ge(m_low_done, DC)
            m_hl = (m_high, m_low)

            def turn_norm2(t):
                pe.wait_ge(n2_done, t + 1)
                if t:
                    pe.wait_ge(h2T_done, 2 * t)
                else:
                    for b in range(2):
                        pe.wait_ge(tp_free[b], (n_tp + 1 - b) // 2)
                for f in range(2):
                    for k in range(4):
                        ins = pe.transpose(tp[f][:, k * P:(k + 1) * P], xg[t % 2][:, (4 * f + k) * P:(4 * f + k + 1) * P], ident[:])
                    ins.then_inc(tp_full, 1)

            def router(t):
                pe.wait_ge(h2T_done, 2 * (t + 1))
                for k in range(DC):
                    ins = pe.matmul(sc[0][:, t * (NG + NE):(t + 1) * (NG + NE)], xgT[t % 2][:, k, :], rw[:, k, :],
                                    start=k == 0, stop=k == DC - 1)
                ins.then_inc(lg_full, 1)

            for t in range(TT):
                for p_ in range(NOUT):
                    if t == 0:
                        piece_ready(P_OUT + p_)
                    w = piece_w(P_OUT + p_, k=DC, n=256)
                    n = NOUT * t + p_
                    if n >= 2:
                        pe.wait_ge(x2_done, n - 1)
                    product(pj[n % 2][:, 0:256], [(both(m_hl, k, slice(t * P, (t + 1) * P)), both(w, k, slice(None))) for k in range(DC)]
                            ).then_inc(pj_full, 1)
                    if t and p_ == NOUT // 2 - 1:
                        turn_norm2(t - 1)
                    if t and p_ == NOUT - 1:
                        router(t - 1)
            turn_norm2(TT - 1)
            router(TT - 1)
            pe.wait_ge(r_pe, 1)
            pe.wait_ge(const_ready, 10)
            flat = lambda i: rt[:, i].rearrange("p t e -> p (t e)")
            pe.matmul(sc[0][:, 0:TT * NE], before[:], flat(6), start=True, stop=False)
            pe.matmul(sc[0][:, 0:TT * NE], ones[:], flat(7), start=False, stop=True).then_inc(lg_full, 1)
            pe.matmul(mb[0][:, 0:NE], ones[:], cnt[:], start=True, stop=True).then_inc(lg_full, 1)

            pe.wait_ge(route_done, 1)
            for e in range(NE):
                k = 0 if e < EARLY else 1
                c0 = 128 + 4 * (e - EARLY * k)
                pe.wait_ge(pick_done, e + 1)
                for t in range(TT):
                    ins = pe.matmul(sc[k][:, c0:c0 + 4], pick[e % 2][:, t, :], tg[:, e, t, :], start=t == 0, stop=t == TT - 1)
                ins.then_inc(idx_full, 1)

            def turn_rows(e4, e, n_rows):
                pe.wait_ge(gathered[e4 % 2], n_rows)
                for f in range(2):
                    if not (isinstance(e, int) and e == 0):
                        pe.wait_ge(xt_done, e * 2 + (f - 1))
                    for k in range(4):
                        ins = pe.transpose(tp[f][:, k * P:(k + 1) * P], xg[e4 % 2][:, (4 * f + k) * P:(4 * f + k + 1) * P], ident[:])
                    ins.then_inc(xt_full, 1)

            def up(e4, e, n_loaded):
                pe.wait_ge(ring_loaded[e4], n_loaded)
                pe.wait_ge(xt_done, (e + 1) * 2)
                if not (isinstance(e, int) and e < 2):
                    pe.wait_ge(act_done, e * 2 - 2)
                w = ring[e4].rearrange("p (k n) -> p k n", k=DC)
                for k in range(DC):
                    ins = pe.matmul(pj[e4 % 2][:], xgT[e4 % 2][:, k, :], w[:, k, :], start=k == 0, stop=k == DC - 1)
                ins.then_inc(up_full, 1)

            def turn_act(n4, e):
                e4 = (n4 + 3) % 4
                pe.wait_ge(act_done, (e + 1) * 2)
                if not (isinstance(e, int) and e == 0):
                    pe.wait_ge(at_done, e)
                for k in range(2):
                    ins = pe.transpose(sc[1][:, k * P:(k + 1) * P], act_e[e4 % 2][:, k * P:(k + 1) * P], ident[:])
                ins.then_inc(at_full, 1)

            def down_(e4, e, n_loaded):
                pe.wait_ge(at_done, e + 1)
                pe.wait_ge(down_loaded[e4], n_loaded)
                if not (isinstance(e, int) and e == 0):
                    pe.wait_ge(y_scaled, e * 2)
                for h in range(2):
                    for k in range(2):
                        ins = pe.matmul(mb[h][:], actT[e4 % 2][:, k, :], down[e4][:, k, h * 512:(h + 1) * 512], start=k == 0, stop=k == 1)
                ins.then_inc(dn_full, 1)

            def step(e4, e, rnd, first=False, last=False):
                up(e4, e, rnd * 16 + 16)
                if not first:
                    turn_act(e4, e - 1)
                if not last:
                    n4 = (e4 + 1) % 4
                    turn_rows(n4, e + 1, (rnd if e4 < 3 else rnd + 1) * 32 + (16 * (n4 // 2) + 16))
                if not first:
                    p4 = (e4 + 3) % 4
                    down_(p4, e - 1, (rnd if e4 else rnd - 1) * 16 + 16)

            pe.wait_ge(idx_done, 2)
            turn_rows(0, 0, 16)
            for e in range(4):
                step(e, e, 0, first=e == 0)
            with pe.Fori(0, NE // 4 - 2) as i:
                for r in range(4):
                    step(r, i * 4 + (r + 4), i + 1)
            for e in range(NE - 4, NE):
                step(e % 4, e, e // 4, last=e == NE - 1)
            turn_act(0, NE - 1)
            down_(3, NE - 1, 16 * (NE // 4))
            pe.wait_ge(dn_full, NE)
            pe.sem_inc(o_dn, 1)
            pe.wait_ge(flag_done, 1)
            over = pe.value_load(flag[0:1, 0:1], min_val=0, max_val=1)
            with pe.If(over > 0):
                w = ring[0].rearrange("p (k n) -> p k n", k=DC)
                with pe.Fori(0, MORE) as j:
                    with pe.Fori(0, NE) as e:
                        b = j * NE + e
                        pe.wait_ge(o_pick, b + 1)
                        for t in range(TT):
                            ins = pe.matmul(sc[0][:, 128:132], pick[0][:, t, :],
                                            tg[:, bass.ds(e, 1), t, :].rearrange("p e n -> p (e n)"), start=t == 0, stop=t == TT - 1)
                        ins.then_inc(o_idxf, 1)
                        pe.wait_ge(o_gath, (b + 1) * 16)
                        for k in range(DC):
                            ins = pe.transpose(tp[k // 4][:, (k % 4) * P:(k % 4 + 1) * P], xg[0][:, k * P:(k + 1) * P], ident[:])
                        ins.then_inc(o_xt, 1)
                        pe.wait_ge(o_xtd, (b + 1) * 2)
                        pe.wait_ge(o_w, (b + 1) * 32)
                        for k in range(DC):
                            ins = pe.matmul(pj[0][:], xgT[0][:, k, :], w[:, k, :], start=k == 0, stop=k == DC - 1)
                        ins.then_inc(o_up, 1)
                        pe.wait_ge(o_act, (b + 1) * 2)
                        for k in range(2):
                            ins = pe.transpose(sc[1][:, k * P:(k + 1) * P], act_e[0][:, k * P:(k + 1) * P], ident[:])
                        ins.then_inc(o_at, 1)
                        pe.wait_ge(o_atd, b + 1)
                        for h in range(2):
                            for k in range(2):
                                ins = pe.matmul(mb[h][:], actT[0][:, k, :], down[0][:, k, h * 512:(h + 1) * 512], start=k == 0, stop=k == 1)
                        ins.then_inc(o_dn, 1)


_INS = ['x', 'norm_mix', 'w_in', 'ssm_lam_re', 'ssm_lam_im', 'ssm_log_dt', 'ssm_b_re', 'ssm_b_im', 'ssm_c_re',
        'ssm_c_im', 'ssm_d', 'w_ssm_glu_val', 'w_ssm_glu_gate', 'q_norm', 'k_norm', 'attn_sinks', 'w_attn_up',
        'w_out', 'norm_ffn', 'w_coarse', 'w_fine', 'w_expert_up', 'w_expert_down']
_OUTS = [((1, 512, 1024), 'float32')]


def kernel(**inputs):
    import numpy as _np
    import concourse.bacc as _bacc
    from concourse import mybir as _mybir
    from concourse.bass_utils import run_bass_kernel_spmd as _run

    nc = _bacc.Bacc("TRN2", target_bir_lowering=False, num_devices=1)
    arrays, args = {}, []
    for name in _INS:
        a = _np.ascontiguousarray(inputs[name])
        arrays[f"in_{name}_dram"] = a
        args.append(nc.dram_tensor(f"in_{name}_dram", a.shape, _mybir.dt.from_np(a.dtype), kind="ExternalInput").ap())
    for i, (shape, dtype) in enumerate(_OUTS):
        dt = _mybir.dt.from_np(_np.dtype(dtype))
        args.append(nc.dram_tensor(f"out_{i}_dram", shape, dt, kind="ExternalOutput").ap())
    hybrid_layer(nc, *args)
    r = _run(nc, [arrays], core_ids=[0])
    got = tuple(r.results[0][f"out_{i}_dram"] for i in range(len(_OUTS)))
    return got[0]
```

```python
import math
from contextlib import ExitStack

import concourse.bass as bass
from concourse import mybir

F32 = mybir.dt.float32
F32R = mybir.dt.float32r
I32 = mybir.dt.int32
U32 = mybir.dt.uint32
ALU = mybir.AluOpType
ACT = mybir.ActivationFunctionType
AX_X = mybir.AxisListType.X

P = 128
EPS = 1e-6
MAGIC = 1.5 * 2.0 ** 23
TWO_PI_HIGH = 6.28125
TWO_PI_LOW = 2.0 * math.pi - TWO_PI_HIGH
HIDE = 1e30
GELU_IN = math.sqrt(2.0 / math.pi)
GELU_CUBE = 0.044715


def hybrid_layer(nc, x, norm_mix, w_in, lam_re, lam_im, log_dt, b_re, b_im, c_re, c_im, d_skip,
                 w_glu_val, w_glu_gate, q_norm, k_norm, sinks, w_attn_up, w_out, norm_ffn,
                 w_coarse, w_fine, w_up, w_down, out):
    SEQ, D = x.shape[1], x.shape[2]
    DC = D // P
    TT = SEQ // P
    SSM_W = d_skip.shape[1]
    CT_ = SSM_W // P
    GROUPS, STATE = lam_re.shape[1], lam_re.shape[2]
    GCH = b_re.shape[3]
    ST = GROUPS * STATE // P
    SPC = ST // CT_
    SUB = 4
    CH = SEQ // SUB
    TCH = 2 * GCH
    HEADS, HD = sinks.shape[1], q_norm.shape[1]
    KVH = 2
    QPK = HEADS // KVH
    AW = HEADS * HD
    KW = KVH * HD
    NG = w_coarse.shape[2]
    NE = w_fine.shape[2]
    EPG = NE // NG
    DE = w_down.shape[2]
    UP_N = 2 * DE
    CAP = P
    MORE = SEQ // CAP - 1
    LISTS = [0, 2, NE // 2, NE]
    NQ = TT * KVH
    assert CH == P and TCH * SUB == P and SPC * TCH == P and HD * 2 == P and UP_N == 512

    h2_rows = nc.dram_tensor("h2_rows", [SEQ, D], F32, kind="Internal").ap()
    y_rows = nc.dram_tensor("y_rows", [NE * CAP, D], F32, kind="Internal").ap()
    y_all = nc.dram_tensor("y_all", [NE * SEQ, D], F32, kind="Internal").ap()

    with ExitStack() as ctx:
        def sb(name, shape, dt=F32):
            return ctx.enter_context(nc.sbuf_tensor(name, shape, dt))

        def sem(name):
            return ctx.enter_context(nc.semaphore(name))

        SLOT = DC * 512
        DOWN = 2 * D
        SSM_FLOATS = 2 * 512 + 2 * 512 + 2 * SPC * (SUB + 1) * TCH + 512 + 2 * 512 + 2 * 512 + 2 * 512 + 6 * 512
        PIECE = DC * 256
        sizes = dict(raw=2 * PIECE, pair=4 * PIECE, ht=2 * SLOT, uz=CT_ * 512, qy=4 * 512, gs=SLOT, ga=SLOT, u4=ST * CH,
                     att=3 * 1024, v=TT * KW, kt=KVH * SEQ, rot=4 * SPC * CH // 2, ssm=max(SSM_FLOATS, 4 * DOWN + 6 * 256))
        arena_at = (nc.sbuf_base + 31) // 32 * 32
        front = ("raw", "pair", "ht")
        n_front = sum(sizes[name] for name in front)
        arenas = [sb("arena_front", [P, n_front]), sb("arena_back", [P, sum(sizes.values()) - n_front])]
        at, off = {}, 0
        for name, n in sizes.items():
            at[name] = off
            off += n

        def part(name, start, size, /, **dims):
            o = at[name] + start
            v = arenas[0][:, o:o + size] if name in front else arenas[1][:, o - n_front:o - n_front + size]
            if dims:
                v = v.rearrange("row (%s) -> row %s" % (" ".join(dims), " ".join(dims)),
                                **{k: d for k, d in list(dims.items())[1:]})
            return v

        def rounded(name, where, start, shape):
            return nc.alloc_sbuf_tensor_at(name, shape, F32R, offset=arena_at + 4 * (at[where] + start))

        raw = [part("raw", s * PIECE, PIECE) for s in range(2)]
        places = [("pair", 0), ("pair", 2 * PIECE), ("ht", 0), ("ht", 2 * PIECE)]
        split = rounded("split", "pair", 0, [P, 2, 2, 2, PIECE])
        q_split = rounded("q_split", "gs", 0, [P, 2, 2, PIECE])
        w_high = [split[:, s // 2, s % 2, 0] for s in range(4)] + [q_split[:, s, 0] for s in range(2)]
        w_low = [split[:, s // 2, s % 2, 1] for s in range(4)] + [q_split[:, s, 1] for s in range(2)]
        out_high, out_low = split[:, :, :, 0], split[:, :, :, 1]
        h_high = rounded("h_high", "ht", 0, [P, DC, SEQ])
        h_low = rounded("h_low", "ht", SLOT, [P, DC, SEQ])
        m_high = rounded("m_high", "gs", 0, [P, DC, SEQ])
        m_low = rounded("m_low", "ga", 0, [P, DC, SEQ])
        down = [part("ssm", s * DOWN, DOWN, k=2, n=D) for s in range(2)]
        up_high = [rounded(f"up_high{s}", "gs", s * SLOT, [P, SLOT]) for s in range(2)]
        down_high = [rounded(f"down_high{s}", "ssm", (2 + s) * DOWN, [P, DOWN]) for s in range(2)]
        down_low = [rounded(f"down_low{s}", "ssm", s * DOWN, [P, DOWN]) for s in range(2)]
        x_in = part("gs", 0, SLOT, t=TT, d=D)
        xn = part("ga", 0, SLOT, t=TT, d=D)
        mix_gain = part("qy", 0, D)
        ffn_gain = part("kt", 0, D)
        x2 = part("uz", 0, SLOT, t=TT, d=D)
        ts_gate = part("gs", 0, SLOT, m=DC, t=SEQ)
        ta_gate = part("ga", 0, SLOT, m=DC, t=SEQ)
        uT = part("uz", 0, CT_ * 512, c=CT_, j=SUB, n=CH)
        zT = part("uz", 0, CT_ * 512, c=CT_, t=SEQ)
        qT = part("qy", 0, 4 * 512, h=4, t=SEQ)
        u4 = part("u4", 0, ST * CH, s=ST, n=CH)
        qk_raw = [part("att", 512 * i, 512, h=HEADS, d=HD) for i in range(2)]
        qk_sq = [part("att", 1024 + 512 * i, 512, h=HEADS, d=HD) for i in range(2)]
        qk_nrm = [part("att", 2048 + 512 * i, 512, h=HEADS, d=HD) for i in range(2)]
        v_tok = part("v", 0, TT * KW, t=TT, n=KW)
        kT = part("kt", 0, KVH * SEQ, g=KVH, t=SEQ)
        probs = [part("att", 1024 * i, 1024, h=QPK, k=2 * P) for i in range(2)]
        pT = part("att", 2048, 1024, f=2, h=QPK, q=P)
        def R(i):
            return part("att", i * P, P)[0:ST, :]

        o = 0
        ssm = {}
        for name, n in [("Bre", 512), ("Bim", 512), ("Cre", 512), ("Cim", 512), ("CL", 2 * SPC * (SUB + 1) * TCH), ("toep", 512), ("Ec", 512), ("Es", 512),
                        ("w1T", 1024), ("w1", 1024)] + [(f"t{i}", 512) for i in range(4)] + [("Sre", 512), ("Sim", 512)]:
            ssm[name] = (o, n)
            o += n

        def spart(name, start=0, size=None, /, **dims):
            return part("ssm", ssm[name][0] + start, size or ssm[name][1], **dims)

        Bre, Bim = (spart(n, s=ST, c=TCH) for n in ("Bre", "Bim"))
        Cre, Cim = (spart(n, s=ST, c=TCH) for n in ("Cre", "Cim"))
        NCL = SPC * (SUB + 1) * TCH
        CLre, CLim = (spart("CL", f * NCL, NCL, s=SPC, j=SUB + 1, c=TCH) for f in range(2))
        toep = spart("toep", q=SPC, n=SUB * TCH)
        Ec, Es = spart("Ec", q=SPC, n=CH), spart("Es", q=SPC, n=CH)
        w1T = spart("w1T", f=2, q=SPC, n=P)
        w1 = spart("w1", f=2, q=SPC, i=SUB, c=TCH)
        tb = [spart(f"t{i}", q=SPC, n=CH) for i in range(4)]
        Sre, Sim = spart("Sre", q=SPC, n=CH), spart("Sim", q=SPC, n=CH)
        xg = [part("raw", D * i, D) for i in range(2)]
        xgT = [part("raw", 2 * D + D * i, D, k=DC, n=P) for i in range(2)]
        xt_high = [rounded("xt_high0", "raw", 2 * D, [P, DC, P]), rounded("xt_high1", "u4", 0, [P, DC, P])]
        xt_low = [rounded("xt_low0", "raw", 3 * D, [P, DC, P]), rounded("xt_low1", "u4", D, [P, DC, P])]
        h2 = [part("u4", D * i, D) for i in range(2)]
        y_out = [part("att", 1280 + D * i, D) for i in range(2)]
        at_high = [rounded(f"at_high{i}", "att", 1280 + 2 * D + 512 * i, [P, 2, P]) for i in range(2)]
        at_low = [rounded(f"at_low{i}", "att", 1280 + 2 * D + 512 * i + 256, [P, 2, P]) for i in range(2)]
        actT = part("att", 1280 + 2 * D, 256, k=2, n=P)
        th_e = [part("ssm", 4 * DOWN + 256 * i, 256) for i in range(2)]
        a1_e = [part("ssm", 4 * DOWN + 512 + 256 * i, 256) for i in range(2)]
        act_e = [part("ssm", 4 * DOWN + 1024 + 256 * i, 256) for i in range(2)]
        pick = [rounded(f"pick{i}", "rot", 512 * i, [P, TT, CAP])[:] for i in range(2)]
        gath = [part("pair", D * i, D) for i in range(2 * TT)]

        ident = sb("ident", [P, P])
        before = sb("before", [P, P])
        ones = sb("ones", [P, P])
        slot_no = sb("slot_no", [P, CAP])
        neg_dist = sb("neg_dist", [P, 2 * P])
        tok_id = sb("tok_id", [P, TT])
        e_no = sb("e_no", [P, NE])
        e_rev = sb("e_rev", [P, NE])
        par_i = sb("par_i", [P, 1], I32)
        par = sb("par", [P, 3])
        half_col = sb("half_col", [P, 16])
        halfpi = sb("halfpi", [P, 1])
        d_col = sb("d_col", [P, CT_])
        qg = sb("qg", [P, 3])
        sink = sb("sink", [P, HEADS])
        ssq = sb("ssq", [P, 2 * TT])
        rstd = sb("rstd", [P, 2 * TT])
        qss = sb("qss", [P, 2 * TT, HEADS])
        qrs = sb("qrs", [P, 2 * TT, HEADS])
        ldt = sb("ldt", [ST, 2, 2])
        prm = sb("prm", [P, 7, ST])
        b_raw = spart("Sre", 0, 512, f=2, s=ST, h=GCH)
        c_raw = spart("Sim", 0, 512, f=2, c=CT_, p=STATE)
        c_exp = part("ga", 0, 1024, f=2, c=CT_, g=2, p=STATE)
        pw = sb("pw", [P, 2, SUB + 1, ST])
        pw_down = sb("pw_down", [P, 2, SUB - 1, ST])
        e1 = sb("e1", [P, 2, 3, ST])
        sc_t = sb("sc_t", [P, 6, ST])
        et = part("rot", 0, 4 * SPC * CH // 2, f=4, s=SPC, n=CH // 2)
        weight_tmp = sb("weight_tmp", [P, SPC, SUB * TCH])
        smx = sb("smx", [P, 2, 6, QPK])
        rw = sb("rw", [P, DC, NG + NE])
        rt = part("att", 0, 12 * TT * NE, f=12, t=TT, e=NE)
        lg = part("att", 768, TT * (NG + NE), t=TT, n=NG + NE)
        rs_ = sb("rs_", [P, 16, TT])
        tg = rounded("tg", "att", 1024, [P, NE, TT, 4])
        pos = sb("pos", [P, NE, TT])
        cnt = sb("cnt", [P, NE])
        flag_f = sb("flag_f", [P, 1])
        flag = sb("flag", [1, 1], I32)
        idx_all = sb("idx_all", [P, NE], U32)
        gate_all = sb("gate_all", [P, NE])
        idx = sb("idx", [P, 2], U32)
        gate = sb("gate", [P, 1])
        dest = sb("dest", [P, 2, TT], U32)

        def bank(name):
            return ctx.enter_context(nc.psum_tensor(name, [P, 512], F32))

        pj = [bank("pj0"), bank("pj1")]
        tp = [bank("tp0"), bank("tp1")]
        sc = [bank("sc0"), bank("sc1")]
        mb = [bank("m0"), bank("m1")]

        const_ready = sem("const_ready")
        small_loaded, rows_loaded = sem("small_loaded"), sem("rows_loaded")
        mix_gain_loaded, ffn_gain_loaded = sem("mix_gain_loaded"), sem("ffn_gain_loaded")
        x_loaded = [sem(f"x_loaded{t}") for t in range(TT)]
        x_again = sem("x_again")
        ring_loaded = [sem(f"ring_loaded{s}") for s in range(4)]
        raw_loaded = [sem("raw_loaded0"), sem("raw_loaded1")]
        high_done, low_done_v, low_done_p = sem("high_done"), sem("low_done_v"), sem("low_done_p")
        h_high_done = sem("h_high_done")
        zy_high, zy_low = sem("zy_high"), sem("zy_low")
        m_high_done, m_low_done = sem("m_high_done"), sem("m_low_done")
        down_loaded = [sem(f"down_loaded{s}") for s in range(2)]
        sq_done = sem("sq_done")
        var_done = sem("var_done")
        rstd_done = sem("rstd_done")
        xn_done = sem("xn_done")
        pj_full, tp_full = sem("pj_full"), sem("tp_full")
        pj_free = [sem("pj_free0"), sem("pj_free1")]
        tp_free = [sem("tp_free0"), sem("tp_free1")]
        uT_done, u4_loaded = sem("uT_done"), sem("u4_loaded")
        qk_evac, qk_var, qk_rstd, qk_norm = sem("qk_evac"), sem("qk_var"), sem("qk_rstd"), sem("qk_norm")
        v_done, qT_done = sem("v_done"), sem("qT_done")
        gates_done = sem("gates_done")
        sc_full, sc_read, m_ready, exp_done, p_done = (sem(n) for n in ("sc_full", "sc_read", "m_ready", "exp_done", "p_done"))
        sum_ready = sem("sum_ready")
        pT_done, av_done = sem("pT_done"), sem("av_done")
        prm_act, prm_dve = sem("prm_act"), sem("prm_dve")
        rows_done, cexp_done, bbd_done = (sem(n) for n in ("rows_done", "cexp_done", "bbd_done"))
        rot_done = sem("rot_done")
        e_done = sem("e_done")
        w1_done, w1T_done, cl_done, toep_done = (sem(n) for n in ("w1_done", "w1T_done", "cl_done", "toep_done"))
        bu_full, bu_read, S_done = sem("bu_full"), sem("bu_read"), sem("S_done")
        y_full, y_evac, z_full, yv_done = (sem(n) for n in ("y_full", "y_evac", "z_full", "yv_done"))
        z_sq, z_arg, z_th, z_done = (sem(n) for n in ("z_sq", "z_arg", "z_th", "z_done"))
        mg_full, mg_act, mg_free, merged_done = (sem(n) for n in ("mg_full", "mg_act", "mg_free", "merged_done"))
        x2_done = sem("x2_done")
        n2_done, h2_scaled, h2T_done, lg_full = (sem(n) for n in ("n2_done", "h2_scaled", "h2T_done", "lg_full"))
        h2_stored = [sem(f"h2_stored{t}") for t in range(TT)]
        r_dve, r_act, r_pe = sem("r_dve"), sem("r_act"), sem("r_pe")
        route_done, flag_done = sem("route_done"), sem("flag_done")
        dve_chain, pool_chain = sem("dve_chain"), sem("pool_chain")
        pick_done, idx_full, idx_done = (sem(n) for n in ("pick_done", "idx_full", "idx_done"))
        gathered = [sem("gathered0"), sem("gathered1")]
        y_stored = [sem("y_stored0"), sem("y_stored1")]
        xt_full, xt_done, up_full, th_done, act_done = (sem(n) for n in ("xt_full", "xt_done", "up_full", "th_done", "act_done"))
        up_high_done, first_low_done, up_low_done = sem("up_high_done"), sem("first_low_done"), sem("up_low_done")
        down_high_done, down_low_done = sem("down_high_done"), sem("down_low_done")
        xt_high_done, at_high_done = sem("xt_high_done"), sem("at_high_done")
        at_full, at_done, dn_full, y_scaled = (sem(n) for n in ("at_full", "at_done", "dn_full", "y_scaled"))
        o_pick, o_idxf, o_idx, o_gath, o_xt, o_xtd, o_up = (sem(n) for n in ("o_pick", "o_idxf", "o_idx", "o_gath", "o_xt", "o_xtd", "o_up"))
        o_th, o_act, o_at, o_atd, o_dn, o_y, o_st, o_w, o_pos, o_copy = (sem(n) for n in ("o_th", "o_act", "o_at", "o_atd", "o_dn", "o_y", "o_st", "o_w", "o_pos", "o_copy"))
        rows_back = [[sem(f"rows_back{k}_{t}") for t in range(TT)] for k in range(2)]
        idx_taken = sem("idx_taken")
        gather_turn = sem("gather_turn")
        sum_done, out_stored = sem("sum_done"), sem("out_stored")

        pj_order, tp_order = [], []
        for t in range(TT):
            tp_order += [("h", t, f) for f in range(2)]
        pj_order += [("u", c) for c in range(CT_)]
        tp_order += [("prm",), ("ct", 0), ("ct", 1)]
        for j in range(2 * TT):
            pj_order += [("qkv", j)]
            if j >= 2:
                tp_order += [("qkt", j - 2)]
        tp_order += [("qkt", j) for j in range(2 * TT - 2, 2 * TT)]
        for i in range(2 * DC + 1):
            if i < 2 * DC:
                pj_order += [("gate", i)]
            if i % 4 == 0 and i < 2 * DC:
                tp_order += [("w", i // 4, 0), ("w", i // 4, 1)]
            if i % 4 == 2:
                tp_order += [("k", i // 4)]
            if i % 2 == 1:
                tp_order += [("pt", i // 2, f) for f in range(2 if i // 2 >= KVH else 1)]
            if i % 2 == 0 and i >= 2:
                pj_order += [("av", i // 2 - 1)]
        n_pj, n_tp = len(pj_order), len(tp_order)

        def uses(order, key):
            n = order.index(key)
            return n, n % 2, n // 2

        KV0 = SSM_W + AW
        G0 = KV0 + 2 * KW
        pieces = [("in", 0), ("in", 256), ("in", KV0), ("in", SSM_W), ("in", SSM_W + 256)] + \
                 [("in", G0 + 256 * i) for i in range(DC)] + [("merge", P * m) for m in range(DC)] + \
                 [("out", 256 * i) for i in range(D // 256)]
        NP = len(pieces)
        P_U, P_QKV, P_G, P_M, P_OUT = 0, 2, 5, 5 + DC, 5 + 2 * DC
        NOUT = NP - P_OUT
        SPLITS = {0: P_QKV + 2, TT + 1: P_G}
        on_pool = [n for n in range(NP) if n == 0 or P_G < n < P_M]
        on_dve = [n for n in range(NP) if n not in on_pool]

        def split_place(n):
            if P_QKV < n < P_G:
                return 4 + n - P_QKV - 1
            return n % 2 if n < P_OUT + 2 else 2 + n % 2

        ring = [part(name, o, SLOT) for name, o in (places[split_place(P_OUT + e)] for e in range(4))]
        up_low = [rounded(f"up_low{e}", *places[split_place(P_OUT + e)], [P, SLOT]) for e in range(4)]

        def piece_size(n):
            return 3 * 512 if pieces[n][0] == "merge" else PIECE

        def piece_used(eng, n):
            if n < P_QKV:
                eng.wait_ge(pj_full, pj_order.index(("u", 2 * n + 1)) + 1)
            elif n < P_G:
                eng.wait_ge(pj_full, pj_order.index(("qkv", TT - 1 if n == P_QKV else 2 * TT - 1)) + 1)
            elif n < P_M:
                eng.wait_ge(pj_full, pj_order.index(("gate", 2 * (n - P_G) + 1)) + 1)
            elif n < P_OUT:
                eng.wait_ge(mg_full, 3 * (n - P_M + 1))
            else:
                eng.wait_ge(pj_full, n_pj + NOUT * (TT - 1) + (n - P_OUT) // 2 * 2 + 2)

        def low_ready(eng, n):
            if n in on_pool:
                eng.wait_ge(low_done_p, on_pool.index(n) + 1)
            else:
                eng.wait_ge(low_done_v, on_dve.index(n) + 1)

        def piece_loads(n):
            return sum(16 * (3 if pieces[j][0] == "merge" else 1) for j in range(n % 2, n + 1, 2))

        def split_high(n):
            nc.scalar.wait_ge(raw_loaded[n % 2], piece_loads(n))
            if n >= P_OUT + 2:
                piece_used(nc.scalar, P_OUT - 1)
            elif P_QKV < n < P_G:
                nc.scalar.wait_ge(tp_full, tp_order.index(("ct", 1)) + 1)
            elif n >= 2:
                piece_used(nc.scalar, n - 4 if P_G <= n < P_G + 2 else n - 2)
            z = piece_size(n)
            nc.scalar.activation(w_high[split_place(n)][:, 0:z], raw[n % 2][:, 0:z], ACT.Copy).then_inc(high_done, 1)

        def split_low(eng, n):
            eng.wait_ge(high_done, n + 1)
            z = piece_size(n)
            s = split_place(n)
            eng.tensor_tensor(w_low[s][:, 0:z], raw[n % 2][:, 0:z], w_high[s][:, 0:z].bitcast(F32), ALU.subtract
                              ).then_inc(low_done_p if n in on_pool else low_done_v, 1)

        def half(h):
            return slice(h * SLOT // 2, (h + 1) * SLOT // 2)

        def piece_w(n, /, **dims):
            z = piece_size(n)
            pat = "p (%s) -> p %s" % (" ".join(dims), " ".join(dims))
            return [w[split_place(n)][:, 0:z].rearrange(pat, **dims) for w in (w_high, w_low)]

        def zy_parts(dst):
            early = slice(0, SEQ - P)
            return [(dst[:, 0:CT_ - 1, :], zT[:, 0:CT_ - 1, :]), (dst[:, CT_:, early], qT[:, :, early]),
                    (dst[:, CT_:, SEQ - P:], qT[:, :, SEQ - P:]), (dst[:, CT_ - 1, :], zT[:, CT_ - 1, :])]

        def merge_banks(m):
            return [pj[0], sc[0], mb[0]] if m % 2 == 0 else [pj[1], sc[1], mb[1]]

        def merge_tmp(m):
            return part("att", (m % 2) * 1536, 1536, f=3, t=SEQ)

        def bc(v, shape):
            return v.broadcast_to(shape)

        block = ctx.enter_context(nc.Block())

        ctx.enter_context(nc.allow_non_contiguous_dma(reason="small parameters"))

        @block.sync
        def _(sp):
            for t in range(TT):
                sp.dma_start(x_in[:, t, :], x[0, t * P:(t + 1) * P, :]).then_inc(x_loaded[t], 16)

            def load_piece(n):
                kind, c0 = pieces[n]
                if n >= 2:
                    low_ready(sp, n - 2)
                done = raw_loaded[n % 2]
                if kind == "merge":
                    v = raw[n % 2][:, 0:1536].rearrange("p (f k n) -> p f k n", f=3, k=4)
                    for f, w in enumerate((w_glu_gate, w_glu_val, w_attn_up)):
                        sp.dma_start(v[:, f], w[0, :, c0:c0 + P].rearrange("(k p) n -> p k n", p=P)).then_inc(done, 16)
                else:
                    w = w_in if kind == "in" else w_out
                    sp.dma_start(raw[n % 2].rearrange("p (k n) -> p k n", k=DC),
                                 w[0, :, c0:c0 + 256].rearrange("(k p) n -> p k n", p=P)).then_inc(done, 16)

            load_piece(0)
            load_piece(1)
            for f, m in enumerate((b_re, b_im)):
                v = m[0].rearrange("(s g) p h -> g p s h", g=2)
                for gl in range(2):
                    sp.dma_start(b_raw[gl * STATE:(gl + 1) * STATE, f], v[gl]).then_inc(small_loaded, 16)
            for f, m in enumerate((c_re, c_im)):
                sp.dma_start(c_raw[:, f], m[0].rearrange("(c g) h p -> (g h) c p", c=CT_)).then_inc(small_loaded, 16)
            sp.dma_start(d_col[:], d_skip[0].rearrange("(k p) -> p k", p=P)).then_inc(small_loaded, 16)
            for h in range(2):
                sp.dma_start(qg[h * HD:(h + 1) * HD, 0:1], q_norm[0].rearrange("(p o) -> p o", o=1)).then_inc(small_loaded, 16)
                sp.dma_start(qg[h * HD:(h + 1) * HD, 1:2], k_norm[0].rearrange("(p o) -> p o", o=1)).then_inc(small_loaded, 16)
            sp.dma_start(sink[:], sinks[0:1, :].broadcast_to([P, HEADS])).then_inc(small_loaded, 16)
            sp.dma_start(rw[:, :, 0:NG], w_coarse[0].rearrange("(k p) n -> p k n", p=P)).then_inc(small_loaded, 16)
            sp.dma_start(rw[:, :, NG:NG + NE], w_fine[0].rearrange("(k p) n -> p k n", p=P)).then_inc(small_loaded, 16)
            load_piece(2)
            load_piece(3)
            load_piece(4)
            sp.wait_ge(uT_done, CT_)
            for j in range(SUB):
                for q in range(SPC):
                    sp.dma_start(u4[j * TCH:(j + 1) * TCH, q::SPC, :],
                                 uT[q * TCH:(q + 1) * TCH, :, j, :]).then_inc(u4_loaded, 16)
            for n in range(5, NP):
                if n == P_OUT:
                    sp.wait_ge(zy_low, 4)
                    sp.dma_start(ffn_gain, norm_ffn[0:1, :].broadcast_to([P, D])).then_inc(ffn_gain_loaded, 16)
                    sp.dma_start(x2[:, :, :], x[0].rearrange("(t p) d -> p t d", p=P)).then_inc(x_again, 16)
                load_piece(n)
            for e in range(2):
                sp.dma_start(down[e], w_down[0, e].rearrange("(k p) n -> p k n", p=P)).then_inc(down_loaded[e], 16)
            for e in range(4):
                piece_used(sp, P_OUT + e)
                if e == 1:
                    sp.wait_ge(h2_stored[TT - 1], 16)
                if e == 2:
                    sp.wait_ge(gathered[0], 16)
                sp.dma_start(ring[e].rearrange("p (k n) -> p k n", k=DC),
                             w_up[0, e].rearrange("(k p) n -> p k n", p=P)).then_inc(ring_loaded[e], 16)
            with sp.Fori(0, NE // 4 - 1) as i:
                for r in range(4):
                    sp.wait_ge(up_full, i * 4 + (r + 1))
                    sp.dma_start(ring[r].rearrange("p (k n) -> p k n", k=DC),
                                 w_up[0, bass.ds(i * 4 + (r + 4), 1)].rearrange("e (k p) n -> p (e k) n", p=P)
                                 ).then_inc(ring_loaded[r], 16)
                    sp.wait_ge(dn_full, i * 4 + (r + 1))
                    sp.dma_start(down[r % 2], w_down[0, bass.ds(i * 4 + (r + 2), 1)].rearrange("e (k p) n -> p (e k) n", p=P)
                                 ).then_inc(down_loaded[r % 2], 16)
            for e in range(NE - 4, NE - 2):
                sp.wait_ge(dn_full, e + 1)
                sp.dma_start(down[e % 2], w_down[0, e + 2].rearrange("(k p) n -> p k n", p=P)).then_inc(down_loaded[e % 2], 16)
            sp.wait_ge(flag_done, 1)
            over = sp.value_load(flag[0:1, 0:1], min_val=0, max_val=1)
            with sp.If(over > 0):
                with sp.Fori(0, MORE) as j:
                    with sp.Fori(0, NE) as e:
                        sp.wait_ge(o_dn, j * NE + e + 1)
                        sp.dma_start(ring[0].rearrange("p (k n) -> p k n", k=DC),
                                     w_up[0, bass.ds(e, 1)].rearrange("e (k p) n -> p (e k) n", p=P)).then_inc(o_w, 16)
                        sp.dma_start(down[0], w_down[0, bass.ds(e, 1)].rearrange("e (k p) n -> p (e k) n", p=P)).then_inc(o_w, 16)
            for t in range(TT):
                sp.wait_ge(sum_done, t + 1)
                sp.dma_start(out[0, t * P:(t + 1) * P, :], x2[:, t, :]).then_inc(out_stored, 16)
            sp.wait_ge(out_stored, 16 * TT)
            for b in range(2):
                sp.wait_ge(y_stored[b], 8 * NE)
            for t in range(TT):
                sp.wait_ge(h2_stored[t], 16)

        @block.gpsimd
        def _(g):
            n_pool = [0]

            def link(ins):
                n_pool[0] += 1
                ins.then_inc(pool_chain, 1)
                g.wait_ge(pool_chain, n_pool[0])

            g.memset(half_col[:], -0.5).then_inc(const_ready, 1)
            g.memset(halfpi[:], math.pi / 2).then_inc(const_ready, 1)
            link(g.memset(ident[:], 0.0))
            g.affine_select(out=ident[:], in_=ident[:], compare_op=ALU.not_equal, fill=1.0, base=0,
                            pattern=[[-1, P]], channel_multiplier=1).then_inc(const_ready, 1)
            g.iota(par_i[:], pattern=[[0, 1]], base=0, channel_multiplier=1).then_inc(const_ready, 1)

            g.wait_ge(const_ready, 1)

            def inverse_root(dst, src, width, ready, n, done):
                g.wait_ge(ready, n)
                g.tensor_tensor(dst, src, half_col[:, 0:width], ALU.pow).then_inc(done, 1)

            for t in range(TT):
                inverse_root(rstd[:, t:t + 1], ssq[:, t:t + 1], 1, var_done, t + 1, rstd_done)
            split_low(g, 0)
            link(g.memset(ones[:], 1.0))
            g.affine_select(out=before[:], in_=ones[:], compare_op=ALU.is_gt, fill=0.0, base=0,
                            pattern=[[1, P]], channel_multiplier=-1).then_inc(const_ready, 1)
            g.iota(slot_no[:], pattern=[[1, CAP]], base=0, channel_multiplier=0,
                   allow_small_or_imprecise_dtypes=True).then_inc(const_ready, 1)
            g.iota(tok_id[:], pattern=[[P, TT]], base=0, channel_multiplier=1,
                   allow_small_or_imprecise_dtypes=True).then_inc(const_ready, 1)
            g.iota(e_no[:], pattern=[[1, NE]], base=0, channel_multiplier=0,
                   allow_small_or_imprecise_dtypes=True).then_inc(const_ready, 1)
            g.iota(e_rev[:], pattern=[[-1, NE]], base=NE, channel_multiplier=0,
                   allow_small_or_imprecise_dtypes=True).then_inc(const_ready, 1)
            link(g.iota(neg_dist[:], pattern=[[1, 2 * P]], base=-P, channel_multiplier=-1,
                        allow_small_or_imprecise_dtypes=True))
            link(g.affine_select(out=neg_dist[:], in_=neg_dist[:], compare_op=ALU.is_ge, fill=-HIDE, base=P,
                                 pattern=[[-1, 2 * P]], channel_multiplier=1))
            g.affine_select(out=neg_dist[:], in_=neg_dist[:], compare_op=ALU.is_ge, fill=-HIDE, base=-1,
                            pattern=[[1, 2 * P]], channel_multiplier=-1).then_inc(const_ready, 1)
            def rotations(c):
                s0 = slice(c * SPC, (c + 1) * SPC)
                if c:
                    g.wait_ge(S_done, c)
                g.memset(Ec[:, :, 0:1], 1.0)
                link(g.memset(Es[:, :, 0:1], 0.0))
                g.tensor_copy(Ec[:, :, 1:2], e1[:, 0, 2, s0].rearrange("p (s o) -> p s o", o=1))
                link(g.tensor_copy(Es[:, :, 1:2], e1[:, 1, 2, s0].rearrange("p (s o) -> p s o", o=1)))
                m = 1
                while m < CH // 2:
                    er, ei = Ec[:, :, m:m + 1], Es[:, :, m:m + 1]
                    tq = et[:, :, :, 0:1]
                    g.tensor_tensor(tq[:, 0], er, er, ALU.mult)
                    g.tensor_tensor(tq[:, 1], ei, ei, ALU.mult)
                    link(g.tensor_tensor(tq[:, 2], er, ei, ALU.mult))
                    g.tensor_tensor(Ec[:, :, 2 * m:2 * m + 1], tq[:, 0], tq[:, 1], ALU.subtract)
                    link(g.tensor_tensor(Es[:, :, 2 * m:2 * m + 1], tq[:, 2], tq[:, 2], ALU.add))
                    m *= 2
                    w = m - 1
                    er, ei = (bc(v[:, :, m:m + 1], [P, SPC, w]) for v in (Ec, Es))
                    ar, ai = Ec[:, :, 1:m], Es[:, :, 1:m]
                    tq = et[:, :, :, 0:w]
                    g.tensor_tensor(tq[:, 0], ar, er, ALU.mult)
                    g.tensor_tensor(tq[:, 1], ai, ei, ALU.mult)
                    g.tensor_tensor(tq[:, 2], ar, ei, ALU.mult)
                    link(g.tensor_tensor(tq[:, 3], ai, er, ALU.mult))
                    g.tensor_tensor(Ec[:, :, m + 1:2 * m], tq[:, 0], tq[:, 1], ALU.subtract)
                    link(g.tensor_tensor(Es[:, :, m + 1:2 * m], tq[:, 2], tq[:, 3], ALU.add))
                g.sem_inc(e_done, 1)

            g.wait_ge(rot_done, 1)
            rotations(0)
            for j in range(2 * TT):
                H = KVH if j < TT else HEADS
                inverse_root(qrs[:, j, 0:H], qss[:, j, 0:H], H, qk_var, j + 1, qk_rstd)
            split_low(g, P_G + 1)
            for c in range(1, CT_):
                split_low(g, P_G + 2 * c)
                rotations(c)
                split_low(g, P_G + 2 * c + 1)

            for t in range(TT):
                inverse_root(rstd[:, TT + t:TT + t + 1], ssq[:, TT + t:TT + t + 1], 1, var_done, TT + t + 1, rstd_done)

            def gather(e2, e, n_free):
                if n_free is not None:
                    g.wait_ge(xt_full, n_free)
                g.tensor_copy(idx[:, e2:e2 + 1], idx_all[:, bass.ds(e, 1)]).then_inc(idx_taken, 1)
                g.wait_ge(idx_taken, e + 1)
                g.sem_inc(gather_turn, 1)
                g.indirect_dma_start(xg[e2], None, h2_rows,
                                     bass.IndirectOffsetOnAxis(idx[:, e2:e2 + 1], 0)).then_inc(gathered[e2], 16)

            for h in range(2):
                g.wait_ge(up_high_done, h + 1)
                g.tensor_tensor(up_low[0][:, half(h)], ring[0][:, half(h)], up_high[0][:, half(h)].bitcast(F32), ALU.subtract
                                ).then_inc(first_low_done, 1)

            def low_down(e2, e):
                g.wait_ge(down_high_done, e + 1)
                g.tensor_tensor(down_low[e2][:], down[e2].rearrange("p k n -> p (k n)"), down_high[e2][:].bitcast(F32), ALU.subtract
                                ).then_inc(down_low_done, 1)

            for t in range(TT):
                g.wait_ge(h2_stored[t], 16)
            g.wait_ge(idx_done, 1)
            gather(0, 0, None)
            gather(1, 1, None)
            g.wait_ge(idx_done, 2)
            gather(0, 2, 2)
            gather(1, 3, 4)
            low_down(0, 0)
            for e in range(4, NE // 2):
                gather(e % 2, e, 2 * (e - 1))
                low_down((e - 3) % 2, e - 3)
            g.wait_ge(idx_done, 3)
            with g.Fori(0, NE // 4) as i:
                for r in range(2):
                    gather(r, i * 2 + (r + 8), i * 4 + 2 * (r + 7))
                    low_down(1 - r, i * 2 + (r + 5))
            for e in range(NE - 3, NE):
                low_down(e % 2, e)
            def rows_of_tokens(rows, k):
                for t in range(TT):
                    g.indirect_dma_start(gath[2 * t + k], None, rows,
                                         bass.IndirectOffsetOnAxis(dest[:, k, t:t + 1], 0)).then_inc(rows_back[k][t], 16)

            g.wait_ge(flag_done, 1)
            over = g.value_load(flag[0:1, 0:1], min_val=0, max_val=1)
            with g.If(over > 0):
                with g.Fori(0, MORE * NE) as b:
                    g.wait_ge(o_idx, b + 1)
                    g.sem_inc(gather_turn, 1)
                    g.indirect_dma_start(xg[0], None, h2_rows,
                                         bass.IndirectOffsetOnAxis(idx[:, 0:1], 0)).then_inc(o_gath, 16)
                g.wait_ge(o_st, 16 * MORE * NE)
                for b in range(2):
                    g.wait_ge(y_stored[b], 8 * NE)
                g.dma_start(y_all[0:NE * CAP, :], y_rows).then_inc(o_copy, 16)
                g.wait_ge(o_copy, 16)
                for k in range(2):
                    rows_of_tokens(y_all, k)
            with g.If(over < 1):
                g.wait_ge(up_full, NE)
                g.wait_ge(y_stored[0], 8 * NE)
                g.wait_ge(y_stored[1], 8 * NE - 16)
                rows_of_tokens(y_rows[0:(NE - 1) * CAP, :], 0)
                g.wait_ge(y_stored[1], 8 * NE)
                rows_of_tokens(y_rows, 1)

        @block.scalar
        def _(act):
            act.dma_start(R(0), lam_re[0].rearrange("(s g) p -> s (g p)", g=2)).then_inc(rows_loaded, 16)
            act.dma_start(R(1), lam_im[0].rearrange("(s g) p -> s (g p)", g=2)).then_inc(rows_loaded, 16)
            act.dma_start(ldt[:, 0, :], log_dt[0].rearrange("(s g) -> s g", g=2)).then_inc(rows_loaded, 16)
            act.dma_start(mix_gain, norm_mix[0:1, :].broadcast_to([P, D])).then_inc(mix_gain_loaded, 16)
            act.wait_ge(rows_loaded, 16 * 3)
            act.activation(ldt[:, 1, :], ldt[:, 0, :], ACT.Exp).then_inc(prm_act, 1)
            act.wait_ge(prm_dve, 1)
            act.activation(R(5), R(2), ACT.Exp).then_inc(prm_act, 1)
            act.activation(R(6), R(2), ACT.Exp, scale=float(SUB)).then_inc(prm_act, 1)
            for t in range(TT):
                act.wait_ge(x_loaded[t], 16)
                act.activation(xn[:, t, :], x_in[:, t, :], ACT.Square, accum_out=ssq[:, t:t + 1]).then_inc(sq_done, 1)
            act.wait_ge(prm_dve, 2)
            act.wait_ge(const_ready, 2)
            act.activation(R(7), R(4), ACT.Sin).then_inc(prm_act, 1)
            act.activation(R(8), R(9), ACT.Sin, scale=-1.0, bias=halfpi[0:ST, :]).then_inc(prm_act, 1)
            for n in range(2 * TT):
                t, f = n // 2, n % 2
                m, b, _ = uses(tp_order, ("h", t, f))
                act.wait_ge(tp_full, m + 1)
                act.activation(h_high[:, 4 * f:4 * f + 4, t * P:(t + 1) * P], tp[b][:].rearrange("p (k n) -> p k n", k=4),
                               ACT.Copy).then_inc(h_high_done, 1)
                if n == 1:
                    split_high(0)
            split_high(1)
            for c in range(CT_):
                n, b, _ = uses(pj_order, ("u", c))
                act.wait_ge(pj_full, n + 1)
                act.activation(uT[:, c].rearrange("p j n -> p n j"), pj[b][:].rearrange("p (n j) -> p n j", j=SUB),
                               ACT.Copy).then_inc(pj_free[b], 1)
                act.wait_ge(pj_free[b], uses(pj_order, ("u", c))[2] + 1)
                act.sem_inc(uT_done, 1)
                if c == 2:
                    split_high(2)
            split_high(P_QKV + 1)
            for j in range(2 * TT):
                n, b, _ = uses(pj_order, ("qkv", j))
                W = KW if j < TT else AW
                act.wait_ge(pj_full, n + 1)
                if j >= 2:
                    act.wait_ge(qk_norm, j - 1)
                act.activation(qk_sq[j % 2][:, 0:W // HD, :], pj[b][:, 0:W], ACT.Square).then_inc(qk_evac, 1)
                if j < TT:
                    act.activation(v_tok[:, j, :], pj[b][:, KW:2 * KW], ACT.Copy).then_inc(v_done, 1)
                act.activation(qk_raw[j % 2][:, 0:W // HD, :], pj[b][:, 0:W], ACT.Copy).then_inc(pj_free[b], 1)
                if j in SPLITS:
                    split_high(SPLITS[j])
            def high_zy(n, ready, count):
                act.wait_ge(ready, count)
                dst, src = zy_parts(h_high)[n]
                act.activation(dst, src, ACT.Copy).then_inc(zy_high, 1)

            for i in range(2 * DC + 1):
                if i < 2 * DC:
                    n, b, used = uses(pj_order, ("gate", i))
                    act.wait_ge(pj_full, n + 1)
                    dst = ts_gate[:, i, :] if i < DC else ta_gate[:, i - DC, :]
                    act.activation(dst, pj[b][:], ACT.Tanh, scale=0.5).then_inc(pj_free[b], 1)
                    if i % 2 == 0:
                        split_high(P_G + 1 + i // 2)
                    act.wait_ge(pj_free[b], used + 1)
                    act.sem_inc(gates_done, 1)
                    if i == 2 * DC - 1:
                        high_zy(0, z_done, CT_ - 1)
                if i % 4 == 0 and i < 2 * DC:
                    c = i // 4
                    if c:
                        act.wait_ge(bu_full, c)
                    for f in range(2):
                        n, b, _ = uses(tp_order, ("w", c, f))
                        act.wait_ge(tp_full, n + 1)
                        act.activation(w1T[:, f], tp[b][:], ACT.Copy).then_inc(tp_free[b], 1)
                        act.wait_ge(tp_free[b], uses(tp_order, ("w", c, f))[2] + 1)
                        act.sem_inc(w1T_done, 1)
                if i % 4 == 2:
                    c = i // 4
                    n, b, _ = uses(tp_order, ("k", c))
                    act.wait_ge(tp_full, n + 1)
                    if c:
                        act.wait_ge(y_full, c)
                    act.wait_ge(bbd_done, 1)
                    kps = tp[b][0:TCH, :].rearrange("p (q n) -> p q n", q=SPC)
                    for j in range(SUB):
                        ins = act.activation(toep[j * TCH:(j + 1) * TCH, :, j * TCH:], kps[:, :, 0:(SUB - j) * TCH], ACT.Copy)
                        ins.then_inc(toep_done if j < SUB - 1 else tp_free[b], 1)
                    act.wait_ge(tp_free[b], uses(tp_order, ("k", c))[2] + 1)
                    act.sem_inc(toep_done, 1)
                if i % 2 == 0 and i >= 2:
                    a = i // 2 - 1
                    n, b, _ = uses(pj_order, ("av", a))
                    act.wait_ge(pj_full, n + 1)
                    blk, kv = a // KVH, a % KVH
                    act.activation(qT[:, 2 * kv:2 * kv + 2, blk * P:(blk + 1) * P],
                                   pj[b][:, 0:2 * P].rearrange("p (h q) -> p h q", h=2), ACT.Copy).then_inc(pj_free[b], 1)
                    act.wait_ge(pj_free[b], uses(pj_order, ("av", a))[2] + 1)
                    act.sem_inc(av_done, 1)
                    if a == NQ - 1:
                        high_zy(2, av_done, NQ)
                if i % 2 == 0 and i < 2 * DC:
                    a = i // 2
                    W = 2 * P if a >= KVH else P
                    act.wait_ge(m_ready, 2 * (a + 1))
                    for h in range(QPK):
                        act.activation(probs[a % 2][:, h, 0:W], probs[a % 2][:, h, 0:W], ACT.Exp,
                                       bias=smx[:, a % 2, 1, h:h + 1],
                                       accum_out=smx[:, a % 2, 4, h:h + 1]).then_inc(exp_done, 1)
                    act.activation(smx[:, a % 2, 3, :], smx[:, a % 2, 2, :], ACT.Exp).then_inc(exp_done, 1)
                if i % 2 == 0 and i < 2 * DC:
                    a = i // 2
                    W = 2 * P if a >= KVH else P
                    act.wait_ge(sum_ready, a + 1)
                    for h in range(QPK):
                        act.activation(probs[a % 2][:, h, 0:W], probs[a % 2][:, h, 0:W], ACT.Copy,
                                       scale=smx[:, a % 2, 5, h:h + 1]).then_inc(p_done, 1)
                if i % 4 == 0 and i >= 4:
                    c = i // 4 - 1
                    act.wait_ge(yv_done, c + 1)
                    act.activation(tb[2], tb[1], ACT.Square).then_inc(z_sq, 1)
                    act.wait_ge(z_arg, c + 1)
                    act.activation(tb[2], tb[2], ACT.Tanh, scale=GELU_IN).then_inc(z_th, 1)
                if i % 2 == 1:
                    a = i // 2
                    if a:
                        act.wait_ge(pj_full, uses(pj_order, ("av", a - 1))[0] + 1)
                    for f in range(2 if a >= KVH else 1):
                        n, b, _ = uses(tp_order, ("pt", a, f))
                        act.wait_ge(tp_full, n + 1)
                        act.activation(pT[:, f], tp[b][:], ACT.Copy).then_inc(tp_free[b], 1)
                        act.wait_ge(tp_free[b], uses(tp_order, ("pt", a, f))[2] + 1)
                        act.sem_inc(pT_done, 1)
                if i % 4 == 3:
                    c = i // 4
                    act.wait_ge(y_full, c + 1)
                    act.activation(tb[0], mb[0][:], ACT.Copy).then_inc(y_evac, 1)
                    if c == CT_ - 1:
                        high_zy(1, av_done, NQ - KVH)
            high_zy(3, z_done, CT_)

            def merged_high(m):
                act.wait_ge(merged_done, m + 1)
                act.activation(m_high[:, m, :], merge_tmp(m)[:, 1, :], ACT.Copy).then_inc(m_high_done, 1)

            for m in range(DC):
                split_high(P_M + m + 1)
                act.wait_ge(mg_full, 3 * m + 2)
                if m >= 2:
                    act.wait_ge(mg_free, m - 1)
                act.activation(merge_tmp(m)[:, 0, :], merge_banks(m)[0][:], ACT.Tanh, scale=0.25).then_inc(mg_act, 1)
                if m:
                    merged_high(m - 1)
            merged_high(DC - 1)
            for n in range(P_OUT + 1, NP):
                split_high(n)
            for t in range(TT):
                act.wait_ge(x2_done, NOUT * (t + 1))
                act.activation(part("att", t % 2 * D, D), x2[:, t, :], ACT.Square, accum_out=ssq[:, TT + t:TT + t + 1]).then_inc(sq_done, 1)
                if t >= 2:
                    act.wait_ge(h2_stored[t - 2], 16)
                act.wait_ge(n2_done, t + 1)
                act.wait_ge(rstd_done, TT + t + 1)
                act.activation(h2[t % 2], xg[t % 2], ACT.Copy, scale=rstd[:, TT + t:TT + t + 1]).then_inc(h2_scaled, 1)
                act.wait_ge(h2_scaled, t + 1)
                act.dma_start(h2_rows[t * P:(t + 1) * P, :], h2[t % 2]).then_inc(h2_stored[t], 16)

            def high_up(e4, e, rnd, h):
                if h == 0:
                    act.wait_ge(ring_loaded[e4], rnd * 16 + 16)
                    if not (isinstance(e, int) and e < 2):
                        act.wait_ge(up_full, e - 1)
                act.activation(up_high[e4 % 2][:, half(h)], ring[e4][:, half(h)], ACT.Copy).then_inc(up_high_done, 1)

            def high_down(e4, e, rnd):
                act.wait_ge(down_loaded[e4 % 2], rnd * 32 + (e4 // 2 * 16 + 16))
                if not (isinstance(e, int) and e < 2):
                    act.wait_ge(dn_full, e - 1)
                act.activation(down_high[e4 % 2][:], down[e4 % 2].rearrange("p k n -> p (k n)"), ACT.Copy).then_inc(down_high_done, 1)

            def high_rows(e4, e):
                for f in range(2):
                    act.wait_ge(xt_full, e * 2 + (f + 1))
                    act.activation(xt_high[e4 % 2][:, 4 * f:4 * f + 4, :], tp[f][:].rearrange("p (k n) -> p k n", k=4),
                                   ACT.Copy).then_inc(xt_high_done, 1)

            def high_act(e4, e):
                act.wait_ge(at_full, e + 1)
                act.activation(at_high[e4 % 2][:], sc[1][:, 0:2 * P].rearrange("p (k n) -> p k n", k=2), ACT.Copy).then_inc(at_high_done, 1)

            def rows_out(e4, e, n_store):
                b = e4 % 2
                if n_store is not None:
                    act.wait_ge(y_stored[b], n_store)
                act.wait_ge(dn_full, e + 1)
                for h in range(2):
                    act.activation(y_out[b][:, h * 512:(h + 1) * 512], mb[h][:], ACT.Copy,
                                   scale=gate_all[:, bass.ds(e, 1)]).then_inc(y_scaled, 1)
                act.wait_ge(y_scaled, (e + 1) * 2)
                act.dma_start(y_rows[bass.ds(e * CAP, CAP), :], y_out[b]).then_inc(y_stored[b], 16)

            def step(r, e, rnd, before=True, two_before=True, last=False):
                n4, nrnd = (r + 1) % 4, (rnd if r < 3 else rnd + 1)
                if not last:
                    high_up(n4, e + 1, nrnd, 0)
                if two_before:
                    n_store = None if isinstance(e, int) and e < 4 else rnd * 32 + (r // 2 * 16 - 16)
                    rows_out((r + 2) % 4, e - 2, n_store)
                if not last:
                    high_up(n4, e + 1, nrnd, 1)
                act.wait_ge(up_full, e + 1)
                act.activation(th_e[r % 2], pj[r % 2][:, 0:DE], ACT.Tanh, scale=0.5).then_inc(th_done, 1)
                if before:
                    high_act((r + 3) % 4, e - 1)
                if not last:
                    high_rows(n4, e + 1)
                high_down(r, e, rnd)

            high_up(0, 0, 0, 0)
            high_up(0, 0, 0, 1)
            act.wait_ge(r_dve, 1)
            act.activation(rt[:, 0, :, 0:NG], rt[:, 0, :, 0:NG], ACT.Exp).then_inc(r_act, 1)
            act.wait_ge(r_dve, 2)
            act.activation(rs_[:, 6, :], rs_[:, 6, :], ACT.Exp).then_inc(r_act, 1)
            high_rows(0, 0)
            for e in range(4):
                step(e, e, 0, before=e >= 1, two_before=e >= 2)
            with act.Fori(0, NE // 4 - 2) as i:
                for r in range(4):
                    step(r, i * 4 + (r + 4), i + 1)
            for e in range(NE - 4, NE):
                step(e % 4, e, e // 4, last=e == NE - 1)
            rows_out(2, NE - 2, 8 * NE - 16)
            high_act(3, NE - 1)
            rows_out(3, NE - 1, 8 * NE - 16)
            act.wait_ge(flag_done, 1)
            over = act.value_load(flag[0:1, 0:1], min_val=0, max_val=1)
            with act.If(over > 0):
                for b in range(2):
                    act.wait_ge(y_stored[b], 8 * NE)
                with act.Fori(0, MORE) as j:
                    with act.Fori(0, NE) as e:
                        act.wait_ge(o_up, j * NE + e + 1)
                        act.activation(th_e[0], pj[0][:, 0:DE], ACT.Tanh, scale=0.5).then_inc(o_th, 1)
                        act.wait_ge(o_at, j * NE + e + 1)
                        act.activation(actT, sc[1][:, 0:2 * P].rearrange("p (k n) -> p k n", k=2), ACT.Copy).then_inc(o_atd, 1)
                        act.wait_ge(o_dn, j * NE + e + 2)
                        for h in range(2):
                            act.activation(y_out[0][:, h * 512:(h + 1) * 512], mb[h][:], ACT.Copy,
                                           scale=gate[:, 0:1]).then_inc(o_y, 1)
                        act.wait_ge(o_y, (j * NE + e + 1) * 2)
                        act.dma_start(y_all[bass.ds((j + 1) * (NE * CAP) + e * CAP, CAP), :], y_out[0]).then_inc(o_st, 16)
                        act.wait_ge(o_st, (j * NE + e + 1) * 16)

        @block.vector
        def _(v):
            n_dve = [0]

            def mark(ins):
                n_dve[0] += 1
                ins.then_inc(dve_chain, 1)

            def settle():
                v.wait_ge(dve_chain, n_dve[0])

            def link(ins):
                mark(ins)
                settle()

            tt, ts, stt = v.tensor_tensor, v.tensor_scalar, v.scalar_tensor_tensor

            def scale_tile(t):
                v.wait_ge(rstd_done, t + 1)
                stt(xn[:, t, :], x_in[:, t, :], rstd[:, t:t + 1], mix_gain, ALU.mult, ALU.mult).then_inc(xn_done, 1)

            def norm2(t):
                if t == 0:
                    v.wait_ge(ffn_gain_loaded, 16)
                    for n in range(NP - 2, NP):
                        low_ready(v, n)
                if t >= 2:
                    v.wait_ge(h2_scaled, t - 1)
                    v.wait_ge(tp_full, n_tp + 2 * (t - 1))
                v.wait_ge(x2_done, NOUT * (t + 1))
                tt(xg[t % 2], x2[:, t, :], ffn_gain, ALU.mult).then_inc(n2_done, 1)
                v.wait_ge(sq_done, TT + t + 1)
                mean_var(ssq[:, TT + t:TT + t + 1], D)

            def norm2_turned(t):
                if t >= 2:
                    v.wait_ge(lg_full, t - 1)
                for f in range(2):
                    v.wait_ge(tp_full, n_tp + 2 * t + f + 1)
                    v.tensor_copy(xgT[t % 2][:, 4 * f:4 * f + 4, :], tp[f][:].rearrange("p (k n) -> p k n", k=4)
                                  ).then_inc(h2T_done, 1)

            def mean_var(dst, n):
                ts(dst, dst, 1.0 / n, EPS, ALU.mult, ALU.add).then_inc(var_done, 1)

            v.wait_ge(rows_loaded, 16 * 3)
            v.wait_ge(prm_act, 1)
            dt_bc = bc(ldt[:, 1, :].rearrange("s (g o) -> s g o", o=1), [ST, 2, STATE])
            g2 = lambda i: R(i).rearrange("s (g p) -> s g p", g=2)
            tt(g2(2), g2(0), dt_bc, ALU.mult).then_inc(prm_dve, 1)
            link(tt(g2(3), g2(1), dt_bc, ALU.mult))
            link(ts(R(10), R(3), 1.0 / (2 * math.pi), MAGIC, ALU.mult, ALU.add))
            link(ts(R(10), R(10), MAGIC, None, ALU.subtract))
            link(stt(R(4), R(10), -TWO_PI_HIGH, R(3), ALU.mult, ALU.add))
            link(stt(R(4), R(10), -TWO_PI_LOW, R(4), ALU.mult, ALU.add))
            link(ts(R(4), R(4), 3.1415925, -3.1415925, ALU.min, ALU.max))
            link(ts(R(9), R(4), -1.0, None, ALU.mult))
            tt(R(9), R(9), R(4), ALU.max).then_inc(prm_dve, 1)
            def turned_low(n):
                t, f = n // 2, n % 2
                _, b, _ = uses(tp_order, ("h", t, f))
                v.wait_ge(h_high_done, n + 1)
                hs = (slice(None), slice(4 * f, 4 * f + 4), slice(t * P, (t + 1) * P))
                tt(h_low[hs], tp[b][:].rearrange("p (k n) -> p k n", k=4), h_high[hs].bitcast(F32), ALU.subtract
                   ).then_inc(tp_free[b], 1)

            v.wait_ge(mix_gain_loaded, 16)
            for t in range(TT + 2):
                if t < TT:
                    v.wait_ge(sq_done, t + 1)
                    mean_var(ssq[:, t:t + 1], D)
                if 1 <= t <= TT:
                    scale_tile(t - 1)
                if t >= 2:
                    turned_low(2 * t - 4)
                    turned_low(2 * t - 3)
            mark(tt(R(11), R(0), R(0), ALU.mult))
            link(tt(R(12), R(1), R(1), ALU.mult))
            link(tt(R(11), R(11), R(12), ALU.add))
            link(v.reciprocal(R(12), R(11)))
            v.wait_ge(prm_act, 5)
            mark(tt(R(13), R(5), R(8), ALU.mult))
            mark(tt(R(14), R(5), R(7), ALU.mult))
            settle()
            link(ts(R(17), R(13), 1.0, None, ALU.subtract))
            mark(tt(R(18), R(17), R(0), ALU.mult))
            mark(tt(R(19), R(14), R(1), ALU.mult))
            mark(tt(R(20), R(14), R(0), ALU.mult))
            mark(tt(R(21), R(17), R(1), ALU.mult))
            settle()
            mark(tt(R(18), R(18), R(19), ALU.add))
            mark(tt(R(20), R(20), R(21), ALU.subtract))
            settle()
            mark(tt(R(15), R(18), R(12), ALU.mult))
            link(tt(R(16), R(20), R(12), ALU.mult))
            v.sem_inc(rows_done, 1)
            split_low(v, 1)
            v.wait_ge(const_ready, 4)
            v.wait_ge(small_loaded, 16 * 14)
            link(ts(par_i[:], par_i[:], GCH, None, ALU.bitwise_and))
            link(ts(par[:, 0:1], par_i[:], 0.0, None, ALU.is_gt))
            link(ts(par[:, 1:2], par[:, 0:1], -1.0, 1.0, ALU.mult, ALU.add))
            for f in range(2):
                for gl in range(2):
                    mark(ts(c_exp[:, f, :, gl, :], c_raw[:, f], par[:, 1 - gl:2 - gl], (1.0, -1.0)[f], ALU.mult, ALU.mult))
            settle()
            v.sem_inc(cexp_done, 1)
            n, b, used = uses(tp_order, ("prm",))
            v.wait_ge(tp_full, n + 1)
            v.tensor_copy(prm[:], tp[b][:, 0:7 * ST].rearrange("p (f s) -> p f s", f=7)).then_inc(tp_free[b], 1)
            v.wait_ge(tp_free[b], used + 1)
            pr, pi = (lambda j: pw[:, 0, j, :]), (lambda j: pw[:, 1, j, :])
            mark(v.memset(pr(0), 1.0))
            mark(v.memset(pi(0), 0.0))
            mark(v.tensor_copy(pw[:, :, 1, :], prm[:, 0:2, :]))
            mark(v.tensor_copy(e1[:, :, 0, :], prm[:, 5:7, :]))
            settle()

            def cmul(dst, a, b_, tmp):
                mark(tt(tmp(0), a[0], b_[0], ALU.mult))
                mark(tt(tmp(1), a[1], b_[1], ALU.mult))
                mark(tt(tmp(2), a[0], b_[1], ALU.mult))
                mark(tt(tmp(3), a[1], b_[0], ALU.mult))
                settle()
                mark(tt(dst[0], tmp(0), tmp(1), ALU.subtract))
                mark(tt(dst[1], tmp(2), tmp(3), ALU.add))
                settle()

            pwj = lambda j: (pr(j), pi(j))
            ej = lambda j: (e1[:, 0, j, :], e1[:, 1, j, :])
            stmp = lambda i: sc_t[:, i, :]
            cmul(ej(1), ej(0), ej(0), stmp)
            cmul(ej(2), ej(1), ej(1), stmp)
            v.sem_inc(rot_done, 1)
            cmul(pwj(2), pwj(1), pwj(1), stmp)
            cmul(pwj(3), pwj(2), pwj(1), stmp)
            cmul(pwj(4), pwj(2), pwj(2), stmp)
            for i in range(SUB - 1):
                mark(v.tensor_copy(pw_down[:, :, i, :], pw[:, :, SUB - 1 - i, :]))
            mark(v.memset(Bre, 0.0))
            mark(v.memset(Bim, 0.0))
            mark(v.memset(toep, 0.0))
            coef = [bc(prm[:, 2 + i, :].rearrange("p (s o) -> p s o", o=1), [P, ST, GCH]) for i in range(2)]
            bt = [tb[i][:, :, :].rearrange("p q n -> p (q n)")[:, 0:ST * GCH].rearrange("p (s h) -> p s h", s=ST) for i in range(4)]
            mark(tt(bt[0], b_raw[:, 0], coef[0], ALU.mult))
            mark(tt(bt[1], b_raw[:, 1], coef[1], ALU.mult))
            mark(tt(bt[2], b_raw[:, 0], coef[1], ALU.mult))
            mark(tt(bt[3], b_raw[:, 1], coef[0], ALU.mult))
            settle()
            mark(v.memset(Sre[:, :, 0:1], 0.0))
            mark(v.memset(Sim[:, :, 0:1], 0.0))
            v.sem_inc(bbd_done, 1)
            for gl in range(2):
                ps = slice(gl * STATE, (gl + 1) * STATE)
                cs = slice(gl * GCH, (gl + 1) * GCH)
                mark(tt(Bre[ps, :, cs], bt[0][ps], bt[1][ps], ALU.subtract))
                mark(tt(Bim[ps, :, cs], bt[2][ps], bt[3][ps], ALU.add))
            settle()
            split_low(v, 2)
            for f, dst in enumerate((Cre, Cim)):
                n, b, used = uses(tp_order, ("ct", f))
                v.wait_ge(tp_full, n + 1)
                v.tensor_copy(dst, tp[b][:].rearrange("p (s c) -> p s c", c=TCH)).then_inc(tp_free[b], 1)
                v.wait_ge(tp_free[b], used + 1)
            mark(ts(qg[:, 2:3], qg[:, 0:1], qg[:, 1:2], HD ** -0.5, ALU.mult, ALU.mult))
            settle()

            def qk_variance(j):
                H = KVH if j < TT else HEADS
                v.wait_ge(qk_evac, j + 1)
                link(v.tensor_reduce(qss[:, j, 0:H], qk_sq[j % 2][:, 0:H, :], AX_X, ALU.add))
                ts(qss[:, j, 0:H], qss[:, j, 0:H], 1.0 / HD, EPS, ALU.mult, ALU.add).then_inc(qk_var, 1)

            def qk_normalise(j):
                _, b, used = uses(pj_order, ("qkv", j))
                v.wait_ge(pj_free[b], used + 1)
                v.wait_ge(qk_rstd, j + 1)
                rb = qrs[:, j, :].rearrange("p (h o) -> p h o", o=1)
                if j < TT:
                    k2 = qk_nrm[j % 2][:, 0:2 * KVH, :].rearrange("p (g r) d -> p g r d", r=2)
                    for r in range(2):
                        mark(tt(k2[:, :, r, :], qk_raw[j % 2][:, 0:2, :], bc(rb[:, 0:2], [P, 2, HD]), ALU.mult))
                else:
                    mark(tt(qk_nrm[j % 2], qk_raw[j % 2], bc(rb, [P, HEADS, HD]), ALU.mult))
                settle()
                v.sem_inc(qk_norm, 1)

            def qk_turned(j):
                n, b, used = uses(tp_order, ("qkt", j))
                v.wait_ge(tp_full, n + 1)
                t = j % TT
                nh = KVH if j < TT else HEADS // 2
                src = tp[b][:, 0:nh * P].rearrange("p (h n) -> p h n", h=nh)
                if j < TT:
                    v.tensor_copy(kT[:, :, t * P:(t + 1) * P], src).then_inc(tp_free[b], 1)
                else:
                    ts(qT[:, :, t * P:(t + 1) * P], src, qg[:, 2:3], None, ALU.mult).then_inc(tp_free[b], 1)
                v.wait_ge(tp_free[b], used + 1)
                v.sem_inc(qT_done, 1)

            def input_weights(c):
                s0 = slice(c * SPC, (c + 1) * SPC)
                if c:
                    v.wait_ge(tp_full, uses(tp_order, ("w", c - 1, 1))[0] + 1)
                br, bi = Bre[:, s0], Bim[:, s0]
                mark(v.tensor_copy(w1[:, 0, :, SUB - 1, :], br))
                mark(v.tensor_copy(w1[:, 1, :, SUB - 1, :], bi))
                J = SUB - 1
                a, b_ = (bc(pw_down[:, f, :, s0].rearrange("p j (s o) -> p s j o", o=1), [P, SPC, J, TCH]) for f in range(2))
                cmul((w1[:, 0, :, 0:J, :], w1[:, 1, :, 0:J, :]), (steps(br, J), steps(bi, J)), (a, b_), lambda k: lt(k, J))
                v.sem_inc(w1_done, 1)

            def steps(w, n):
                return bc(w.rearrange("p s (o c) -> p s o c", o=1), [P, SPC, n, TCH])

            def lt(k, n):
                m = tb[k + 1] if k < 3 else weight_tmp
                return m.rearrange("p s (j c) -> p s j c", j=SUB)[:, :, 0:n, :]

            def output_weights(c):
                s0 = slice(c * SPC, (c + 1) * SPC)
                if c:
                    v.wait_ge(y_full, c)
                cr, cn = Cre[:, s0], Cim[:, s0]
                mark(v.tensor_copy(CLre[:, :, 0, :], cr))
                mark(v.tensor_copy(CLim[:, :, 0, :], cn))
                a, b_ = (bc(pw[:, f, 1:, s0].rearrange("p j (s o) -> p s j o", o=1), [P, SPC, SUB, TCH]) for f in range(2))
                cr, cn = steps(cr, SUB), steps(cn, SUB)
                t = [lt(k, SUB) for k in range(4)]
                mark(tt(t[0], cr, a, ALU.mult))
                mark(tt(t[1], cn, b_, ALU.mult))
                mark(tt(t[2], cn, a, ALU.mult))
                mark(tt(t[3], cr, b_, ALU.mult))
                settle()
                mark(tt(CLre[:, :, 1:, :], t[0], t[1], ALU.add))
                mark(tt(CLim[:, :, 1:, :], t[2], t[3], ALU.subtract))
                settle()
                v.sem_inc(cl_done, 1)

            def score_max(a):
                blk, kv = a // KVH, a % KVH
                W = 2 * P if blk else P
                p_ = probs[a % 2]
                k0 = 2 * P - W
                if a >= 2:
                    v.wait_ge(tp_full, uses(tp_order, ("pt", a - 2, 1 if (a - 2) >= KVH else 0))[0] + 1)
                v.wait_ge(const_ready, 10)
                v.wait_ge(sc_full, a + 1)
                for h in range(QPK):
                    slope = 2.0 ** (-8.0 * (kv * QPK + h + 1) / HEADS)
                    mark(stt(p_[:, h, 0:W], neg_dist[:, k0:], slope,
                             sc[h % 2][:, (h // 2) * 2 * P:(h // 2) * 2 * P + W], ALU.mult, ALU.add))
                settle()
                v.sem_inc(sc_read, 1)
                st = lambda i: smx[:, a % 2, i, :]
                link(v.tensor_reduce(st(0), p_[:, :, 0:W], AX_X, ALU.max))
                snk = sink[:, kv * QPK:(kv + 1) * QPK]
                link(tt(st(0), st(0), snk, ALU.max))
                ts(st(1), st(0), -1.0, None, ALU.mult).then_inc(m_ready, 1)
                tt(st(2), snk, st(0), ALU.subtract).then_inc(m_ready, 1)

            def softmax_sum(a):
                st = lambda i: smx[:, a % 2, i, :]
                v.wait_ge(exp_done, (QPK + 1) * (a + 1))
                link(tt(st(4), st(4), st(3), ALU.add))
                v.reciprocal(st(5), st(4)).then_inc(sum_ready, 1)

            def scan_tile(c):
                v.wait_ge(bu_full, c + 1)
                v.wait_ge(e_done, c + 1)
                if c:
                    v.wait_ge(z_done, c)
                X, Y = (mb[i][:].rearrange("p (q n) -> p q n", q=SPC) for i in range(2))
                mark(tt(tb[0], X, Ec, ALU.mult))
                mark(tt(tb[1], Y, Es, ALU.mult))
                mark(tt(tb[2], Y, Ec, ALU.mult))
                mark(tt(tb[3], X, Es, ALU.mult))
                settle()
                v.sem_inc(bu_read, 1)
                mark(tt(tb[0], tb[0], tb[1], ALU.add))
                mark(tt(tb[2], tb[2], tb[3], ALU.subtract))
                settle()
                for q in range(SPC):
                    dec = bc(prm[:, 4, c * SPC + q:c * SPC + q + 1], [P, CH])
                    mark(v.tensor_tensor_scan(tb[1][:, q, :], dec, tb[0][:, q, :], 0.0, ALU.mult, ALU.add))
                    mark(v.tensor_tensor_scan(tb[3][:, q, :], dec, tb[2][:, q, :], 0.0, ALU.mult, ALU.add))
                settle()
                L = slice(0, CH - 1)
                wr, wi = tb[1][:, :, L], tb[3][:, :, L]
                if c:
                    v.wait_ge(y_full, c)
                mark(tt(tb[0][:, :, L], wr, Ec[:, :, L], ALU.mult))
                mark(tt(tb[2][:, :, L], wi, Es[:, :, L], ALU.mult))
                settle()
                mark(tt(Sre[:, :, 1:CH], tb[0][:, :, L], tb[2][:, :, L], ALU.subtract))
                settle()
                mark(tt(tb[0][:, :, L], wr, Es[:, :, L], ALU.mult))
                mark(tt(tb[2][:, :, L], wi, Ec[:, :, L], ALU.mult))
                settle()
                mark(tt(Sim[:, :, 1:CH], tb[0][:, :, L], tb[2][:, :, L], ALU.add))
                settle()
                v.sem_inc(S_done, 1)

            def low_zy(n):
                v.wait_ge(zy_high, n + 1)
                dst, src = zy_parts(h_low)[n]
                tt(dst, src, zy_parts(h_high)[n][0].bitcast(F32), ALU.subtract).then_inc(zy_low, 1)

            def gelu(c):
                v.wait_ge(z_full, c + 1)
                uc = uT[:, c].rearrange("p j n -> p (j n)")
                f1, f2 = (tb[i].rearrange("p q n -> p (q n)") for i in (1, 2))
                stt(f1, uc, d_col[:, c:c + 1], mb[1][:], ALU.mult, ALU.add).then_inc(yv_done, 1)
                if c == CT_ - 1:
                    low_zy(1)
                v.wait_ge(z_sq, c + 1)
                link(ts(f2, f2, GELU_CUBE, 1.0, ALU.mult, ALU.add))
                v.wait_ge(yv_done, c + 1)
                tt(f2, f2, f1, ALU.mult).then_inc(z_arg, 1)
                if c == CT_ - 1:
                    low_zy(2)
                v.wait_ge(z_th, c + 1)
                v.wait_ge(u4_loaded, 16 * SUB * SPC)
                stt(zT[:, c, :].rearrange("p (n j) -> p j n", j=SUB), f2.rearrange("p (j n) -> p j n", j=SUB), 1.0,
                    f1.rearrange("p (j n) -> p j n", j=SUB), ALU.add, ALU.mult).then_inc(z_done, 1)

            split_low(v, P_QKV + 1)
            for j in range(2 * TT):
                qk_variance(j)
                if j >= 3:
                    qk_turned(j - 3)
                if j >= 1:
                    qk_normalise(j - 1)
                if j in SPLITS:
                    split_low(v, SPLITS[j])
                if j == TT:
                    input_weights(0)
                if j == TT + 2:
                    output_weights(0)
            qk_turned(2 * TT - 3)
            qk_normalise(2 * TT - 1)
            for j in range(2 * TT - 2, 2 * TT):
                qk_turned(j)
            for i in range(2 * DC + 1):
                if i % 2 == 0 and i < 2 * DC:
                    score_max(i // 2)
                    softmax_sum(i // 2)
                if i % 4 == 0 and i >= 4:
                    gelu(i // 4 - 1)
                if i % 4 == 1:
                    scan_tile(i // 4)
                if i % 4 == 2 and i // 4 + 1 < CT_:
                    input_weights(i // 4 + 1)
                if i % 4 == 3 and i // 4 + 1 < CT_:
                    output_weights(i // 4 + 1)
                if i == 2 * DC - 1:
                    split_low(v, P_M)
                    low_zy(0)
            low_zy(3)

            def merged_low(m):
                v.wait_ge(m_high_done, m + 1)
                mark(tt(m_low[:, m, :], merge_tmp(m)[:, 1, :], m_high[:, m, :].bitcast(F32), ALU.subtract))
                settle()
                v.sem_inc(m_low_done, 1)

            v.wait_ge(gates_done, 2 * DC)
            for m in range(DC):
                G, V, A = merge_banks(m)
                t3 = merge_tmp(m)
                split_low(v, P_M + m + 1)
                v.wait_ge(mg_act, m + 1)
                v.wait_ge(mg_full, 3 * (m + 1))
                mark(stt(t3[:, 1, :], t3[:, 0, :], 1.0, V[:], ALU.add, ALU.mult))
                mark(stt(t3[:, 2, :], ta_gate[:, m, :], 1.0, A[:], ALU.add, ALU.mult))
                settle()
                v.sem_inc(mg_free, 1)
                link(stt(t3[:, 1, :], ts_gate[:, m, :], 1.0, t3[:, 1, :], ALU.add, ALU.mult))
                stt(t3[:, 1, :], t3[:, 1, :], 0.25, t3[:, 2, :], ALU.mult, ALU.add).then_inc(merged_done, 1)
                if m:
                    merged_low(m - 1)
            merged_low(DC - 1)
            v.wait_ge(x_again, 16)
            for t in range(TT):
                if t:
                    norm2(t - 1)
                for p_ in range(NOUT):
                    n = NOUT * t + p_
                    if t == 0 and p_ + 1 < NOUT:
                        split_low(v, P_OUT + p_ + 1)
                    xs = x2[:, t, p_ * 256:(p_ + 1) * 256]
                    if t == 0:
                        v.wait_ge(pj_full, n_pj + n + 1)
                        got = pj[n % 2][:, 0:256]
                    else:
                        v.wait_ge(pj_full, n_pj + NOUT * t + p_ // 2 * 2 + 2)
                        got = pj[p_ // 2][:, (1 - p_ % 2) * 256:(2 - p_ % 2) * 256]
                    stt(xs, got, 0.5, xs, ALU.mult, ALU.add).then_inc(x2_done, 1)
                    if t and p_ == NOUT // 2 - 1:
                        norm2_turned(t - 1)
            norm2(TT - 1)
            norm2_turned(TT - 1)
            v.wait_ge(const_ready, 10)
            for n in (0, 3):
                mark(v.tensor_copy(tg[:, :, :, n], bc(tok_id[:, :].rearrange("p (o t) -> p o t", o=1), [P, NE, TT])))
            mark(v.memset(rt[:, 7, 0:1, :], 0.0))
            v.wait_ge(lg_full, TT)
            v.wait_ge(rstd_done, 2 * TT)
            for t in range(TT):
                mark(ts(lg[:, t, :], sc[0][:, t * (NG + NE):(t + 1) * (NG + NE)], rstd[:, TT + t:TT + t + 1], None, ALU.mult))
            settle()
            r = lambda i, n=NE: rt[:, i, :, 0:n]
            s_ = lambda i: rs_[:, i, :]
            col = lambda i: s_(i).rearrange("p (t o) -> p t o", o=1)
            rev = lambda n: bc(e_rev[:, NE - n:NE].rearrange("p (o n) -> p o n", o=1), [P, TT, n])

            def first_max(dst, src, top, n):
                link(tt(r(11, n), src, bc(col(top), [P, TT, n]), ALU.is_equal))
                link(tt(r(11, n), r(11, n), rev(n), ALU.mult))
                link(v.tensor_reduce(s_(15), r(11, n), AX_X, ALU.max))
                link(tt(dst, r(11, n), bc(col(15), [P, TT, n]), ALU.is_equal))

            coarse, fine = lg[:, :, 0:NG], lg[:, :, NG:NG + NE]
            link(v.tensor_reduce(s_(0), coarse, AX_X, ALU.max))
            tt(r(0, NG), coarse, bc(col(0), [P, TT, NG]), ALU.subtract).then_inc(r_dve, 1)
            v.wait_ge(const_ready, 10)
            first_max(r(1, NG), coarse, 0, NG)
            link(ts(r(1, NG), r(1, NG), HIDE, -HIDE, ALU.mult, ALU.add))
            link(tt(r(2).rearrange("p t (g e) -> p t g e", g=NG), fine.rearrange("p t (g e) -> p t g e", g=NG),
                    bc(r(1, NG).rearrange("p t (g o) -> p t g o", o=1), [P, TT, NG, EPG]), ALU.add))
            link(v.tensor_reduce(s_(1), r(2), AX_X, ALU.max))
            first_max(r(3), r(2), 1, NE)
            link(stt(r(4), r(3), -3 * HIDE, r(2), ALU.mult, ALU.add))
            link(v.tensor_reduce(s_(2), r(4), AX_X, ALU.max))
            first_max(r(5), r(4), 2, NE)
            link(tt(r(6), r(3), r(5), ALU.add))
            for t in range(1, TT):
                link(tt(rt[:, 7, t, :], rt[:, 7, t - 1, :], rt[:, 6, t - 1, :], ALU.add))
            link(tt(cnt[:], rt[:, 7, TT - 1, :], rt[:, 6, TT - 1, :], ALU.add))
            v.sem_inc(r_pe, 1)
            tt(s_(6), s_(2), s_(1), ALU.subtract).then_inc(r_dve, 1)
            v.wait_ge(r_act, 1)
            link(v.tensor_reduce(s_(3), r(0, NG), AX_X, ALU.add))
            link(v.reciprocal(s_(4), s_(3)))
            v.wait_ge(r_act, 2)
            link(ts(s_(7), s_(6), 1.0, None, ALU.add))
            link(v.reciprocal(s_(8), s_(7)))
            link(tt(s_(9), s_(8), s_(4), ALU.mult))
            link(tt(s_(10), s_(9), s_(6), ALU.mult))
            link(tt(r(8), r(3), bc(col(9), [P, TT, NE]), ALU.mult))
            link(tt(r(9), r(5), bc(col(10), [P, TT, NE]), ALU.mult))
            ev = lambda w: w.rearrange("p t e -> p e t")
            link(tt(r(8), r(8), r(9), ALU.add))
            link(v.tensor_copy(tg[:, :, :, 1], ev(r(8))))
            mark(tt(tg[:, :, :, 2], ev(r(8)), tg[:, :, :, 1].bitcast(F32), ALU.subtract))
            settle()
            v.wait_ge(lg_full, TT + 1)
            link(v.tensor_copy(r(10), sc[0][:, 0:TT * NE].rearrange("p (t e) -> p t e", t=TT)))
            link(ts(r(7), r(6), -float(4 * SEQ), float(4 * SEQ), ALU.mult, ALU.add))
            tt(pos[:].rearrange("p e t -> p t e"), r(10), r(7), ALU.add).then_inc(route_done, 1)

            v.wait_ge(route_done, 1)
            def fill_lists(k):
                lo, hi = LISTS[k], LISTS[k + 1]
                for e in range(lo, hi):
                    if e >= 2:
                        v.wait_ge(idx_full, e - 1)
                    tt(pick[e % 2], bc(slot_no[:].rearrange("p (o n) -> p o n", o=1), [P, TT, CAP]),
                       bc(pos[:, e, :].rearrange("p (t o) -> p t o", o=1), [P, TT, CAP]), ALU.is_equal).then_inc(pick_done, 1)
                v.wait_ge(idx_full, hi)
                c0 = 128 + 64 * (k // 2)
                got = sc[k % 2][:, c0:c0 + 4 * (hi - lo)].rearrange("p (e n) -> p e n", n=4)
                v.tensor_copy(idx_all[:, lo:hi], got[:, :, 0])
                v.tensor_reduce(gate_all[:, lo:hi], got[:, :, 1:3], AX_X, ALU.add).then_inc(idx_done, 1)

            fill_lists(0)
            fill_lists(1)
            v.wait_ge(lg_full, TT + 2)
            link(v.tensor_reduce(flag_f[:], mb[0][:, 0:NE], AX_X, ALU.max))
            v.tensor_scalar(flag[0:1, 0:1], flag_f[0:1, 0:1], float(CAP), None, ALU.is_gt).then_inc(flag_done, 1)

            def low_rows(e4, e):
                for f in range(2):
                    v.wait_ge(xt_high_done, e * 2 + (f + 1))
                    fs = (slice(None), slice(4 * f, 4 * f + 4), slice(None))
                    tt(xt_low[e4 % 2][fs], tp[f][:].rearrange("p (k n) -> p k n", k=4), xt_high[e4 % 2][fs].bitcast(F32),
                       ALU.subtract).then_inc(xt_done, 1)

            def low_up(e4, e, h):
                v.wait_ge(up_high_done, e * 2 + (h + 1))
                tt(up_low[e4][:, half(h)], ring[e4][:, half(h)], up_high[e4 % 2][:, half(h)].bitcast(F32), ALU.subtract
                   ).then_inc(up_low_done, 1)

            def low_act(e4, e):
                v.wait_ge(at_high_done, e + 1)
                tt(at_low[e4 % 2][:], sc[1][:, 0:2 * P].rearrange("p (k n) -> p k n", k=2), at_high[e4 % 2][:].bitcast(F32),
                   ALU.subtract).then_inc(at_done, 1)

            def swiglu(e4, e):
                b = e4 % 2
                v.wait_ge(th_done, e + 1)
                stt(a1_e[b], th_e[b], 1.0, pj[b][:, 0:DE], ALU.add, ALU.mult).then_inc(act_done, 1)
                v.wait_ge(act_done, e * 2 + 1)
                stt(act_e[b], a1_e[b], 0.5, pj[b][:, DE:UP_N], ALU.mult, ALU.mult).then_inc(act_done, 1)

            def step(r, e, before=True, last=False):
                n4 = (r + 1) % 4
                if not last:
                    low_up(n4, e + 1, 0)
                swiglu(r, e)
                if before:
                    low_act((r + 3) % 4, e - 1)
                if not last:
                    low_rows(n4, e + 1)
                    low_up(n4, e + 1, 1)

            low_rows(0, 0)
            step(0, 0, before=False)
            step(1, 1)
            step(2, 2)
            fill_lists(2)
            step(3, 3)
            for k, oh in enumerate((3, 5)):
                link(tt(r(8), r(oh), bc(e_no[:].rearrange("p (o n) -> p o n", o=1), [P, TT, NE]), ALU.mult))
                link(v.tensor_reduce(s_(11), r(8), AX_X, ALU.add))
                link(tt(r(9), r(oh), r(10), ALU.mult))
                link(v.tensor_reduce(s_(12), r(9), AX_X, ALU.add))
                row = s_((14, 5)[k])
                link(stt(row, s_(11), float(CAP), s_(12), ALU.mult, ALU.add))
                for j in range(1, MORE + 1):
                    link(ts(s_(13), s_(12), float(j * CAP), float((NE - 1) * CAP), ALU.is_ge, ALU.mult))
                    link(tt(row, row, s_(13), ALU.add))
            for k, op in enumerate((ALU.min, ALU.max)):
                link(tt(s_(11), s_(14), s_(5), op))
                link(v.tensor_copy(dest[:, k, :], s_(11)))
            with v.Fori(0, NE // 4 - 2) as i:
                for r_ in range(4):
                    step(r_, i * 4 + (r_ + 4))
            for e in range(NE - 4, NE):
                step(e % 4, e, last=e == NE - 1)
            low_act(3, NE - 1)
            over = v.value_load(flag[0:1, 0:1], min_val=0, max_val=1)
            with v.If(over > 0):
                for b in range(2):
                    v.wait_ge(y_stored[b], 8 * NE)
                with v.Fori(0, MORE) as j:
                    ts(pos[:], pos[:], float(-CAP), None, ALU.add).then_inc(o_pos, 1)
                    v.wait_ge(o_pos, j + 1)
                    v.sem_inc(gather_turn, 1)
                    with v.Fori(0, NE) as e:
                        tt(pick[0], bc(slot_no[:].rearrange("p (o n) -> p o n", o=1), [P, TT, CAP]),
                           bc(pos[:, bass.ds(e, 1), :].rearrange("p e (t o) -> p (e t) o", o=1), [P, TT, CAP]),
                           ALU.is_equal).then_inc(o_pick, 1)
                        v.wait_ge(o_idxf, j * NE + e + 1)
                        v.tensor_copy(idx[:, 0:1], sc[0][:, 128:129])
                        v.tensor_reduce(gate[:, 0:1], sc[0][:, 129:131], AX_X, ALU.add).then_inc(o_idx, 1)
                        v.wait_ge(o_xt, j * NE + e + 1)
                        for f in range(2):
                            v.tensor_copy(xgT[0][:, 4 * f:4 * f + 4, :], tp[f][:].rearrange("p (k n) -> p k n", k=4)
                                          ).then_inc(o_xtd, 1)
                        v.wait_ge(o_th, j * NE + e + 1)
                        stt(a1_e[0], th_e[0], 1.0, pj[0][:, 0:DE], ALU.add, ALU.mult).then_inc(o_act, 1)
                        v.wait_ge(o_act, (j * NE + e) * 2 + 1)
                        stt(act_e[0], a1_e[0], 0.5, pj[0][:, DE:UP_N], ALU.mult, ALU.mult).then_inc(o_act, 1)
                        v.wait_ge(o_st, (j * NE + e + 1) * 16)
            for k in range(2):
                for t in range(TT):
                    v.wait_ge(rows_back[k][t], 16)
                    ins = tt(x2[:, t, :], x2[:, t, :], gath[2 * t + k], ALU.add)
                    if k:
                        ins.then_inc(sum_done, 1)
                    else:
                        mark(ins)
                settle()

        @block.tensor
        def _(pe):
            def fill(order, frees, key):
                n, b, used = uses(order, key)
                if used:
                    pe.wait_ge(frees[b], used)
                return b

            pe.wait_ge(const_ready, 3)
            for t in range(TT):
                pe.wait_ge(xn_done, t + 1)
                for f in range(2):
                    b = fill(tp_order, tp_free, ("h", t, f))
                    for k in range(4):
                        ins = pe.transpose(tp[b][:, k * P:(k + 1) * P], xn[:, t, (4 * f + k) * P:(4 * f + k + 1) * P], ident[:])
                    ins.then_inc(tp_full, 1)
            def product(dst, terms, first=True, last=True):
                for i, ((sh, sl), (mh, ml)) in enumerate(terms):
                    pe.matmul(dst, sh, mh, start=first and i == 0, stop=False)
                    pe.matmul(dst, sh, ml, start=False, stop=False)
                    ins = pe.matmul(dst, sl, mh, start=False, stop=last and i == len(terms) - 1)
                return ins

            def piece_ready(n):
                pe.wait_ge(high_done, n + 1)
                low_ready(pe, n)

            both = lambda hl, *ix: tuple(x[(slice(None),) + ix] for x in hl)
            h_hl = (h_high, h_low)
            for b in range(2):
                pe.wait_ge(tp_free[b], TT)
            for c in range(CT_):
                if c % 2 == 0:
                    piece_ready(P_U + c // 2)
                w = piece_w(P_U + c // 2, k=DC, n=256)
                b = fill(pj_order, pj_free, ("u", c))
                c0 = c % 2 * P
                product(pj[b][:], [(both(w, k, slice(c0, c0 + P)), both(h_hl, k, slice(None))) for k in range(DC)]
                        ).then_inc(pj_full, 1)
                if c == 0:
                    b = fill(tp_order, tp_free, ("prm",))
                    pe.wait_ge(rows_done, 1)
                    for i, src in enumerate((13, 14, 15, 16, 6, 8, 7)):
                        ins = pe.transpose(tp[b][:, i * ST:(i + 1) * ST], R(src), ident[0:ST, 0:ST])
                    ins.then_inc(tp_full, 1)
                if c == 2:
                    pe.wait_ge(cexp_done, 1)
                    for f in range(2):
                        b = fill(tp_order, tp_free, ("ct", f))
                        for g in range(CT_):
                            ins = pe.transpose(tp[b][:, g * P:(g + 1) * P], c_exp[:, f, g].rearrange("p g s -> p (g s)"), ident[:])
                        ins.then_inc(tp_full, 1)

            def turn_qk(j):
                pe.wait_ge(qk_norm, j + 1)
                b = fill(tp_order, tp_free, ("qkt", j))
                for k in range(KVH if j < TT else HEADS // 2):
                    ins = pe.transpose(tp[b][:, k * P:(k + 1) * P],
                                       qk_nrm[j % 2][:, 2 * k:2 * k + 2, :].rearrange("p h d -> p (h d)"), ident[:])
                ins.then_inc(tp_full, 1)

            for j in range(2 * TT):
                b = fill(pj_order, pj_free, ("qkv", j))
                tok = slice(j % TT * P, (j % TT + 1) * P)
                if j < TT:
                    if j == 0:
                        piece_ready(P_QKV)
                    dst, w, at_k = pj[b][:, 0:256], piece_w(P_QKV, k=DC, n=256), lambda w, k: both(w, k, slice(None))
                else:
                    if j == TT:
                        piece_ready(P_QKV + 1)
                        piece_ready(P_QKV + 2)
                    dst = pj[b][:].rearrange("p (s n) -> p s n", s=2)
                    w = [q_split[:, :, f].rearrange("p s (k n) -> p s k n", k=DC) for f in range(2)]
                    at_k = lambda w, k: both(w, slice(None), k, slice(None))
                product(dst, [(both(h_hl, k, tok), at_k(w, k)) for k in range(DC)]).then_inc(pj_full, 1)
                if j >= 2:
                    turn_qk(j - 2)
            def scores(a):
                blk, kv = a // KVH, a % KVH
                W = 2 * P if blk else P
                t0 = blk * P
                pe.wait_ge(qT_done, 2 * TT)
                if a:
                    pe.wait_ge(sc_read, a)
                for h in range(QPK):
                    hh = kv * QPK + h
                    ps = slice((hh % 2) * HD, (hh % 2) * HD + HD)
                    ins = pe.matmul(sc[h % 2][:, (h // 2) * 2 * P:(h // 2) * 2 * P + W], qT[ps, hh // 2, t0:t0 + P],
                                    kT[ps, kv, t0 + P - W:t0 + P], start=True, stop=True)
                ins.then_inc(sc_full, 1)

            def turn_probs(a):
                blk = a // KVH
                pe.wait_ge(p_done, QPK * (a + 1))
                for f in range(2 if blk else 1):
                    b = fill(tp_order, tp_free, ("pt", a, f))
                    for h in range(QPK):
                        ins = pe.transpose(tp[b][:, h * P:(h + 1) * P], probs[a % 2][:, h, f * P:(f + 1) * P], ident[:])
                    ins.then_inc(tp_full, 1)

            n_pt = [0]

            def values(a):
                blk, kv = a // KVH, a % KVH
                nf = 2 if blk else 1
                n_pt[0] += nf
                pe.wait_ge(pT_done, n_pt[0])
                pe.wait_ge(v_done, TT)
                b = fill(pj_order, pj_free, ("av", a))
                ph = pT.rearrange("p f (a b) q -> p f b a q", b=2)
                for odd in range(2):
                    for f in range(nf):
                        ins = pe.matmul(pj[b][odd * HD:(odd + 1) * HD, 0:2 * P].rearrange("p (a q) -> p a q", a=2),
                                        v_tok[:, blk - nf + 1 + f, kv * HD:(kv + 1) * HD], ph[:, f, odd],
                                        start=f == 0, stop=f == nf - 1)
                ins.then_inc(pj_full, 1)

            def turn_input_weights(c):
                pe.wait_ge(w1_done, c + 1)
                for f in range(2):
                    b = fill(tp_order, tp_free, ("w", c, f))
                    for q in range(SPC):
                        ins = pe.transpose(tp[b][:, q * P:(q + 1) * P], w1[:, f, q].rearrange("p i c -> p (i c)"), ident[:])
                    ins.then_inc(tp_full, 1)

            def own_inputs(c):
                pe.wait_ge(cl_done, c + 1)
                b = fill(tp_order, tp_free, ("k", c))
                for q in range(SPC):
                    s = c * SPC + q
                    dst = tp[b][0:TCH, q * P:(q + 1) * P]
                    pe.matmul(dst, Bre[:, s, :], CLre[:, q, 0:SUB, :], start=True, stop=False)
                    ins = pe.matmul(dst, Bim[:, s, :], CLim[:, q, 0:SUB, :], start=False, stop=True)
                ins.then_inc(tp_full, 1)

            def chunk_inputs(c):
                pe.wait_ge(w1T_done, 2 * (c + 1))
                pe.wait_ge(u4_loaded, 16 * SUB * SPC)
                if c:
                    pe.wait_ge(yv_done, c)
                    pe.wait_ge(y_evac, c)
                for q in range(SPC):
                    for f in range(2):
                        ins = pe.matmul(mb[f][:, q * P:(q + 1) * P], w1T[:, f, q, :], u4[:, c * SPC + q, :], start=True, stop=True)
                ins.then_inc(bu_full, 1)

            def chunk_outputs(c):
                pe.wait_ge(S_done, c + 1)
                pe.wait_ge(toep_done, SUB * (c + 1))
                yb = mb[0][:].rearrange("p (j c) -> p j c", j=SUB)
                for q in range(SPC):
                    dst = yb[:, :, q * TCH:(q + 1) * TCH]
                    pe.matmul(dst, u4[:, c * SPC + q, :], toep[:, q, :], start=q == 0, stop=False, skip_group_check=True)
                for q in range(SPC):
                    dst = yb[:, :, q * TCH:(q + 1) * TCH]
                    pe.matmul(dst, Sre[:, q, :], CLre[:, q, 1:, :], start=False, stop=False, skip_group_check=True)
                    ins = pe.matmul(dst, Sim[:, q, :], CLim[:, q, 1:, :], start=False, stop=q == SPC - 1, skip_group_check=True)
                ins.then_inc(y_full, 1)

            def turn_outputs(c):
                pe.wait_ge(y_evac, c + 1)
                yt = tb[0].rearrange("p q n -> p (q n)")
                for j in range(SUB):
                    ins = pe.transpose(mb[1][:, j * P:(j + 1) * P], yt[:, j * P:(j + 1) * P], ident[:])
                ins.then_inc(z_full, 1)

            for i in range(2 * DC + 1):
                if i < 2 * DC:
                    if i % 2 == 0:
                        piece_ready(P_G + i // 2)
                    w = piece_w(P_G + i // 2, k=DC, n=256)
                    b = fill(pj_order, pj_free, ("gate", i))
                    c0 = i % 2 * P
                    product(pj[b][:], [(both(w, k, slice(c0, c0 + P)), both(h_hl, k, slice(None))) for k in range(DC)]
                            ).then_inc(pj_full, 1)
                if i == 0:
                    for j in range(2 * TT - 2, 2 * TT):
                        turn_qk(j)
                if i % 4 == 0 and i >= 4:
                    turn_outputs(i // 4 - 1)
                if i % 4 == 0 and i < 2 * DC:
                    turn_input_weights(i // 4)
                if i % 4 == 1:
                    chunk_inputs(i // 4)
                if i % 4 == 2:
                    own_inputs(i // 4)
                if i % 2 == 0 and i < 2 * DC:
                    scores(i // 2)
                if i % 2 == 1:
                    if i % 4 == 3:
                        chunk_outputs(i // 4)
                    turn_probs(i // 2)
                if i % 2 == 0 and i >= 2:
                    values(i // 2 - 1)
            pe.wait_ge(gates_done, 2 * DC)
            pe.wait_ge(sc_read, NQ)
            for m in range(DC):
                if m >= 2:
                    pe.wait_ge(mg_free, m - 1)
                piece_ready(P_M + m)
                w = piece_w(P_M + m, f=3, k=4, n=P)
                G, V, A = merge_banks(m)
                early = CT_ - 1 if m == 0 else 0
                if early:
                    pe.wait_ge(zy_low, 1)
                    for f, dst in ((0, G), (1, V)):
                        product(dst[:], [(both(w, f, k, slice(None)), both(h_hl, k, slice(None))) for k in range(early)], last=False)
                for f, dst, k0, done in ((2, A, CT_, 0), (0, G, 0, early), (1, V, 0, early)):
                    if m == 0:
                        pe.wait_ge(zy_low, 3 if f == 2 else 4)
                    product(dst[:], [(both(w, f, k, slice(None)), both(h_hl, k0 + k, slice(None))) for k in range(done, 4)],
                            first=not done).then_inc(mg_full, 1)
            m_hl = (m_high, m_low)

            def turn_norm2(t):
                pe.wait_ge(n2_done, t + 1)
                if t:
                    pe.wait_ge(h2T_done, 2 * t)
                else:
                    for b in range(2):
                        pe.wait_ge(tp_free[b], (n_tp + 1 - b) // 2)
                for f in range(2):
                    for k in range(4):
                        ins = pe.transpose(tp[f][:, k * P:(k + 1) * P], xg[t % 2][:, (4 * f + k) * P:(4 * f + k + 1) * P], ident[:])
                    ins.then_inc(tp_full, 1)

            def router(t):
                pe.wait_ge(h2T_done, 2 * (t + 1))
                for k in range(DC):
                    ins = pe.matmul(sc[0][:, t * (NG + NE):(t + 1) * (NG + NE)], xgT[t % 2][:, k, :], rw[:, k, :],
                                    start=k == 0, stop=k == DC - 1)
                ins.then_inc(lg_full, 1)

            for t in range(TT):
                for p_ in range(NOUT):
                    if t == 0:
                        piece_ready(P_OUT + p_)
                    w = piece_w(P_OUT + p_, k=DC, n=256)
                    n = NOUT * t + p_
                    tok = slice(t * P, (t + 1) * P)
                    if t == 0:
                        if n >= 2:
                            pe.wait_ge(x2_done, n - 1)
                        for k in range(DC):
                            if n == 0:
                                pe.wait_ge(m_low_done, k + 1)
                            ins = product(pj[n % 2][:, 0:256], [(both(m_hl, k, tok), both(w, k, slice(None)))],
                                          k == 0, k == DC - 1)
                        ins.then_inc(pj_full, 1)
                    elif p_ % 2 == 0:
                        pe.wait_ge(x2_done, n - 1 if n == NOUT else n - 2)
                        w2 = [x[:, p_ // 2].rearrange("p s (k n) -> p s k n", k=DC) for x in (out_high, out_low)]
                        product(pj[p_ // 2][:].rearrange("p (s n) -> p s n", s=2),
                                [(both(m_hl, k, tok), both(w2, slice(None), k, slice(None))) for k in range(DC)]).then_inc(pj_full, 2)
                    if t and p_ == NOUT // 2 - 1:
                        turn_norm2(t - 1)
                    if t and p_ == NOUT - 1:
                        router(t - 1)
            turn_norm2(TT - 1)
            router(TT - 1)
            pe.wait_ge(r_pe, 1)
            pe.wait_ge(const_ready, 10)
            flat = lambda i: rt[:, i].rearrange("p t e -> p (t e)")
            pe.matmul(sc[0][:, 0:TT * NE], before[:], flat(6), start=True, stop=False)
            pe.matmul(sc[0][:, 0:TT * NE], ones[:], flat(7), start=False, stop=True).then_inc(lg_full, 1)
            pe.matmul(mb[0][:, 0:NE], ones[:], cnt[:], start=True, stop=True).then_inc(lg_full, 1)

            pe.wait_ge(route_done, 1)
            def place_lists(lo, hi):
                for e in range(lo, hi):
                    place_list(e)

            def place_list(e):
                k = sum(e >= lo for lo in LISTS[1:])
                c0 = 128 + 64 * (k // 2) + 4 * (e - LISTS[k])
                pe.wait_ge(pick_done, e + 1)
                for t in range(TT):
                    ins = pe.matmul(sc[k % 2][:, c0:c0 + 4], pick[e % 2][:, t, :], tg[:, e, t, :], start=t == 0, stop=t == TT - 1)
                ins.then_inc(idx_full, 1)

            def turn_rows(e4, e, n_rows):
                pe.wait_ge(gathered[e4 % 2], n_rows)
                for f in range(2):
                    if not (isinstance(e, int) and e == 0):
                        pe.wait_ge(xt_done, e * 2 + (f - 1))
                    for k in range(4):
                        ins = pe.transpose(tp[f][:, k * P:(k + 1) * P], xg[e4 % 2][:, (4 * f + k) * P:(4 * f + k + 1) * P], ident[:])
                    ins.then_inc(xt_full, 1)

            def up(e4, e):
                pe.wait_ge(xt_done, (e + 1) * 2)
                if not (isinstance(e, int) and e < 2):
                    pe.wait_ge(act_done, e * 2 - 2)
                w = [x[:].rearrange("p (k n) -> p k n", k=DC) for x in (up_high[e4 % 2], up_low[e4])]
                for h in range(2):
                    if isinstance(e, int) and e == 0:
                        pe.wait_ge(first_low_done, h + 1)
                    else:
                        pe.wait_ge(up_low_done, e * 2 + (h - 1))
                    for k in range(h * DC // 2, (h + 1) * DC // 2):
                        xs, ws = both((xt_high[e4 % 2], xt_low[e4 % 2]), k), both(w, k)
                        pe.matmul(pj[e4 % 2][:], xs[0], ws[0], start=k == 0, stop=False)
                        pe.matmul(pj[e4 % 2][:], xs[0], ws[1], start=False, stop=False)
                        ins = pe.matmul(pj[e4 % 2][:], xs[1], ws[0], start=False, stop=k == DC - 1)
                ins.then_inc(up_full, 1)

            def turn_act(n4, e):
                e4 = (n4 + 3) % 4
                pe.wait_ge(act_done, (e + 1) * 2)
                if not (isinstance(e, int) and e == 0):
                    pe.wait_ge(at_done, e)
                for k in range(2):
                    ins = pe.transpose(sc[1][:, k * P:(k + 1) * P], act_e[e4 % 2][:, k * P:(k + 1) * P], ident[:])
                ins.then_inc(at_full, 1)

            def down_(e4, e):
                pe.wait_ge(at_done, e + 1)
                pe.wait_ge(down_low_done, e + 1)
                if not (isinstance(e, int) and e == 0):
                    pe.wait_ge(y_scaled, e * 2)
                w = [x[:].rearrange("p (k n) -> p k n", k=2) for x in (down_high[e4 % 2], down_low[e4 % 2])]
                for h in range(2):
                    ins = product(mb[h][:], [(both((at_high[e4 % 2], at_low[e4 % 2]), k), both(w, k, slice(h * 512, (h + 1) * 512)))
                                             for k in range(2)])
                ins.then_inc(dn_full, 1)

            def step(e4, e, rnd, first=False, lists=False, last=False):
                up(e4, e)
                if lists:
                    pe.wait_ge(idx_done, 2)
                    place_lists(LISTS[2], NE)
                if not first:
                    turn_act(e4, e - 1)
                if not last:
                    n4 = (e4 + 1) % 4
                    turn_rows(n4, e + 1, (rnd if e4 < 3 else rnd + 1) * 32 + (16 * (n4 // 2) + 16))
                if not first:
                    p4 = (e4 + 3) % 4
                    down_(p4, e - 1)

            place_lists(0, LISTS[2])
            turn_rows(0, 0, 16)
            for e in range(4):
                step(e, e, 0, first=e == 0, lists=e == 3)
            with pe.Fori(0, NE // 4 - 2) as i:
                for r in range(4):
                    step(r, i * 4 + (r + 4), i + 1)
            for e in range(NE - 4, NE):
                step(e % 4, e, e // 4, last=e == NE - 1)
            turn_act(0, NE - 1)
            down_(3, NE - 1)
            pe.wait_ge(dn_full, NE)
            pe.sem_inc(o_dn, 1)
            pe.wait_ge(flag_done, 1)
            over = pe.value_load(flag[0:1, 0:1], min_val=0, max_val=1)
            with pe.If(over > 0):
                w = ring[0].rearrange("p (k n) -> p k n", k=DC)
                with pe.Fori(0, MORE) as j:
                    with pe.Fori(0, NE) as e:
                        b = j * NE + e
                        pe.wait_ge(o_pick, b + 1)
                        for t in range(TT):
                            ins = pe.matmul(sc[0][:, 128:132], pick[0][:, t, :],
                                            tg[:, bass.ds(e, 1), t, :].rearrange("p e n -> p (e n)"), start=t == 0, stop=t == TT - 1)
                        ins.then_inc(o_idxf, 1)
                        pe.wait_ge(o_gath, (b + 1) * 16)
                        for k in range(DC):
                            ins = pe.transpose(tp[k // 4][:, (k % 4) * P:(k % 4 + 1) * P], xg[0][:, k * P:(k + 1) * P], ident[:])
                        ins.then_inc(o_xt, 1)
                        pe.wait_ge(o_xtd, (b + 1) * 2)
                        pe.wait_ge(o_w, (b + 1) * 32)
                        for k in range(DC):
                            ins = pe.matmul(pj[0][:], xgT[0][:, k, :], w[:, k, :], start=k == 0, stop=k == DC - 1)
                        ins.then_inc(o_up, 1)
                        pe.wait_ge(o_act, (b + 1) * 2)
                        for k in range(2):
                            ins = pe.transpose(sc[1][:, k * P:(k + 1) * P], act_e[0][:, k * P:(k + 1) * P], ident[:])
                        ins.then_inc(o_at, 1)
                        pe.wait_ge(o_atd, b + 1)
                        for h in range(2):
                            for k in range(2):
                                ins = pe.matmul(mb[h][:], actT[:, k, :], down[0][:, k, h * 512:(h + 1) * 512], start=k == 0, stop=k == 1)
                        ins.then_inc(o_dn, 1)


_INS = ['x', 'norm_mix', 'w_in', 'ssm_lam_re', 'ssm_lam_im', 'ssm_log_dt', 'ssm_b_re', 'ssm_b_im', 'ssm_c_re',
        'ssm_c_im', 'ssm_d', 'w_ssm_glu_val', 'w_ssm_glu_gate', 'q_norm', 'k_norm', 'attn_sinks', 'w_attn_up',
        'w_out', 'norm_ffn', 'w_coarse', 'w_fine', 'w_expert_up', 'w_expert_down']
_OUTS = [((1, 512, 1024), 'float32')]


def kernel(**inputs):
    import numpy as _np
    import concourse.bacc as _bacc
    from concourse import mybir as _mybir
    from concourse.bass_utils import run_bass_kernel_spmd as _run

    nc = _bacc.Bacc("TRN2", target_bir_lowering=False, num_devices=1)
    arrays, args = {}, []
    for name in _INS:
        a = _np.ascontiguousarray(inputs[name])
        arrays[f"in_{name}_dram"] = a
        args.append(nc.dram_tensor(f"in_{name}_dram", a.shape, _mybir.dt.from_np(a.dtype), kind="ExternalInput").ap())
    for i, (shape, dtype) in enumerate(_OUTS):
        dt = _mybir.dt.from_np(_np.dtype(dtype))
        args.append(nc.dram_tensor(f"out_{i}_dram", shape, dt, kind="ExternalOutput").ap())
    hybrid_layer(nc, *args)
    r = _run(nc, [arrays], core_ids=[0])
    got = tuple(r.results[0][f"out_{i}_dram"] for i in range(len(_OUTS)))
    return got[0]
```
